# Optimizing a Trainium2 kernel written in Bass

```python
import math
import jax, jax.numpy as jnp
from jax import lax
import numpy as np

D_MODEL = 1024
BATCH = 1
SEQ = 2048
DEPTH = 1

CHUNK = 64
CONV_CH = 512
CONV_HEADS = 8
CONV_WIDTH = 31
SSM_CH = 512
SSM_GROUP_CH = 16
SSM_GROUPS = SSM_CH // SSM_GROUP_CH
SSM_STATE = 64
D_MIX = CONV_CH + SSM_CH
D_IN = 2 * CONV_CH + SSM_CH
N_EXPERTS = 64
TOP_K = 8
N_ROUTE_GROUPS = 8
TOPK_ROUTE_GROUPS = 4
D_EXPERT = 256
ROUTED_SCALE = 2.5
MOE_BLOCK = 128
NORM_EPS = 1e-6

kernel_name = 'hymba_conformer_s5_moe_block'

def rms_norm(x, g):
    xf = x.astype(jnp.float32)
    y = xf * lax.rsqrt(jnp.mean(xf * xf, axis=-1, keepdims=True) + NORM_EPS)
    return (y * g.astype(jnp.float32)).astype(x.dtype)

def swiglu(x, w_gate, w_up, w_down):
    return (jax.nn.silu(x @ w_gate) * (x @ w_up)) @ w_down

def conv_module(v, conv_w, conv_b, ln_g, ln_b):
    y = lax.conv_general_dilated(v, conv_w, window_strides=(1,), padding=[(CONV_WIDTH - 1, 0)],
                                 dimension_numbers=('NWC', 'WIO', 'NWC'),
                                 feature_group_count=CONV_CH) + conv_b
    yf = y.astype(jnp.float32)
    mu = jnp.mean(yf, axis=-1, keepdims=True)
    var = jnp.mean(jnp.square(yf - mu), axis=-1, keepdims=True)
    yn = (yf - mu) * lax.rsqrt(var + NORM_EPS) * ln_g.astype(jnp.float32) + ln_b.astype(jnp.float32)
    return jax.nn.silu(yn).astype(v.dtype)

def _complex_affine_combine(e1, e2):
    a1r, a1i, b1r, b1i = e1
    a2r, a2i, b2r, b2i = e2
    ar = a2r * a1r - a2i * a1i
    ai = a2r * a1i + a2i * a1r
    br = a2r * b1r - a2i * b1i + b2r
    bi = a2r * b1i + a2i * b1r + b2i
    return (ar, ai, br, bi)

def s5_layer(u, a_re, a_im, log_dt, b_re, b_im, c_re, c_im, d_skip, w_glu, b_glu):
    bsz, seq, _ = u.shape
    f32 = jnp.float32
    uf = u.astype(f32).reshape(bsz, seq, SSM_GROUPS, SSM_GROUP_CH)
    ar = a_re.astype(f32)
    ai = a_im.astype(f32)
    dt = jnp.exp(log_dt.astype(f32))[:, None]
    mag = jnp.exp(ar * dt)
    lr = mag * jnp.cos(ai * dt)
    li = mag * jnp.sin(ai * dt)
    den = ar * ar + ai * ai
    nr = lr - 1.0
    kr = (nr * ar + li * ai) / den
    ki = (li * ar - nr * ai) / den
    br_ = b_re.astype(f32)
    bi_ = b_im.astype(f32)
    bbr = kr[..., None] * br_ - ki[..., None] * bi_
    bbi = kr[..., None] * bi_ + ki[..., None] * br_
    bu_r = jnp.einsum('blgh,gph->blgp', uf, bbr)
    bu_i = jnp.einsum('blgh,gph->blgp', uf, bbi)
    lam_r = jnp.broadcast_to(lr, bu_r.shape)
    lam_i = jnp.broadcast_to(li, bu_i.shape)
    _, _, s_r, s_i = lax.associative_scan(_complex_affine_combine, (lam_r, lam_i, bu_r, bu_i), axis=1)
    y = (jnp.einsum('blgp,ghp->blgh', s_r, c_re.astype(f32))
         - jnp.einsum('blgp,ghp->blgh', s_i, c_im.astype(f32))
         + d_skip.astype(f32).reshape(SSM_GROUPS, SSM_GROUP_CH) * uf)
    g = jax.nn.gelu(y.reshape(bsz, seq, SSM_CH))
    out = g * jax.nn.sigmoid(g @ w_glu.astype(f32) + b_glu.astype(f32))
    return out.astype(u.dtype)

def dropless_experts(hf, gate_w, top_idx, we_gate, we_up, we_down):
    n_tok, d = hf.shape
    n_assign = n_tok * TOP_K
    flat_e = top_idx.reshape(-1).astype(jnp.int32)
    flat_t = jnp.repeat(jnp.arange(n_tok, dtype=jnp.int32), TOP_K)
    flat_w = gate_w.reshape(-1).astype(hf.dtype)
    order = jnp.argsort(flat_e)
    sorted_e = flat_e[order]
    counts = jnp.bincount(flat_e, length=N_EXPERTS).astype(jnp.int32)
    padded = (counts + MOE_BLOCK - 1) // MOE_BLOCK * MOE_BLOCK
    starts = jnp.cumsum(counts) - counts
    pends = jnp.cumsum(padded)
    pstarts = pends - padded
    dest = pstarts[sorted_e] + jnp.arange(n_assign, dtype=jnp.int32) - starts[sorted_e]
    n_blocks = (n_assign + N_EXPERTS * (MOE_BLOCK - 1) + MOE_BLOCK - 1) // MOE_BLOCK
    n_rows = n_blocks * MOE_BLOCK
    row_tok = jnp.full((n_rows,), n_tok, jnp.int32).at[dest].set(flat_t[order])
    row_w = jnp.zeros((n_rows,), hf.dtype).at[dest].set(flat_w[order])
    block_e = jnp.minimum(
        jnp.searchsorted(pends, jnp.arange(n_blocks, dtype=jnp.int32) * MOE_BLOCK, side='right'),
        N_EXPERTS - 1).astype(jnp.int32)
    x_pad = jnp.concatenate([hf, jnp.zeros((1, d), hf.dtype)], axis=0)

    def block_fn(args):
        tok, w, e = args
        return swiglu(x_pad[tok], we_gate[e], we_up[e], we_down[e]) * w[:, None]

    ys = lax.map(block_fn, (row_tok.reshape(n_blocks, MOE_BLOCK), row_w.reshape(n_blocks, MOE_BLOCK), block_e))
    out = jnp.zeros((n_tok + 1, d), hf.dtype).at[row_tok].add(ys.reshape(n_rows, d))
    return out[:n_tok]

def moe_ffn(h, w_router, b_router, we_gate, we_up, we_down, ws_gate, ws_up, ws_down):
    bsz, seq, d = h.shape
    n_tok = bsz * seq
    hf = h.reshape(n_tok, d)
    scores = jax.nn.sigmoid(hf.astype(jnp.float32) @ w_router.astype(jnp.float32))
    biased = scores + b_router.astype(jnp.float32)
    grp = biased.reshape(n_tok, N_ROUTE_GROUPS, N_EXPERTS // N_ROUTE_GROUPS)
    grp_score = lax.top_k(grp, 2)[0].sum(-1)
    _, top_grp = lax.top_k(grp_score, TOPK_ROUTE_GROUPS)
    grp_mask = jax.nn.one_hot(top_grp, N_ROUTE_GROUPS, dtype=jnp.float32).sum(1) > 0
    exp_mask = jnp.repeat(grp_mask, N_EXPERTS // N_ROUTE_GROUPS, axis=1)
    _, top_idx = lax.top_k(jnp.where(exp_mask, biased, -jnp.inf), TOP_K)
    sel = jnp.take_along_axis(scores, top_idx, axis=1)
    gate_w = sel / (sel.sum(-1, keepdims=True) + 1e-20) * ROUTED_SCALE
    routed = dropless_experts(hf, gate_w, top_idx, we_gate, we_up, we_down)
    shared = swiglu(hf, ws_gate, ws_up, ws_down)
    return (routed + shared).reshape(bsz, seq, d)

def setup_inputs(seed: int = 0) -> dict:
    key = jax.random.key(seed)
    ks = iter(jax.random.split(key, 40))
    f32 = jnp.float32

    def nrm(shape, scale):
        return jax.random.normal(next(ks), shape, f32) * scale

    def gain(shape):
        return 1.0 + nrm(shape, 0.05)

    L = DEPTH
    G, P, H = SSM_GROUPS, SSM_STATE, SSM_GROUP_CH
    inp = {}
    inp['x'] = nrm((BATCH, SEQ, D_MODEL), 1.0)
    inp['c'] = nrm((BATCH, D_MODEL), 1.0)
    inp['w_ada'] = nrm((L, D_MODEL, 6 * D_MODEL), D_MODEL ** -0.5)
    inp['b_ada'] = nrm((L, 6 * D_MODEL), 0.02)
    inp['g_pre_mix'] = gain((L, D_MODEL))
    inp['g_post_mix'] = gain((L, D_MODEL))
    inp['w_in'] = nrm((L, D_MODEL, D_IN), D_MODEL ** -0.5)
    inp['conv_w'] = nrm((L, CONV_WIDTH, 1, CONV_CH), CONV_WIDTH ** -0.5)
    inp['conv_b'] = nrm((L, CONV_CH), 0.02)
    inp['conv_ln_g'] = gain((L, CONV_CH))
    inp['conv_ln_b'] = nrm((L, CONV_CH), 0.02)
    inp['ssm_a_re'] = -0.5 + nrm((L, G, P), 0.01)
    inp['ssm_a_im'] = jnp.broadcast_to(jnp.pi * jnp.arange(P, dtype=f32), (L, G, P)) + nrm((L, G, P), 0.01)
    inp['ssm_log_dt'] = jax.random.uniform(next(ks), (L, G), f32, minval=math.log(0.001), maxval=math.log(0.1))
    inp['ssm_b_re'] = nrm((L, G, P, H), (2 * H) ** -0.5)
    inp['ssm_b_im'] = nrm((L, G, P, H), (2 * H) ** -0.5)
    inp['ssm_c_re'] = nrm((L, G, H, P), (2 * P) ** -0.5)
    inp['ssm_c_im'] = nrm((L, G, H, P), (2 * P) ** -0.5)
    inp['ssm_d'] = nrm((L, SSM_CH), 1.0)
    inp['ssm_w_glu'] = nrm((L, SSM_CH, SSM_CH), SSM_CH ** -0.5)
    inp['ssm_b_glu'] = nrm((L, SSM_CH), 0.02)
    inp['g_out_conv'] = gain((L, CONV_CH))
    inp['g_out_ssm'] = gain((L, SSM_CH))
    inp['w_out'] = nrm((L, D_MIX, D_MODEL), D_MIX ** -0.5)
    inp['g_pre_ffn'] = gain((L, D_MODEL))
    inp['g_post_ffn'] = gain((L, D_MODEL))
    inp['w_router'] = nrm((L, D_MODEL, N_EXPERTS), D_MODEL ** -0.5)
    inp['b_router'] = nrm((L, N_EXPERTS), 0.01)
    inp['we_gate'] = nrm((L, N_EXPERTS, D_MODEL, D_EXPERT), D_MODEL ** -0.5)
    inp['we_up'] = nrm((L, N_EXPERTS, D_MODEL, D_EXPERT), D_MODEL ** -0.5)
    inp['we_down'] = nrm((L, N_EXPERTS, D_EXPERT, D_MODEL), D_EXPERT ** -0.5)
    inp['ws_gate'] = nrm((L, D_MODEL, D_EXPERT), D_MODEL ** -0.5)
    inp['ws_up'] = nrm((L, D_MODEL, D_EXPERT), D_MODEL ** -0.5)
    inp['ws_down'] = nrm((L, D_EXPERT, D_MODEL), D_EXPERT ** -0.5)
    return inp

def reference(x, c, w_ada, b_ada, g_pre_mix, g_post_mix, w_in, conv_w, conv_b, conv_ln_g, conv_ln_b,
              ssm_a_re, ssm_a_im, ssm_log_dt, ssm_b_re, ssm_b_im, ssm_c_re, ssm_c_im, ssm_d,
              ssm_w_glu, ssm_b_glu, g_out_conv, g_out_ssm, w_out, g_pre_ffn, g_post_ffn,
              w_router, b_router, we_gate, we_up, we_down, ws_gate, ws_up, ws_down):
    for l in range(DEPTH):
        mod = jax.nn.silu(c) @ w_ada[l] + b_ada[l]
        sh_m, sc_m, gt_m, sh_f, sc_f, gt_f = [m[:, None, :] for m in jnp.split(mod, 6, axis=-1)]

        h = rms_norm(x, g_pre_mix[l]) * (1.0 + sc_m) + sh_m
        z = h @ w_in[l]
        z_val = z[..., :CONV_CH]
        z_gate = z[..., CONV_CH:2 * CONV_CH]
        z_ssm = z[..., 2 * CONV_CH:]
        a_out = conv_module(z_val * jax.nn.sigmoid(z_gate), conv_w[l], conv_b[l], conv_ln_g[l], conv_ln_b[l])
        b_out = s5_layer(z_ssm, ssm_a_re[l], ssm_a_im[l], ssm_log_dt[l], ssm_b_re[l], ssm_b_im[l],
                         ssm_c_re[l], ssm_c_im[l], ssm_d[l], ssm_w_glu[l], ssm_b_glu[l])
        mixed = jnp.concatenate([rms_norm(a_out, g_out_conv[l]), rms_norm(b_out, g_out_ssm[l])], axis=-1)
        o = mixed @ w_out[l]
        x = x + gt_m * rms_norm(o, g_post_mix[l])

        h = rms_norm(x, g_pre_ffn[l]) * (1.0 + sc_f) + sh_f
        y = moe_ffn(h, w_router[l], b_router[l], we_gate[l], we_up[l], we_down[l],
                    ws_gate[l], ws_up[l], ws_down[l])
        x = x + gt_f * rms_norm(y, g_post_ffn[l])
    return x


_drawn_inputs = setup_inputs


def setup_inputs(seed=0):
    import zlib

    import numpy as np

    out = dict(_drawn_inputs(seed))
    spreads = {}
    factors = {'ssm_a_re': 5.791, 'ssm_b_glu': 2.85}
    for name, (base, spread) in spreads.items():
        noise = np.random.default_rng([zlib.crc32(name.encode()), seed]).standard_normal(out[name].shape)
        drawn = base * np.exp(spread * noise) if base else spread * noise
        out[name] = __import__('jax').numpy.asarray(drawn.astype(out[name].dtype))
    for name, factor in factors.items():
        out[name] = (out[name] * factor).astype(out[name].dtype)
    return out
```

```python
from contextlib import ExitStack

import numpy as np
import concourse.bass as bass
from concourse import mybir

ALU = mybir.AluOpType
ACT = mybir.ActivationFunctionType
AX = mybir.AxisListType
F32 = mybir.dt.float32
BF16 = mybir.dt.bfloat16
I32 = mybir.dt.int32
U32 = mybir.dt.uint32

P = 128
T, D = 2048, 1024
KD = D // P
NH = 2
HT = T // NH
TPH = HT // P
NT = T // P
CC = 512
CT = CC // P
TAPS = 31
PAD = TAPS - 1
CH = 8
NC = HT // CH
G, HG, S = 32, 16, 64
NPR = G // 2
E, TOPK, NG, TOPG = 64, 8, 8, 4
DE = 256
FE = DE // P
BLK = 128
NB = (T * TOPK + E * (BLK - 1)) // BLK + 1
NBT = NT + NB + 2
EPS = 1e-6
BIG = 1e30
WSLOT = 2 * KD * DE + FE * D



class Chain:

    def __init__(self, eng, sem):
        self.eng, self.sem, self.n = eng, sem, 0

    def add(self, ins):
        ins.then_inc(self.sem, 1)
        self.n += 1
        return self.n

    def sync(self):
        self.eng.wait_ge(self.sem, self.n)

    def do(self, *instructions):
        for ins in instructions:
            self.add(ins)
        self.sync()


def numbered(keys):
    return {k: n for n, k in enumerate(keys)}


def build(nc, A, out):
    ctx = ExitStack()
    with ctx:
        def sb(name, shape, dt=F32):
            return ctx.enter_context(nc.sbuf_tensor(name, shape, dt))

        def sem(name):
            return ctx.enter_context(nc.semaphore(name))

        def dram(name, shape, dt=F32):
            return nc.dram_tensor(name, shape, dt).ap()

        mod_d = dram("mod_d", [6, D])
        tab_d = dram("tab_d", [P, 12288])
        et_d = dram("et_d", [P, 4096])
        mix_d = dram("mix_d", [NT, P, KD, P])
        x1_d = dram("x1_d", [T, D])
        h2_d = dram("h2_d", [T + BLK, D])
        acc_d = dram("acc_d", [T + BLK, D])
        rows_d = dram("rows_d", [P * (NB + 2), 2])
        be_d = dram("be_d", [2 * P], I32)

        arena = sb("arena", [P, 50104])
        pos = [0]

        def cut(n):
            a = pos[0]
            pos[0] += n
            assert pos[0] <= 50104, pos[0]
            return arena[:, a:a + n]

        big0 = cut(8192)
        us = cut(4096)
        ut = cut(4096)
        eg = cut(6144)
        tabs = cut(8192)
        vacc = cut(4216 + 4096)
        wio = cut(4096)
        xbr = cut(3072)
        work = cut(3904)
        hT = big0.rearrange("p (k t) -> p k t", k=KD)
        U = us.rearrange("p (g j h) -> p g j h", g=G, j=CH)
        SR = us[:, 0:2048].rearrange("p (r c) -> p r c", r=NPR)
        SI = us[:, 2048:4096].rearrange("p (r c) -> p r c", r=NPR)
        UT = ut.rearrange("p (g c) -> p g c", g=G)
        GA = ut.rearrange("p (q i c) -> p q i c", q=CT, i=CH)
        EC = eg[:, 0:2048].rearrange("p (r c) -> p r c", r=NPR)
        ES = eg[:, 2048:4096].rearrange("p (r c) -> p r c", r=NPR)
        gT = eg[:, 0:4096].rearrange("p (q t) -> p q t", q=CT)
        arow, brow = eg[:, 4096:5120], eg[:, 5120:6144]
        RT = tabs[:, 0:4096].rearrange("p (g m) -> p g m", g=G)
        TOE = tabs[:, 0:4096].rearrange("p (g m) -> p g m", g=G)
        COR = tabs[:, 4096:6144].rearrange("p (r m) -> p r m", r=NPR)
        COI = tabs[:, 6144:8192].rearrange("p (r m) -> p r m", r=NPR)
        v = vacc[:, 0:4216].rearrange("p (q t) -> p q t", q=CT)
        cacc = vacc[:, 4216:8312].rearrange("p (q t) -> p q t", q=CT)
        wz = wio.rearrange("p (s n) -> p s n", s=2)
        xb = xbr.rearrange("p (s n) -> p s n", s=3)
        rot = work[:, 0:2048].rearrange("p (s n) -> p s n", s=4)
        sg = [work[:, 2048:2560], work[:, 2560:3072]]
        ytok = sb("ytok", [P, 512])
        yn = work[:, 3072:3584]
        bo = sb("bo", [P, 2, 512])
        ly = sb("ly", [P, 512])

        ident = sb("ident", [P, P])
        tri = sb("tri", [P, P], BF16)
        oneb = sb("oneb", [P, P], BF16)
        one = sb("one", [P, 1])
        mhalf = sb("mhalf", [P, 1])
        sel8 = sb("sel8", [P, NG, NG])
        cw = sb("cw", [P, CT, TAPS])
        col = sb("col", [P, 4, CT])
        gout = sb("gout", [P, KD])
        ccol = sb("ccol", [P, KD])
        csig = sb("csig", [P, KD])
        st = sb("st", [P, 64])
        bn = sb("bn", [P, 8])
        lam8 = sb("lam8", [P, 6, NPR])
        last = sb("last", [P, 4, NPR])
        seg = bo
        segb = [ytok, ly]

        psm = ctx.enter_context(nc.psum_tensor("psm", [P, 8, 512], F32))
        mm = [psm[:, b, :] for b in (0, 1)]
        tp = [psm[:, b, :] for b in (2, 3)]
        dv = [psm[:, b, :] for b in (4, 5, 6, 7)]

        s_par_in = sem("par_in")
        s_dv_full = sem("dv_full")
        s_seg_ok = sem("seg_ok")
        s_ada_in0 = sem("ada_in0")
        s_ada_in1 = sem("ada_in1")
        s_small_in = sem("small_in")
        s_mod_out0 = sem("mod_out0")
        s_mod_out1 = sem("mod_out1")
        s_rt_ready = sem("rt_ready")
        s_tab_out = sem("tab_out")
        s_phasor_ready = sem("phasor_ready")
        s_et_out = sem("et_out")
        s_toe_ready = sem("toe_ready")
        s_rows_in = sem("rows_in")
        s_x_in0 = sem("x_in0")
        s_x_in1 = sem("x_in1")
        s_x_in2 = sem("x_in2")
        s_arow_ready = sem("arow_ready")
        s_tp_full = sem("tp_full")
        s_mm_full = sem("mm_full")
        s_wz_in0 = sem("wz_in0")
        s_wz_in1 = sem("wz_in1")
        s_tab_in = sem("tab_in")
        s_bo_full = sem("bo_full")
        s_bo_out0 = sem("bo_out0")
        s_bo_out1 = sem("bo_out1")
        s_et_in = sem("et_in")
        s_wout_in = sem("wout_in")
        s_row_in = sem("row_in")
        s_wr_in = sem("wr_in")
        s_wa_in = sem("wa_in")
        s_wb_in = sem("wb_in")
        s_ob_full = sem("ob_full")
        s_sqm_ready = sem("sqm_ready")
        s_x1_out0 = sem("x1_out0")
        s_x1_out1 = sem("x1_out1")
        s_s1_ready = sem("s1_ready")
        s_ha_ready = sem("ha_ready")
        s_mix_in0 = sem("mix_in0")
        s_mix_in1 = sem("mix_in1")
        s_xs_in0 = sem("xs_in0")
        s_xs_in1 = sem("xs_in1")
        s_zero_ok = sem("zero_ok")
        s_h2z_out = sem("h2z_out")
        s_x1_ready = sem("x1_ready")
        s_h2_ready = sem("h2_ready")
        s_h2_out0 = sem("h2_out0")
        s_h2_out1 = sem("h2_out1")
        s_xg_in = sem("xg_in")
        s_xt_full = sem("xt_full")
        s_y_act = sem("y_act")
        s_y_dve = sem("y_dve")
        s_y_out = sem("y_out")
        s_xp_in = sem("xp_in")
        s_cnt_ready = sem("cnt_ready")
        s_y_full = sem("y_full")
        s_y_free = sem("y_free")
        s_fin_in0 = sem("fin_in0")
        s_fin_in1 = sem("fin_in1")
        s_fin_in2 = sem("fin_in2")
        s_fin_out0 = sem("fin_out0")
        s_fin_out1 = sem("fin_out1")
        s_fin_out2 = sem("fin_out2")
        s_fo_ready = sem("fo_ready")
        s_tp_free = sem("tp_free")
        s_mm_free = sem("mm_free")
        s_dv_free = sem("dv_free")
        s_const_ok = sem("const_ok")
        s_nat_ready = sem("nat_ready")
        s_csig_ok = sem("csig_ok")
        s_c_ready = sem("c_ready")
        s_r_ready = sem("r_ready")
        s_xn_ready = sem("xn_ready")
        s_states_ready = sem("states_ready")
        s_conv_ready = sem("conv_ready")
        s_yn_ready = sem("yn_ready")
        s_wout_ready = sem("wout_ready")
        s_h2t_free = sem("h2t_free")
        s_h2t_full = sem("h2t_full")
        s_sc_ready = sem("sc_ready")
        s_lg_full = sem("lg_full")
        s_ssn_ready = sem("ssn_ready")
        s_ss_full = sem("ss_full")
        s_oa_ready = sem("oa_ready")
        s_oa_full = sem("oa_full")
        s_o_ready = sem("o_ready")
        s_sel_ready = sem("sel_ready")
        s_pos_full = sem("pos_full")
        s_xr_in = sem("xr_in")
        s_xt_act = sem("xt_act")
        s_xt_dve = sem("xt_dve")
        s_gu_full = sem("gu_full")
        s_h_full = sem("h_full")
        s_ht_full = sem("ht_full")
        s_ht_ready = sem("ht_ready")
        s_be_back = sem("be_back")
        s_act_step = sem("act_step")
        s_dt_ready = sem("dt_ready")
        s_nat_angle = sem("nat_angle")
        s_nat_trig = sem("nat_trig")
        s_sq_ready = sem("sq_ready")
        s_sg_free = sem("sg_free")
        s_stat_ready = sem("stat_ready")
        s_xr_ready = sem("xr_ready")
        s_v_tail = sem("v_tail")
        s_ly_full = sem("ly_full")
        s_rr_ready = sem("rr_ready")
        s_so_ready = sem("so_ready")
        s_sig_ready = sem("sig_ready")
        s_fs_ready = sem("fs_ready")
        s_dve_step = sem("dve_step")
        s_v_ready = sem("v_ready")
        s_bn_ready = sem("bn_ready")
        s_row_ready = sem("row_ready")
        s_ro_ready = sem("ro_ready")
        s_t_ready = sem("t_ready")
        s_r1_ready = sem("r1_ready")
        s_rinit_ready = sem("rinit_ready")
        s_pay_ready = sem("pay_ready")
        s_hm_ready = sem("hm_ready")
        s_rows_back = sem("rows_back")
        s_fr_ready = sem("fr_ready")
        s_ft_ready = sem("ft_ready")
        s_pool_step = sem("pool_step")
        s_rinit_out = sem("rinit_out")
        s_be_out = sem("be_out")
        s_disp_out = sem("disp_out")
        s_idx_ready = sem("idx_ready")
        s_idy_ready = sem("idy_ready")
        s_ya_out = sem("ya_out")

        tpk = []
        mmk = []
        for h in range(NH):
            tpk += [("hT", h, i, b) for i in range(TPH) for b in range(2)]
            tpk += [("UT", h, n) for n in range(8)]
            if h == 1:
                for i in range(TPH + 1):
                    tpk += [("LF", 0, i)] if i < TPH else []
                    tpk += [("LB", 0, i - 1)] if i >= 1 else []
            tpk += [("GT", h, q, b) for q in range(CT) for b in range(2)]
            mmk += [("zs", h, j) for j in range(CH)]
            mmk += [("zc", h, q, b, w) for q in range(CT) for b in range(2) for w in range(2)]
            mmk += [("Y", h, n) for n in range(8)]
            mmk += [("glu", h, b, q) for b in range(2) for q in range(CT)]
        for i in range(TPH + 1):
            tpk += [("LF", 1, i)] if i < TPH else []
            tpk += [("LB", 1, i - 1)] if i >= 1 else []
        dvk = [("nat", 0)] + [("ada", n) for n in range(12)] + [("C", n) for n in range(3)]
        dvk += [("RT", n) for n in range(8)] + [("TOE", n) for n in range(8)]
        for h in range(NH):
            dvk += [("V", h, n, w) for n in range(4) for w in range(2)]
        TPN, MMN, DVN = numbered(tpk), numbered(mmk), numbered(dvk)

        C1, C2 = 6.28125, float(np.float32(2 * np.pi - 6.28125))
        C3 = float(2 * np.pi - 6.28125 - np.float64(np.float32(2 * np.pi - 6.28125)))
        MAGIC = 1.5 * 2.0 ** 23

        nat = [xbr[0:G, n * P:(n + 1) * P] for n in range(20)]
        (nar, nai, nth, nn, nr_, nmag, nsin, ncos, nlr, nli, nden, nkr, nki, nm8, nc8, ns8, nd, nt1,
         nt2, nt3) = nat
        cwn = xbr[0:TAPS, 20 * P:24 * P]
        ndt = sb("ndt", [G, 4])
        L = work[:, 0:9 * G * 2].rearrange("p (w k g) -> p w k g", w=2, k=9)
        LP = work[:, 576:576 + 9 * NPR * 2].rearrange("p (w k r) -> p w k r", w=2, k=9)
        dup = work[:, 864:864 + 256].rearrange("p (n g) -> p n g", n=8)
        Y1 = work[:, 1120:1632].rearrange("p (g h) -> p g h", g=G)
        CRP = work[:, 1632:1888].rearrange("p (r h) -> p r h", r=NPR)
        CIP = work[:, 1888:2144].rearrange("p (r h) -> p r h", r=NPR)
        CN = work[:, 2144:3680].rearrange("p (w q m) -> p w q m", w=3, q=4)
        X1 = wio[:, 0:512].rearrange("p (g h) -> p g h", g=G)
        X2 = wio[:, 512:1024].rearrange("p (g h) -> p g h", g=G)
        BB1 = wio[:, 1024:1536].rearrange("p (g h) -> p g h", g=G)
        BB2 = wio[:, 1536:2048].rearrange("p (g h) -> p g h", g=G)
        PT = [wio[:, 2048 + n * 1024:3072 + n * 1024] for n in range(2)] + [eg[:, 4096:5120], eg[:, 5120:6144]]
        R = big0[:, 0:G * 15 * HG].rearrange("p (g s h) -> p g s h", g=G, s=15)
        ctoe = cacc.rearrange("p q t -> p (q t)").rearrange("p (g m) -> p g m", g=G)
        vflat = vacc[:, 0:4096]
        ccor = vflat[:, 0:2048].rearrange("p (r i h) -> p r i h", r=NPR, i=CH)
        ccoi = vflat[:, 2048:4096].rearrange("p (r i h) -> p r i h", r=NPR, i=CH)
        wada = [us.rearrange("p (k n) -> p k n", k=KD), ut.rearrange("p (k n) -> p k n", k=KD)]

        x_t = A["x"][0].rearrange("(i p) d -> i p d", p=P)
        wada_d = A["w_ada"][0].rearrange("(k p) n -> p k n", p=P)
        bada_d = A["b_ada"]
        win_d = A["w_in"][0].rearrange("(k p) n -> p k n", p=P)
        modf = mod_d.rearrange("a n -> (a n)")

        first = [(nar[:, 0:S], A["ssm_a_re"][0]), (nar[:, S:P], A["ssm_a_re"][0]),
                 (nai[:, 0:S], A["ssm_a_im"][0]), (nai[:, S:P], A["ssm_a_im"][0]),
                 (ndt[:, 0:1], A["ssm_log_dt"][0].unsqueeze(1)),
                 (nd[:, 0:HG], A["ssm_d"][0].rearrange("(g h) -> g h", g=G)), (cwn, A["conv_w"][0, :, 0, :]),
                 (ccol[:, :], A["c"][0].rearrange("(k p) -> p k", p=P))]
        b_re = A["ssm_b_re"][0].rearrange("g p h -> p g h")
        b_im = A["ssm_b_im"][0].rearrange("g p h -> p g h")
        small = [(X1[0:S], b_re), (X1[S:P], b_im), (X2[0:S], b_im), (X2[S:P], b_re)]
        c_re = A["ssm_c_re"][0].rearrange("(q a) h p -> (a h) q p", a=8)
        c_im = A["ssm_c_im"][0].rearrange("(q a) h p -> (a h) q p", a=8)
        for w, (lo, hi) in enumerate(((c_re, c_im), (c_re, c_re), (c_im, c_im))):
            small += [(CN[:, w, :, 0:S], lo), (CN[:, w, :, S:P], hi)]
        for n, a in enumerate(("conv_b", "conv_ln_g", "conv_ln_b", "ssm_b_glu")):
            small += [(col[:, n, :], A[a][0].rearrange("(q p) -> p q", p=P))]
        small += [(gout[:, 0:CT], A["g_out_conv"][0].rearrange("(q p) -> p q", p=P)),
                  (gout[:, CT:KD], A["g_out_ssm"][0].rearrange("(q p) -> p q", p=P))]
        NSMALL, NFIRST = len(small), len(first)

        def wz_conv(q):
            return wz[:, q % 2, :].rearrange("p (w k n) -> p w k n", w=2, k=KD)


        blk = ctx.enter_context(nc.Block())
        V, SC, TE, PO, SY = nc.vector, nc.scalar, nc.tensor, nc.gpsimd, nc.sync

        wout = big0.rearrange("p (k n) -> p k n", k=KD)
        mixb = us[:, 0:2048].rearrange("p (s k t) -> p s k t", s=2, k=KD)
        sqb = us[:, 2048:3072].rearrange("p (k t) -> p k t", k=KD)
        h2T = us[:, 3072:4096].rearrange("p (k t) -> p k t", k=KD)
        ob = ut[:, 0:1024]
        h2b = ut[:, 1024:3072].rearrange("p (s n) -> p s n", s=2)
        junk = ut[:, 3072:4096]
        rows = wio.rearrange("p (n d) -> p n d", n=4)
        rtmp = tabs[:, 4096:7168].rearrange("p (n d) -> p n d", n=3)
        cur = [0]

        def cut2(size, shape=None, dt=F32, base=tabs, **kw):
            a = cur[0]
            cur[0] += size
            r = base[:, a:a + size]
            if dt is not F32:
                r = r.bitcast(dt)
            return r.rearrange(shape, **kw) if shape else r

        wr = cut2(512, "p (k e) -> p k e", k=KD)
        scores, biased, bm, rep, pen, rbias = (cut2(64) for _ in range(6))
        v8 = cut2(64, "p (g m) -> p g m", g=NG)
        cmpa, cmpb = (cut2(64, "p (g m) -> p g m", g=NG) for _ in range(2))
        gs, rank, gm, gp, t8 = (cut2(8) for _ in range(5))
        gsum = cut2(8)
        selbf = cut2(512, "p (i e) -> p i e", dt=BF16, i=NT)
        selcum = cut2(544, "p (i e) -> p i e", dt=BF16, i=NT + 1)
        selall = cut2(1024, "p (i e) -> p i e", i=NT)
        gwall = cut2(1024, "p (i e) -> p i e", i=NT)
        DD = cut2(1024, "p (i e) -> p i e", i=NT)
        eqb = cut2(1024, "p (i e) -> p i e", i=NT)
        d8 = cut2(128, "p (i k) -> p i k", i=NT)
        w8 = cut2(128, "p (i k) -> p i k", i=NT)
        qi = cut2(128, dt=I32)
        bi = cut2(128, dt=I32)
        bf_ = cut2(128)
        qf = cut2(128)
        di = cut2(128, dt=U32)
        pay = cut2(256, "p (n w) -> p n w", n=P)
        cntf, nbf, pend, basef, ones64 = (cut2(64) for _ in range(5))
        cnti = cut2(64, dt=I32)
        assert cur[0] <= 8192, cur[0]
        cur[0] = 2816
        W = work
        rinit = cut2(2 * (NB + 2), "p (b w) -> p b w", base=W, w=2)
        tabl = cut2(2 * (NB + 2), "p (b w) -> p b w", base=W, w=2)
        pint = cut2(64, dt=I32, base=W)
        bep = cut2(2, base=W)
        bei = cut2(2, dt=I32, base=W)
        bidx = cut2(2, base=W)
        idxg = cut2(1, dt=U32, base=W)
        idxs = cut2(1, dt=U32, base=W)
        assert cur[0] <= 3904, cur[0]
        berow = bo[0:1, 0, 0:256].bitcast(I32)
        xg = xbr[:, 0:1024]
        XT = xbr[:, 1024:2048].rearrange("p (k t) -> p k t", k=KD)
        yb = work[:, 0:1024]
        sigb, htmp, hs = (work[:, 1024 + n * DE:1024 + (n + 1) * DE] for n in range(3))
        hTs = work[:, 1792:2048].rearrange("p (f t) -> p f t", f=FE)
        zrow = work[:, 1024:2048]
        EG0, VA0 = 16384, 16384 + 6144 + 8192
        WSTEP = VA0 - EG0
        xp = arena[:, 0:16384].rearrange("p (i d) -> p i d", i=NT)
        NPAIR = (E - 2) // 2

        sgk, bok = [], []
        for h in range(NH):
            if h == 1:
                sgk += [("ln", 0, i) for i in range(TPH)]
            sgk += [("zc", h, q, b) for q in range(CT) for b in range(2)]
            sgk += [("glu", h, b, q) for b in range(2) for q in range(CT)]
        sgk += [("ln", 1, i) for i in range(TPH)]
        bok = [k for k in sgk if k[0] != "zc"]
        SGN, BON = numbered(sgk), numbered(bok)

        @blk.sync
        def _(sp):
            for dst, src in first:
                SY.dma_start(dst, src, allow_slow_non_contiguous=True).then_inc(s_par_in, 16)
            for n in range(12):
                if n >= 2:
                    sp.wait_ge(s_dv_full, DVN["ada", n - 2] + 1)
                    sp.wait_ge(s_seg_ok, n - 1)
                SY.dma_start(wada[n % 2], wada_d[:, :, n * 512:(n + 1) * 512]).then_inc([s_ada_in0, s_ada_in1][n % 2], 16)
                SY.dma_start(segb[n % 2][0:1, :], bada_d[:, n * 512:(n + 1) * 512]).then_inc([s_ada_in0, s_ada_in1][n % 2], 16)
                if n == 1:
                    for dst, src in small:
                        SY.dma_start(dst, src, allow_slow_non_contiguous=True).then_inc(s_small_in, 16)
                if n >= 1:
                    sp.wait_ge(s_seg_ok, n)
                    SY.dma_start(modf[(n - 1) * 512:n * 512].unsqueeze(0), seg[0:1, (n - 1) % 2, :]).then_inc([s_mod_out0, s_mod_out1][(n - 1) % 2], 16)
            sp.wait_ge(s_seg_ok, 12)
            SY.dma_start(modf[11 * 512:12 * 512].unsqueeze(0), seg[0:1, 1, :]).then_inc(s_mod_out1, 16)
            sp.wait_ge(s_rt_ready, 8)
            SY.dma_start(tab_d[:, 0:4096], tabs[:, 0:4096]).then_inc(s_tab_out, 16)
            sp.wait_ge(s_phasor_ready, 1)
            SY.dma_start(et_d, eg[:, 0:4096]).then_inc(s_et_out, 16)
            sp.wait_ge(s_toe_ready, 1)
            SY.dma_start(tab_d[:, 4096:8192], vacc[:, 4216:8312]).then_inc(s_tab_out, 16)
            SY.dma_start(tab_d[:, 8192:12288], vflat).then_inc(s_tab_out, 16)
            sp.wait_ge(s_mod_out0, 6 * 16)
            sp.wait_ge(s_mod_out1, 6 * 16)
            sp.wait_ge(s_toe_ready, 1)
            SY.dma_start(brow, mod_d[0].partition_broadcast(P)).then_inc(s_rows_in, 16)
            SY.dma_start(arow, mod_d[1].partition_broadcast(P)).then_inc(s_rows_in, 16)
            SY.dma_start(xb[:, 2, :], A["g_pre_mix"][0].partition_broadcast(P)).then_inc(s_rows_in, 16)
            xin = [s_x_in0, s_x_in1, s_x_in2]

            def load_x(n):
                if n == 2:
                    sp.wait_ge(s_arow_ready, 1)
                if n >= 3:
                    h, i = divmod(n - 3, TPH)
                    sp.wait_ge(s_tp_full, TPN["hT", h, i, 1] + 1)
                SY.dma_start(xb[:, n % 3, :], x_t[n]).then_inc(xin[n % 3], 16)

            def load_wz_ssm(h):
                if h:
                    sp.wait_ge(s_mm_full, MMN["glu", 0, 1, 3] + 1)
                for w in range(2):
                    SY.dma_start(wz[:, w, :].rearrange("p (k n) -> p k n", k=4),
                                 win_d[:, 4 * w:4 * w + 4, 2 * CC:3 * CC]).then_inc([s_wz_in0, s_wz_in1][w], 16)

            def load_wz_conv(h, q):
                sp.wait_ge(s_mm_full, (MMN["zs", h, 7] if q < 2 else MMN["zc", h, q - 2, 1, 1]) + 1)
                for w in range(2):
                    SY.dma_start(wz_conv(q)[:, w], win_d[:, :, w * CC + q * P:w * CC + (q + 1) * P])\
                      .then_inc([s_wz_in0, s_wz_in1][q % 2], 16)

            def load_wglu(h):
                sp.wait_ge(s_mm_full, MMN["zc", h, 2, 1, 1] + 1)
                SY.dma_start(wz[:, 0, :].rearrange("p (q n) -> p q n", q=CT),
                             A["ssm_w_glu"][0].rearrange("(q p) n -> p q n", p=P)).then_inc(s_wz_in0, 16)

            def load_toe(h):
                sp.wait_ge(s_dv_full, DVN["V", h, 3, 1] + 1)
                if h == 0:
                    sp.wait_ge(s_tab_out, 48)
                SY.dma_start(tabs, tab_d[:, 4096:12288]).then_inc(s_tab_in, 16)

            def store_bo(key):
                n = BON[key]
                sp.wait_ge(s_bo_full, n + 1)
                o = [s_bo_out0, s_bo_out1][n % 2]
                src = bo[:, n % 2, :].rearrange("p (a t) -> p a t", a=4)
                if key[0] == "ln":
                    SY.dma_start(mix_d[key[1] * TPH + key[2], :, 0:CT, :], src).then_inc(o, 16)
                else:
                    _, h, b, q = key
                    i0 = h * TPH + 4 * b
                    SY.dma_start(mix_d[i0:i0 + 4, :, CT + q, :].rearrange("i p t -> p i t"), src).then_inc(o, 16)

            sp.wait_ge(s_toe_ready, 1)
            load_wz_ssm(0)
            for n in range(TPH + 3):
                load_x(n)
            load_wz_conv(0, 0)
            load_wz_conv(0, 1)
            load_toe(0)
            load_wz_conv(0, 2)
            load_wz_conv(0, 3)
            load_wglu(0)
            sp.wait_ge(s_mm_full, MMN["Y", 0, 7] + 1)
            SY.dma_start(tabs[:, 0:4096], tab_d[:, 0:4096]).then_inc(s_tab_in, 16)
            for b in range(2):
                for q in range(CT):
                    store_bo(("glu", 0, b, q))
            load_wz_ssm(1)
            SY.dma_start(eg[:, 0:4096], et_d).then_inc(s_et_in, 16)
            for n in range(TPH + 3, NT):
                load_x(n)
            load_wz_conv(1, 0)
            load_wz_conv(1, 1)
            load_toe(1)
            for i in range(TPH):
                store_bo(("ln", 0, i))
            load_wz_conv(1, 2)
            load_wz_conv(1, 3)
            load_wglu(1)
            sp.wait_ge(s_mm_full, MMN["zc", 1, 3, 1, 1] + 1)
            for k in range(KD):
                SY.dma_start(wout[:, k, :], A["w_out"][0, k * P:(k + 1) * P, :]).then_inc(s_wout_in, 16)
            for b in range(2):
                for q in range(CT):
                    store_bo(("glu", 1, b, q))
            for dst, src in ((rows[:, 0], mod_d[2]), (rows[:, 1], mod_d[4]), (rows[:, 2], mod_d[3]), (rows[:, 3], mod_d[5]),
                             (rtmp[:, 0], A["g_post_mix"][0]), (rtmp[:, 1], A["g_pre_ffn"][0]), (rtmp[:, 2], A["g_post_ffn"][0])):
                SY.dma_start(dst, src.partition_broadcast(P)).then_inc(s_row_in, 16)
            SY.dma_start(wr, A["w_router"][0].rearrange("(k p) e -> p k e", p=P)).then_inc(s_wr_in, 16)
            SY.dma_start(rbias, A["b_router"][0].partition_broadcast(P)).then_inc(s_wr_in, 16)

            def load_w(sl, gate, up, down):
                base = EG0 + sl * WSTEP
                o = [s_wa_in, s_wb_in][sl]
                gu = arena[:, base:base + 2 * KD * DE].rearrange("p (k w f) -> p k w f", k=KD, w=2)
                SY.dma_start(gu[:, :, 0, :], gate.rearrange("(k p) f -> p k f", p=P)).then_inc(o, 16)
                SY.dma_start(gu[:, :, 1, :], up.rearrange("(k p) f -> p k f", p=P)).then_inc(o, 16)
                SY.dma_start(arena[:, base + 4096:base + 6144].rearrange("p (k f) -> p k f", k=FE), down.rearrange("(k p) f -> p k f", p=P)).then_inc(o, 16)

            for i in range(TPH):
                store_bo(("ln", 1, i))
            load_w(0, A["ws_gate"][0], A["ws_up"][0], A["ws_down"][0])
            sp.wait_ge(s_tp_full, TPN["LF", 1, TPH - 1] + 1)
            load_w(1, A["we_gate"][0, 0], A["we_up"][0, 0], A["we_down"][0, 0])
            for w in range(2):
                sp.wait_ge([s_bo_out0, s_bo_out1][w], 16 * (len(bok) // 2))

            def load_tile(i):
                if i >= 2:
                    sp.wait_ge(s_ob_full, i - 1)
                    sp.wait_ge(s_sqm_ready, i - 1)
                    sp.wait_ge([s_x1_out0, s_x1_out1][i % 2], 16 * (i // 2))
                    sp.wait_ge(s_s1_ready, i - 1)
                    sp.wait_ge(s_ha_ready, i - 1)
                SY.dma_start(mixb[:, i % 2], mix_d[i]).then_inc([s_mix_in0, s_mix_in1][i % 2], 16)
                SY.dma_start(xb[:, i % 2, :], x_t[i]).then_inc([s_xs_in0, s_xs_in1][i % 2], 16)

            sp.wait_ge(s_zero_ok, 1)
            SY.dma_start(h2_d[T:T + BLK, :], xb[:, 2, :]).then_inc(s_h2z_out, 16)
            SY.dma_start(acc_d[T:T + BLK, :], xb[:, 2, :]).then_inc(s_h2z_out, 16)
            load_tile(0)
            load_tile(1)
            for i in range(NT):
                sp.wait_ge(s_x1_ready, i + 1)
                SY.dma_start(x1_d[i * P:(i + 1) * P, :], xb[:, i % 2, :]).then_inc([s_x1_out0, s_x1_out1][i % 2], 16)
                sp.wait_ge(s_h2_ready, i + 1)
                SY.dma_start(h2_d[i * P:(i + 1) * P, :], h2b[:, i % 2, :]).then_inc([s_h2_out0, s_h2_out1][i % 2], 16)
                if i + 2 < NT:
                    load_tile(i + 2)
            for w in range(2):
                sp.wait_ge([s_h2_out0, s_h2_out1][w], 16 * (NT // 2))
                sp.wait_ge([s_x1_out0, s_x1_out1][w], 16 * (NT // 2))
            sp.wait_ge(s_h2z_out, 32)

            def load_rows(b):
                SY.dma_start(xg, h2_d[bass.ds(b * BLK, BLK), :]).then_inc(s_xg_in, 16)

            load_rows(0)
            sp.wait_ge(s_xt_full, 1)
            load_rows(1)
            with sp.Fori(0, NT - 2) as b:
                sp.wait_ge(s_xt_full, b + 2)
                load_rows(b + 2)
                sp.wait_ge(s_y_act, b + 1)
                sp.wait_ge(s_y_dve, b + 1)
                SY.dma_start(acc_d[bass.ds(b * BLK, BLK), :], yb).then_inc(s_y_out, 16)
            for b in range(NT - 2, NT):
                sp.wait_ge(s_y_act, b + 1)
                sp.wait_ge(s_y_dve, b + 1)
                SY.dma_start(acc_d[b * BLK:(b + 1) * BLK, :], yb).then_inc(s_y_out, 16)
                if b == NT - 2:
                    for i in range(NT):
                        SY.dma_start(xp[:, i, :], x1_d[i * P:(i + 1) * P, :]).then_inc(s_xp_in, 16)
            load_w(0, A["we_gate"][0, 1], A["we_up"][0, 1], A["we_down"][0, 1])
            sp.wait_ge(s_cnt_ready, 1)
            with sp.Fori(0, NPAIR) as n:
                for w in range(2):
                    done = sp.value_load(pint[0:1, bass.ds(2 * n + w, 1)], min_val=0, max_val=NB)
                    sp.wait_ge(s_y_full, done + NT)
                    e = 2 * n + (2 + w)
                    load_w(1 - w, A["we_gate"][0, bass.ds(e, 1)].rearrange("a k f -> (a k) f"),
                           A["we_up"][0, bass.ds(e, 1)].rearrange("a k f -> (a k) f"),
                           A["we_down"][0, bass.ds(e, 1)].rearrange("a k f -> (a k) f"))
            nb = sp.value_load(pint[0:1, E - 1:E], min_val=1, max_val=NB)
            sp.wait_ge(s_y_free, nb + 1)
            fin_in = [s_fin_in0, s_fin_in1, s_fin_in2]
            fin_out = [s_fin_out0, s_fin_out1, s_fin_out2]
            for i in range(NT + 2):
                if i < NT:
                    if i >= 3:
                        sp.wait_ge(fin_out[i % 3], 16 * (i // 3))
                    SY.dma_start(xb[:, i % 3, :], acc_d[i * P:(i + 1) * P, :]).then_inc(fin_in[i % 3], 16)
                if i >= 2:
                    sp.wait_ge(s_fo_ready, i - 1)
                    SY.dma_start(out[0, (i - 2) * P:(i - 1) * P, :], xb[:, (i - 2) % 3, :]).then_inc(fin_out[(i - 2) % 3], 16)
            for w in range(3):
                sp.wait_ge(fin_out[w], 16 * len(range(w, NT, 3)))

        @blk.tensor
        def _(pe):
            def take(ring, n, full, free, banks):
                if n >= banks:
                    pe.wait_ge(free, n - banks + 1)
                return ring[n % banks]

            def take_tp(key):
                return take(tp, TPN[key], s_tp_full, s_tp_free, 2)

            def take_mm(key):
                return take(mm, MMN[key], s_mm_full, s_mm_free, 2)

            def take_dv(key):
                return take(dv, DVN[key], s_dv_full, s_dv_free, 4)

            pe.wait_ge(s_const_ok, 1)
            pe.wait_ge(s_nat_ready, 1)
            b = take_dv(("nat", 0))
            for n, a in enumerate((nlr, nli, nkr, nki, nm8, nc8, ns8, nt3)):
                TE.transpose(b[:, n * G:(n + 1) * G], a, ident[0:G, 0:G])
            for q in range(CT):
                m = TE.transpose(b[:, 8 * G + q * TAPS:8 * G + (q + 1) * TAPS], cwn[:, q * P:(q + 1) * P], ident[0:TAPS, 0:TAPS])
            m.then_inc(s_dv_full, 1)
            pe.wait_ge(s_csig_ok, 2)
            for n in range(12):
                b = take_dv(("ada", n))
                pe.wait_ge([s_ada_in0, s_ada_in1][n % 2], 32 * (n // 2 + 1))
                for k in range(KD):
                    m = TE.matmul(b[0:1, :], ccol[:, k:k + 1], wada[n % 2][:, k, :], start=(k == 0), stop=(k == KD - 1))
                m.then_inc(s_dv_full, 1)
            pe.wait_ge(s_small_in, 16 * NSMALL)
            pe.wait_ge(s_c_ready, 1)
            for w in range(3):
                b = take_dv(("C", w))
                for q in range(4):
                    m = TE.transpose(b[:, q * P:(q + 1) * P], CN[:, w, q, :], ident[:, :])
                m.then_inc(s_dv_full, 1)
            pe.wait_ge(s_r_ready, 1)
            for n in range(8):
                b = take_dv(("RT", n))
                for j in range(4):
                    m = TE.transpose(b[:, j * P:(j + 1) * P], R[:, 4 * n + j, 0:CH, :].rearrange("p s h -> p (s h)"), ident[:, :])
                m.then_inc(s_dv_full, 1)
            pe.wait_ge(s_c_ready, 2)
            for n in range(8):
                b = take_dv(("TOE", n))
                for j in range(4):
                    g = 4 * n + j
                    for i in range(CH):
                        m = TE.matmul(b[:, j * P + i * HG:j * P + (i + 1) * HG],
                                      R[:, g, CH - 1 - i:2 * CH - 1 - i, :].rearrange("p s h -> p (s h)"), Y1[:, g, :],
                                      start=True, stop=True)
                m.then_inc(s_dv_full, 1)

            def to_hT(h):
                for i in range(TPH):
                    n = h * TPH + i
                    pe.wait_ge(s_xn_ready, n + 1)
                    for c in range(2):
                        b = take_tp(("hT", h, i, c))
                        for k in range(4):
                            m = TE.transpose(b[:, k * P:(k + 1) * P], xb[:, n % 3, (4 * c + k) * P:(4 * c + k + 1) * P], ident[:, :])
                        m.then_inc(s_tp_full, 1)

            def z_ssm(h):
                pe.wait_ge(s_tp_free, TPN["hT", h, TPH - 1, 1] + 1)
                pe.wait_ge(s_wz_in0, 96 * h + 16)
                pe.wait_ge(s_wz_in1, 80 * h + 16)
                for j in range(CH):
                    b = take_mm(("zs", h, j))
                    for k in range(KD):
                        m = TE.matmul(b[:, :], hT[:, k, :].rearrange("p (c j) -> p j c", j=CH)[:, j, :],
                                      wio[:, k * CC:(k + 1) * CC], start=(k == 0), stop=(k == KD - 1))
                    m.then_inc(s_mm_full, 1)

            def u_transposed(h):
                pe.wait_ge(s_mm_free, MMN["zs", h, CH - 1] + 1)
                for n in range(8):
                    b = take_tp(("UT", h, n))
                    for j in range(4):
                        m = TE.transpose(b[:, j * P:(j + 1) * P], us[:, (4 * n + j) * P:(4 * n + j + 1) * P], ident[:, :])
                    m.then_inc(s_tp_full, 1)

            def inputs_to_state(h):
                pe.wait_ge(s_tp_free, TPN["UT", h, 7] + 1)
                if h == 0:
                    pe.wait_ge(s_rt_ready, 8)
                else:
                    pe.wait_ge(s_tab_in, 32)
                for n in range(4):
                    for w in range(2):
                        b = take_dv(("V", h, n, w))
                        for r in range(4):
                            for f in range(2):
                                g = 2 * (4 * n + r) + f
                                m = TE.matmul(b[f * S:(f + 1) * S, r * P:(r + 1) * P], RT[:, g, w * S:(w + 1) * S],
                                              UT[:, g, :], start=True, stop=True)
                        m.then_inc(s_dv_full, 1)

            def z_conv(h):
                for q in range(CT):
                    pe.wait_ge([s_wz_in0, s_wz_in1][q % 2], (96, 80)[q % 2] * h + 16 + 32 * (q // 2 + 1))
                    for b2 in range(2):
                        for w in range(2):
                            b = take_mm(("zc", h, q, b2, w))
                            for k in range(KD):
                                m = TE.matmul(b[:, :], wz_conv(q)[:, w, k, :], hT[:, k, b2 * 512:(b2 + 1) * 512],
                                              start=(k == 0), stop=(k == KD - 1))
                            m.then_inc(s_mm_full, 1)

            def outputs(h):
                pe.wait_ge(s_tab_in, 16 + 32 * h)
                for n in range(8):
                    b = take_mm(("Y", h, n))
                    pe.wait_ge(s_states_ready, 4 * h + n // 2 + 1)
                    for j in range(4):
                        g = 8 * (n // 2) + 2 * j + n % 2
                        r, lo = g // 2, (n % 2) * S
                        o = b[:, j * P:(j + 1) * P]
                        TE.matmul(o, UT[:, g, :], TOE[:, g, :], start=True, stop=False)
                        TE.matmul(o, SR[lo:lo + S, r, :], COR[lo:lo + S, r, :], start=False, stop=False)
                        m = TE.matmul(o, SI[lo:lo + S, r, :], COI[lo:lo + S, r, :], start=False, stop=True)
                    m.then_inc(s_mm_full, 1)

            def g_transposed(h):
                for q in range(CT):
                    pe.wait_ge(s_mm_free, MMN["Y", h, 2 * q + 1] + 1)
                    for c in range(2):
                        b = take_tp(("GT", h, q, c))
                        for i in range(4):
                            m = TE.transpose(b[:, i * P:(i + 1) * P], GA[:, q, 4 * c + i, :], ident[:, :])
                        m.then_inc(s_tp_full, 1)

            def glu(h):
                pe.wait_ge(s_tp_free, TPN["GT", h, CT - 1, 1] + 1)
                pe.wait_ge(s_wz_in0, 96 * (h + 1))
                for b2 in range(2):
                    for o in range(CT):
                        b = take_mm(("glu", h, b2, o))
                        for q in range(CT):
                            m = TE.matmul(b[:, :], wz[:, 0, q * CC + o * P:q * CC + (o + 1) * P], gT[:, q, b2 * 512:(b2 + 1) * 512],
                                          start=(q == 0), stop=(q == CT - 1))
                        m.then_inc(s_mm_full, 1)

            def norm_turns(h):
                pe.wait_ge(s_conv_ready, CT * (h + 1))
                for i in range(TPH + 1):
                    if i < TPH:
                        b = take_tp(("LF", h, i))
                        for q in range(CT):
                            m = TE.transpose(b[:, q * P:(q + 1) * P], cacc[:, q, i * P:(i + 1) * P], ident[:, :])
                        m.then_inc(s_tp_full, 1)
                    if i >= 1:
                        b = take_tp(("LB", h, i - 1))
                        pe.wait_ge(s_yn_ready, h * TPH + i)
                        for q in range(CT):
                            m = TE.transpose(b[:, q * P:(q + 1) * P], yn[:, q * P:(q + 1) * P], ident[:, :])
                        m.then_inc(s_tp_full, 1)

            for h in range(NH):
                to_hT(h)
                z_ssm(h)
                u_transposed(h)
                inputs_to_state(h)
                if h == 1:
                    norm_turns(0)
                z_conv(h)
                outputs(h)
                g_transposed(h)
                glu(h)
            norm_turns(1)

            pe.wait_ge(s_mm_free, len(mmk))
            pe.wait_ge(s_tp_free, len(tpk))
            pe.wait_ge(s_dv_free, len(dvk))
            pe.wait_ge(s_wout_ready, KD)
            pe.wait_ge(s_wr_in, 32)

            def turn_h2(i):
                pe.wait_ge(s_h2_ready, i + 1)
                if i:
                    pe.wait_ge(s_h2t_free, i)
                for k in range(KD):
                    m = TE.transpose(psm[:, 2 + k // 4, (k % 4) * P:(k % 4 + 1) * P], h2b[:, i % 2, k * P:(k + 1) * P], ident[:, :])
                m.then_inc(s_h2t_full, 1)

            def route(i):
                pe.wait_ge(s_h2t_free, i + 1)
                if i:
                    pe.wait_ge(s_sc_ready, i)
                for k in range(KD):
                    m = TE.matmul(psm[:, 7, 0:E], h2T[:, k, :], wr[:, k, :], start=(k == 0), stop=(k == KD - 1))
                m.then_inc(s_lg_full, 1)

            for i in range(NT + 2):
                if i < NT:
                    pe.wait_ge(s_sqm_ready, i + 1)
                    if i:
                        pe.wait_ge(s_ssn_ready, i)
                    for f in range(2):
                        for q in range(CT):
                            m = TE.matmul(psm[:, 6, f:f + 1], sqb[:, f * CT + q, :], one[:, :], start=(q == 0), stop=(q == CT - 1))
                    m.then_inc(s_ss_full, 1)
                    pe.wait_ge([s_mix_in0, s_mix_in1][i % 2], 16 * (i // 2 + 1))
                    if i:
                        pe.wait_ge(s_oa_ready, i)
                    for c in range(2):
                        for q in range(CT):
                            m = TE.matmul(psm[:, c, :], mixb[:, i % 2, q, :], wout[:, q, c * 512:(c + 1) * 512],
                                          start=(q == 0), stop=(q == CT - 1))
                    m.then_inc(s_oa_full, 1)
                if i >= 2:
                    turn_h2(i - 2)
                if i < NT:
                    if i:
                        pe.wait_ge(s_o_ready, i)
                    for c in range(2):
                        for q in range(CT):
                            m = TE.matmul(psm[:, 4 + c, :], mixb[:, i % 2, CT + q, :], wout[:, CT + q, c * 512:(c + 1) * 512],
                                          start=(q == 0), stop=(q == CT - 1))
                    m.then_inc(s_ob_full, 1)
                if i >= 2:
                    route(i - 2)
            pe.wait_ge(s_sel_ready, NT)
            pe.wait_ge(s_const_ok, 1)
            for i in range(NT):
                o = psm[:, 6 + i // 8, (i % 8) * E:(i % 8 + 1) * E]
                TE.matmul(o, tri[:, :], selbf[:, i, :], start=True, stop=False)
                TE.matmul(o, oneb[:, :], selcum[:, i, :], start=False, stop=True)
            TE.matmul(psm[:, 1, DE:DE + E], oneb[:, :], selcum[:, NT, :], start=True, stop=True).then_inc(s_pos_full, 1)

            def turn_rows(b, routed=False):
                if routed:
                    pe.wait_ge(s_xr_in, (b - (NT - 1)) * 16)
                else:
                    pe.wait_ge(s_xg_in, (b + 1) * 16)
                for k in range(KD):
                    m = TE.transpose(psm[:, 2 + k // 4, (k % 4) * P:(k % 4 + 1) * P], xg[:, k * P:(k + 1) * P], ident[:, :])
                m.then_inc(s_xt_full, 1)

            def block(b, base, first=False, routed=False):
                pe.wait_ge(s_xt_act, b + 1)
                pe.wait_ge(s_xt_dve, b + 1)
                for k in range(KD):
                    m = TE.matmul(psm[:, 0, :], XT[:, k, :], arena[:, bass.ds(base + k * 2 * DE, 2 * DE)],
                                  start=(k == 0), stop=(k == KD - 1))
                m.then_inc(s_gu_full, 1)
                turn_rows(b + 1, routed)
                pe.wait_ge(s_h_full, b + 1)
                for f in range(FE):
                    m = TE.transpose(psm[:, 1, f * P:(f + 1) * P], hs[:, f * P:(f + 1) * P], ident[:, :])
                m.then_inc(s_ht_full, 1)
                pe.wait_ge(s_ht_ready, b + 1)
                if not first:
                    pe.wait_ge(s_y_act, b)
                    pe.wait_ge(s_y_dve, b)
                for c in range(2):
                    for f in range(FE):
                        m = TE.matmul(psm[:, (4, 5)[c], :], hTs[:, f, :], arena[:, bass.ds(base + 4096 + f * D + c * 512, 512)],
                                      start=(f == 0), stop=(f == FE - 1))
                m.then_inc(s_y_full, 1)

            turn_rows(0)
            pe.wait_ge(s_wa_in, 48)
            block(0, EG0, first=True)
            with pe.Fori(1, NT - 1) as b:
                block(b, EG0)
            block(NT - 1, EG0, routed=True)
            pe.wait_ge(s_be_back, 16)
            pe.wait_ge(s_cnt_ready, 1)
            nb = pe.value_load(pint[0:1, E - 1:E], min_val=1, max_val=NB)
            with pe.Fori(NT, nb + NT) as b:
                e = pe.value_load(berow[0:1, bass.ds(b - NT, 1)], min_val=0, max_val=E - 1)
                pe.wait_ge(s_wa_in, ((e + 1) >> 1) * 48 + 48)
                pe.wait_ge(s_wb_in, ((e + 2) >> 1) * 48)
                block(b, ((e + 1) & 1) * WSTEP + EG0, routed=True)

        @blk.scalar
        def _(act):
            ch = Chain(act, s_act_step)
            act.wait_ge(s_par_in, 16 * NFIRST)
            SC.activation(csig[:, :], ccol[:, :], ACT.Sigmoid).then_inc(s_csig_ok, 1)
            ch.do(SC.activation(ndt[:, 1:2], ndt[:, 0:1], ACT.Exp))
            SC.mul(ndt[:, 2:3], ndt[:, 1:2], 8.0).then_inc(s_dt_ready, 1)
            act.wait_ge(s_dt_ready, 1)
            ch.add(SC.activation(nmag, nar, ACT.Exp, scale=ndt[:, 1:2]))
            ch.add(SC.activation(nm8, nar, ACT.Exp, scale=ndt[:, 2:3]))
            act.wait_ge(s_nat_angle, 1)
            ch.add(SC.activation(nsin, nr_, ACT.Sin))
            ch.add(SC.activation(ncos, nr_, ACT.Sin, scale=0.5))
            ch.add(SC.activation(ns8, nn, ACT.Sin))
            ch.add(SC.activation(nc8, nn, ACT.Sin, scale=0.5))
            ch.sync()
            SC.copy(nden, nar).then_inc(s_nat_trig, 1)

            xin = [s_x_in0, s_x_in1, s_x_in2]

            def to_hT(h):
                def square(n):
                    act.wait_ge(xin[n % 3], 16 * (n // 3 + 1))
                    if n:
                        act.wait_ge(s_sq_ready, n)
                    elif h == 0:
                        act.wait_ge(s_toe_ready, 1)
                    SC.activation(work[:, 2048:3072], xb[:, n % 3, :], ACT.Square, accum_out=st[:, n:n + 1]).then_inc(s_sq_ready, 1)

                def evac(i):
                    for c in range(2):
                        n = TPN["hT", h, i, c]
                        act.wait_ge(s_tp_full, n + 1)
                        SC.copy(hT[:, 4 * c:4 * c + 4, i * P:(i + 1) * P], tp[n % 2].rearrange("p (k t) -> p k t", k=4)).then_inc(s_tp_free, 1)

                if h:
                    act.wait_ge(s_sg_free, SGN["glu", 0, 1, CT - 1] + 1)
                square(h * TPH)
                for i in range(TPH):
                    n = h * TPH + i
                    if i + 1 < TPH:
                        square(n + 1)
                    act.wait_ge(s_stat_ready, n + 1)
                    SC.activation(xb[:, n % 3, :], xb[:, n % 3, :], ACT.Copy, scale=st[:, 32 + n:33 + n]).then_inc(s_xr_ready, 1)
                    if i:
                        evac(i - 1)
                evac(TPH - 1)

            def z_ssm(h):
                for j in range(CH):
                    n = MMN["zs", h, j]
                    act.wait_ge(s_mm_full, n + 1)
                    SC.copy(U[:, :, j, :], mm[n % 2].rearrange("p (g h) -> p g h", g=G)).then_inc(s_mm_free, 1)

            def u_transposed(h):
                for n in range(8):
                    k = TPN["UT", h, n]
                    act.wait_ge(s_tp_full, k + 1)
                    SC.copy(ut[:, n * 512:(n + 1) * 512], tp[k % 2]).then_inc(s_tp_free, 1)

            def z_conv(h):
                for q in range(CT):
                    for b in range(2):
                        n = MMN["zc", h, q, b, 0]
                        act.wait_ge(s_mm_full, n + 1)
                        if h and b == 0:
                            act.wait_ge(s_v_tail, q + 1)
                        if h == 0 and q == 0 and b == 0:
                            act.wait_ge(s_tab_out, 48)
                        SC.copy(v[:, q, PAD + b * 512:PAD + (b + 1) * 512], mm[n % 2]).then_inc(s_mm_free, 1)
                        act.wait_ge(s_mm_full, n + 2)
                        k = SGN["zc", h, q, b]
                        if k >= 2:
                            act.wait_ge(s_sg_free, k - 1)
                        SC.activation(sg[k % 2], mm[(n + 1) % 2], ACT.Sigmoid).then_inc(s_mm_free, 1)

            def outputs(h):
                for n in range(8):
                    k = MMN["Y", h, n]
                    act.wait_ge(s_mm_full, MMN["Y", h, n | 1] + 1)
                    o = GA[:, n // 2].rearrange("p i (g f h) -> p f g i h", f=2, h=HG)[:, n % 2]
                    SC.activation(o, mm[k % 2].rearrange("p (g i h) -> p g i h", g=4, i=CH), ACT.Gelu_apprx_tanh).then_inc(s_mm_free, 1)

            def g_transposed(h):
                for q in range(CT):
                    for c in range(2):
                        n = TPN["GT", h, q, c]
                        act.wait_ge(s_tp_full, n + 1)
                        o = gT[:, q, :].rearrange("p (c i) -> p i c", i=CH)[:, 4 * c:4 * c + 4, :]
                        SC.copy(o, tp[n % 2].rearrange("p (i c) -> p i c", i=4)).then_inc(s_tp_free, 1)

            def glu(h):
                for b in range(2):
                    for q in range(CT):
                        n = MMN["glu", h, b, q]
                        k = SGN["glu", h, b, q]
                        act.wait_ge(s_mm_full, n + 1)
                        act.wait_ge(s_sg_free, k - 1)
                        SC.activation(sg[k % 2], mm[n % 2], ACT.Sigmoid, bias=col[:, 3, q:q + 1]).then_inc(s_mm_free, 1)

            def norm_turns(h):
                for i in range(TPH + 1):
                    if i < TPH:
                        n = TPN["LF", h, i]
                        act.wait_ge(s_tp_full, n + 1)
                        if h * TPH + i:
                            act.wait_ge(s_yn_ready, h * TPH + i)
                        SC.copy(ytok[:, :], tp[n % 2]).then_inc(s_tp_free, 1)
                    if i >= 1:
                        n = TPN["LB", h, i - 1]
                        k = SGN["ln", h, i - 1]
                        act.wait_ge(s_tp_full, n + 1)
                        act.wait_ge(s_sg_free, k)
                        for q in range(CT):
                            m = SC.activation(ly[:, q * P:(q + 1) * P], tp[n % 2][:, q * P:(q + 1) * P], ACT.Identity,
                                              bias=col[:, 2, q:q + 1], scale=col[:, 1, q:q + 1])
                        m.then_inc(s_tp_free, 1)
                        act.wait_ge(s_tp_free, n + 1)
                        SC.activation(sg[k % 2], ly[:, :], ACT.Sigmoid).then_inc(s_ly_full, 1)

            for h in range(NH):
                to_hT(h)
                z_ssm(h)
                u_transposed(h)
                if h == 1:
                    norm_turns(0)
                z_conv(h)
                outputs(h)
                g_transposed(h)
                glu(h)
            norm_turns(1)

            def square_mix(i):
                act.wait_ge([s_mix_in0, s_mix_in1][i % 2], 16 * (i // 2 + 1))
                if i:
                    act.wait_ge(s_ss_full, i)
                SC.activation(us[:, 2048:3072], us[:, (i % 2) * 1024:(i % 2 + 1) * 1024], ACT.Square).then_inc(s_sqm_ready, 1)

            square_mix(0)
            for i in range(NT + 2):
                c0 = 16 * (i % 2)
                if i < NT:
                    act.wait_ge(s_oa_full, i + 1)
                    act.wait_ge(s_rr_ready, i + 1)
                    if i:
                        act.wait_ge(s_x1_ready, i)
                    SC.activation(ob, psm[:, 0:2, :].rearrange("p a n -> p (a n)"), ACT.Copy, scale=st[:, c0 + 2:c0 + 3]).then_inc(s_oa_ready, 1)
                if i + 1 < NT:
                    square_mix(i + 1)
                if i >= 2:
                    act.wait_ge(s_h2t_full, i - 1)
                    if i >= 3:
                        act.wait_ge(s_lg_full, i - 2)
                    SC.copy(us[:, 3072:4096], psm[:, 2:4, :].rearrange("p a n -> p (a n)")).then_inc(s_h2t_free, 1)
                if i < NT:
                    act.wait_ge(s_o_ready, i + 1)
                    if i:
                        act.wait_ge(s_s1_ready, i)
                    SC.activation(junk, ob, ACT.Square, accum_out=st[:, c0 + 4:c0 + 5]).then_inc(s_so_ready, 1)
                if i >= 2:
                    act.wait_ge(s_lg_full, i - 1)
                    if i >= 3:
                        act.wait_ge(s_sel_ready, i - 2)
                    SC.activation(scores, psm[:, 7, 0:E], ACT.Sigmoid).then_inc(s_sc_ready, 1)
                if i < NT:
                    act.wait_ge(s_x1_ready, i + 1)
                    act.wait_ge(s_so_ready, i + 1)
                    SC.activation(junk, xb[:, i % 2, :], ACT.Square, accum_out=st[:, c0 + 7:c0 + 8]).then_inc(s_s1_ready, 1)

            def rows_evac(b, first=False):
                act.wait_ge(s_xt_full, b + 1)
                if not first:
                    act.wait_ge(s_gu_full, b)
                SC.copy(XT[:, 0:4, :], tp[0].rearrange("p (k t) -> p k t", k=4)).then_inc(s_xt_act, 1)

            def block(b, first=False, routed=False):
                act.wait_ge(s_gu_full, b + 1)
                if not first:
                    act.wait_ge(s_h_full, b)
                SC.activation(sigb, psm[:, 0, 0:DE], ACT.Sigmoid).then_inc(s_sig_ready, 1)
                rows_evac(b + 1)
                act.wait_ge(s_ht_full, b + 1)
                if not first:
                    act.wait_ge(s_y_full, b)
                SC.copy(work[:, 1792:2048], psm[:, 1, 0:DE]).then_inc(s_ht_ready, 1)
                act.wait_ge(s_y_full, b + 1)
                if routed:
                    act.wait_ge(s_y_free, b - (NT - 1))
                elif not first:
                    act.wait_ge(s_y_out, b * 16)
                SC.copy(yb[:, 0:512], dv[0]).then_inc(s_y_act, 1)

            rows_evac(0, first=True)
            block(0, first=True)
            with act.Fori(1, NT) as b:
                block(b)
            act.wait_ge(s_cnt_ready, 1)
            nb = act.value_load(pint[0:1, E - 1:E], min_val=1, max_val=NB)
            with act.Fori(NT, nb + NT) as b:
                block(b, routed=True)
            fin_in = [s_fin_in0, s_fin_in1, s_fin_in2]
            for i in range(NT):
                act.wait_ge(fin_in[i % 3], 16 * (i // 3 + 1))
                if i:
                    act.wait_ge(s_fs_ready, i)
                SC.activation(yb, xb[:, i % 3, :], ACT.Square, accum_out=st[:, i:i + 1]).then_inc(s_fs_ready, 1)

        @blk.vector
        def _(dve):
            ch = Chain(dve, s_dve_step)
            tt, ts, stt = V.tensor_tensor, V.tensor_scalar, V.scalar_tensor_tensor
            do, add, sync = ch.do, ch.add, ch.sync

            def got(key):
                n = DVN[key]
                dve.wait_ge(s_dv_full, n + 1)
                return dv[n % 4]

            dve.wait_ge(s_csig_ok, 1)
            V.tensor_mul(ccol[:, :], ccol[:, :], csig[:, :]).then_inc(s_csig_ok, 1)
            dve.wait_ge(s_dt_ready, 1)
            do(ts(nth, nai, ndt[:, 1:2], None, ALU.mult))
            for mul_, o in ((1.0, nr_), (float(CH), nn)):
                do(ts(nt1, nth, mul_, None, ALU.mult))
                do(ts(nt2, nt1, 1.0 / (2 * np.pi), MAGIC, ALU.mult, ALU.add))
                do(ts(nt2, nt2, MAGIC, None, ALU.subtract))
                for c in (C1, C2, C3):
                    do(stt(nt1, nt2, -c, nt1, ALU.mult, ALU.add))
                do(ts(o, nt1, 3.1415925, -3.1415925, ALU.min, ALU.max))
            V.tensor_copy(nt3.rearrange("g (j h) -> g j h", j=CH),
                          nd[:, 0:HG].unsqueeze(1).to_broadcast([G, CH, HG])).then_inc(s_nat_angle, 1)
            dve.wait_ge(s_nat_trig, 1)
            do(tt(ncos, ncos, ncos, ALU.mult), tt(nc8, nc8, nc8, ALU.mult))
            do(ts(ncos, ncos, -2.0, 1.0, ALU.mult, ALU.add), ts(nc8, nc8, -2.0, 1.0, ALU.mult, ALU.add))
            do(tt(nlr, nmag, ncos, ALU.mult), tt(nli, nmag, nsin, ALU.mult))
            do(tt(nt1, nar, nar, ALU.mult), tt(nt2, nai, nai, ALU.mult))
            do(tt(nden, nt1, nt2, ALU.add), ts(nth, nlr, -1.0, None, ALU.add))
            do(V.reciprocal(nden, nden), tt(nt1, nth, nar, ALU.mult), tt(nt2, nli, nai, ALU.mult))
            do(tt(nkr, nt1, nt2, ALU.add))
            do(tt(nt1, nli, nar, ALU.mult), tt(nt2, nth, nai, ALU.mult))
            do(tt(nki, nt1, nt2, ALU.subtract), tt(nkr, nkr, nden, ALU.mult))
            do(tt(nki, nki, nden, ALU.mult))
            V.tensor_copy(nt1, nki).then_inc(s_nat_ready, 1)
            b = got(("nat", 0))
            dve.wait_ge(s_nat_ready, 1)
            add(V.tensor_copy(cw[:, :, :], b[:, 8 * G:8 * G + CT * TAPS].rearrange("p (q t) -> p q t", q=CT)))
            V.tensor_copy(dup, b[:, 0:8 * G].rearrange("p (n g) -> p n g", n=8)).then_inc(s_dv_free, 1)
            dve.wait_ge(s_dv_free, 1)
            LR_, LI_, KR, KI, M8, C8, S8, DC = (dup[:, n, :] for n in range(8))
            halves = ((0, S, 0), (S, P, 1))

            def powers():
                do(V.memset(L[:, 0, 0, :], 1.0), V.memset(L[:, 1, 0, :], 0.0), V.memset(last[:, :, :], 0.0))
                t = [PT[0][:, n * G:(n + 1) * G] for n in range(4)]
                for k in range(1, CH + 1):
                    do(tt(t[0], L[:, 0, k - 1], LR_, ALU.mult), tt(t[1], L[:, 1, k - 1], LI_, ALU.mult),
                       tt(t[2], L[:, 0, k - 1], LI_, ALU.mult), tt(t[3], L[:, 1, k - 1], LR_, ALU.mult))
                    do(tt(L[:, 0, k], t[0], t[1], ALU.subtract), tt(L[:, 1, k], t[2], t[3], ALU.add))
                for lo, hi, f in halves:
                    pick = lambda a: a.rearrange("p (r f) -> p f r", f=2)[:, f, :]
                    for w in range(2):
                        add(V.tensor_copy(LP[lo:hi, w], L[lo:hi, w].rearrange("p k (r f) -> p f k r", f=2)[:, f]))
                        add(V.tensor_copy(lam8[lo:hi, w], pick(L[lo:hi, w, CH])))
                    for n, a in ((2, M8), (3, C8), (4, S8)):
                        add(V.tensor_copy(lam8[lo:hi, n], pick(a[lo:hi])))
                sync()

            def inputs():
                dve.wait_ge(s_small_in, 16 * NSMALL)
                do(ts(X2[0:S], X2[0:S], -1.0, None, ALU.mult))
                kr, ki = (a.unsqueeze(2).to_broadcast([P, G, HG]) for a in (KR, KI))
                t = [PT[0][:, 0:512].rearrange("p (g h) -> p g h", g=G), PT[0][:, 512:1024].rearrange("p (g h) -> p g h", g=G),
                     PT[1][:, 0:512].rearrange("p (g h) -> p g h", g=G), PT[1][:, 512:1024].rearrange("p (g h) -> p g h", g=G)]
                do(tt(t[0], X1, kr, ALU.mult), tt(t[1], X2, ki, ALU.mult), tt(t[2], X2, kr, ALU.mult), tt(t[3], X1, ki, ALU.mult))
                do(tt(BB1, t[0], t[1], ALU.add), tt(BB2, t[2], t[3], ALU.subtract), V.memset(R[:, :, CH:, :], 0.0))
                do(ts(CN[:, 0, :, S:P], CN[:, 0, :, S:P], -1.0, None, ALU.mult))
                V.tensor_copy(ndt[:, 3:4], ndt[:, 0:1]).then_inc(s_c_ready, 1)

            def input_powers(ks):
                for k in ks:
                    t = [PT[2 * (k % 2)][:, 0:512].rearrange("p (g h) -> p g h", g=G), PT[2 * (k % 2) + 1][:, 0:512].rearrange("p (g h) -> p g h", g=G)]
                    do(tt(t[0], BB1, L[:, 0, k].unsqueeze(2).to_broadcast([P, G, HG]), ALU.mult),
                       tt(t[1], BB2, L[:, 1, k].unsqueeze(2).to_broadcast([P, G, HG]), ALU.mult))
                    m = tt(R[:, :, CH - 1 - k, :], t[0], t[1], ALU.add)
                    add(m)
                sync()
                if ks[-1] == CH - 1:
                    V.tensor_copy(ndt[:, 3:4], ndt[:, 0:1]).then_inc(s_r_ready, 1)

            cm = bn[:, 0:4]
            cmt = [PT[3][:, n * NPR:(n + 1) * NPR] for n in range(6)]

            def phasors(ms):
                for m in ms:
                    if m == 1:
                        do(V.memset(EC[:, :, 0], 1.0), V.memset(ES[:, :, 0], 0.0), V.tensor_copy(cmt[0], lam8[:, 3]), V.tensor_copy(cmt[1], lam8[:, 4]))
                    t = [PT[n][:, 0:NPR * min(m, 64)].rearrange("p (r c) -> p r c", r=NPR) for n in range(3)]
                    cr, ci = (cmt[n].unsqueeze(2).to_broadcast([P, NPR, m]) for n in range(2))
                    do(tt(t[0], EC[:, :, 0:m], cr, ALU.mult), tt(t[1], ES[:, :, 0:m], ci, ALU.mult), tt(t[2], ES[:, :, 0:m], cr, ALU.mult))
                    do(tt(EC[:, :, m:2 * m], t[0], t[1], ALU.subtract))
                    do(tt(t[0], EC[:, :, 0:m], ci, ALU.mult), tt(cmt[2], cmt[0], cmt[0], ALU.mult), tt(cmt[3], cmt[1], cmt[1], ALU.mult), tt(cmt[4], cmt[0], cmt[1], ALU.mult))
                    do(tt(ES[:, :, m:2 * m], t[0], t[2], ALU.add), tt(cmt[0], cmt[2], cmt[3], ALU.subtract), ts(cmt[1], cmt[4], 2.0, None, ALU.mult))
                if ms[-1] == 64:
                    V.tensor_copy(ndt[:, 3:4], ndt[:, 0:1]).then_inc(s_phasor_ready, 1)

            pieces = [powers, inputs, lambda: input_powers([0, 1, 2, 3]), lambda: input_powers([4, 5, 6, 7]),
                      lambda: phasors([1, 2, 4]), lambda: phasors([8, 16]), lambda: phasors([32]), lambda: phasors([64])]
            for n in range(12):
                b = got(("ada", n))
                dve.wait_ge([s_ada_in0, s_ada_in1][n % 2], 32 * (n // 2 + 1))
                if n >= 2:
                    dve.wait_ge([s_mod_out0, s_mod_out1][n % 2], 16 * (n // 2))
                tt(seg[0:1, n % 2, :], b[0:1, :], segb[n % 2][0:1, :], ALU.add).then_inc(s_dv_free, 1)
                dve.wait_ge(s_dv_free, DVN["ada", n] + 1)
                V.tensor_copy(ndt[:, 3:4], ndt[:, 0:1]).then_inc(s_seg_ok, 1)
                if n < len(pieces):
                    pieces[n]()
            b = got(("C", 0))
            V.tensor_copy(Y1.rearrange("p g h -> p (g h)"), b).then_inc(s_dv_free, 1)
            for n, o in ((1, CRP), (2, CIP)):
                b = got(("C", n)).rearrange("p (r f h) -> p f r h", f=2, h=HG)
                add(V.tensor_copy(o[0:S], b[0:S, 0]))
                V.tensor_copy(o[S:P], b[S:P, 1]).then_inc(s_dv_free, 1)
            sync()
            dve.wait_ge(s_dv_free, DVN["C", 2] + 1)
            V.tensor_copy(ndt[:, 3:4], ndt[:, 0:1]).then_inc(s_c_ready, 1)
            for n in range(8):
                b = got(("RT", n))
                V.tensor_copy(tabs[:, n * 512:(n + 1) * 512], b).then_inc(s_dv_free, 1)
                dve.wait_ge(s_dv_free, DVN["RT", n] + 1)
                V.tensor_copy(ndt[:, 3:4], ndt[:, 0:1]).then_inc(s_rt_ready, 1)
            for n in range(8):
                b = got(("TOE", n))
                for j in range(4):
                    g = 4 * n + j
                    m = stt(ctoe[:, g, :], ident[:, :], DC[:, g:g + 1], b[:, j * P:(j + 1) * P], ALU.mult, ALU.add)
                    if j == 3:
                        m.then_inc(s_dv_free, 1)
                    else:
                        add(m)
                lr, li = (LP[:, w, n + 1].unsqueeze(2).to_broadcast([P, NPR, HG]) for w in range(2))
                t = [PT[j][:, 0:256].rearrange("p (r h) -> p r h", r=NPR) for j in range(4)]
                do(tt(t[0], CRP, lr, ALU.mult), tt(t[1], CIP, li, ALU.mult), tt(t[2], CRP, li, ALU.mult), tt(t[3], CIP, lr, ALU.mult))
                do(tt(ccor[:, :, n, :], t[0], t[1], ALU.subtract), stt(ccoi[:, :, n, :], t[2], -1.0, t[3], ALU.mult, ALU.subtract))
            dve.wait_ge(s_dv_free, DVN["TOE", 7] + 1)
            V.tensor_copy(ndt[:, 3:4], ndt[:, 0:1]).then_inc(s_toe_ready, 1)
            dve.wait_ge(s_rows_in, 48)
            stt(arow, arow, 1.0, xb[:, 2, :], ALU.add, ALU.mult).then_inc(s_arow_ready, 1)
            dve.wait_ge(s_tab_out, 48)
            do(V.memset(v[:, :, 0:PAD], 0.0))

            def states(h):
                if h:
                    dve.wait_ge(s_et_in, 16)
                    c8, s8, l0, l1 = lam8[:, 3], lam8[:, 4], last[:, 0], last[:, 1]
                    t = [rot[:, n, 0:NPR] for n in range(4)]
                    do(tt(t[0], c8, l0, ALU.mult), tt(t[1], s8, l1, ALU.mult), tt(t[2], s8, l0, ALU.mult), tt(t[3], c8, l1, ALU.mult))
                    do(tt(last[:, 2], t[0], t[1], ALU.subtract), tt(last[:, 3], t[2], t[3], ALU.add))
                t = [rot[:, n, :].rearrange("p (r c) -> p r c", r=4) for n in range(4)]
                for n in range(4):
                    r = slice(4 * n, 4 * n + 4)
                    vr = got(("V", h, n, 0)).rearrange("p (r c) -> p r c", r=4)
                    add(tt(t[0], vr, EC[:, r], ALU.mult))
                    tt(t[3], vr, ES[:, r], ALU.mult).then_inc(s_dv_free, 1)
                    vi = got(("V", h, n, 1)).rearrange("p (r c) -> p r c", r=4)
                    add(tt(t[1], vi, ES[:, r], ALU.mult))
                    tt(t[2], vi, EC[:, r], ALU.mult).then_inc(s_dv_free, 1)
                    sync()
                    dve.wait_ge(s_dv_free, DVN["V", h, n, 1] + 1)
                    do(tt(SR[:, r], t[0], t[1], ALU.add), tt(SI[:, r], t[2], t[3], ALU.subtract))
                    for q in range(4 * n, 4 * n + 4):
                        for w, a in ((0, SR), (1, SI)):
                            add(V.tensor_tensor_scan(a[:, q, :], lam8[:, 2, q:q + 1].to_broadcast([P, NC]), a[:, q, :],
                                                     last[:, 2 + w, q:q + 1] if h else 0.0, ALU.mult, ALU.add))
                    sync()
                    do(tt(t[0], SR[:, r], EC[:, r], ALU.mult), tt(t[1], SI[:, r], ES[:, r], ALU.mult),
                       tt(t[2], SR[:, r], ES[:, r], ALU.mult), tt(t[3], SI[:, r], EC[:, r], ALU.mult))
                    for w, (a, x0, x1, op) in enumerate(((SR, t[0], t[1], ALU.subtract), (SI, t[2], t[3], ALU.add))):
                        add(tt(a[:, r, 1:NC], x0[:, :, 0:NC - 1], x1[:, :, 0:NC - 1], op))
                        if h == 0:
                            add(tt(last[:, w, r], x0[:, :, NC - 1], x1[:, :, NC - 1], op))
                            add(V.memset(a[:, r, 0:1], 0.0))
                        else:
                            add(V.tensor_copy(a[:, r, 0], last[:, w, r]))
                    sync()
                    V.tensor_copy(ndt[:, 3:4], ndt[:, 0:1]).then_inc(s_states_ready, 1)

            def conv(h):
                if h:
                    dve.wait_ge(s_tp_full, TPN["LF", 0, TPH - 1] + 1)
                for q in range(CT):
                    dve.wait_ge(s_v_ready, (h * CT + q + 1) * 2)
                    o = cacc[:, q, :]
                    do(ts(o, v[:, q, 0:HT], cw[:, q, 0:1], col[:, 0, q:q + 1], ALU.mult, ALU.add))
                    for k in range(1, TAPS):
                        m = stt(o, v[:, q, k:k + HT], cw[:, q, k:k + 1], o, ALU.mult, ALU.add)
                        if k < TAPS - 1:
                            do(m)
                        else:
                            m.then_inc(s_conv_ready, 1)
                    if h == 0:
                        dve.wait_ge(s_conv_ready, q + 1)
                        V.tensor_copy(v[:, q, 0:PAD], v[:, q, HT:HT + PAD]).then_inc(s_v_tail, 1)

            def norm_stats(h):
                for i in range(TPH):
                    k = h * TPH + i
                    dve.wait_ge(s_tp_free, TPN["LF", h, i] + 1)
                    if k:
                        dve.wait_ge(s_yn_ready, k)
                    do(V.bn_stats(bn[:, 0:6], ytok[:, :]))
                    V.bn_aggr(bn[:, 6:8], bn[:, 0:6]).then_inc(s_bn_ready, 1)
                    dve.wait_ge(s_bn_ready, k + 1)

            states(0)
            conv(0)
            states(1)
            norm_stats(0)
            conv(1)
            norm_stats(1)

            dve.wait_ge(s_row_in, 7 * 16)
            do(tt(rows[:, 0], rows[:, 0], rtmp[:, 0], ALU.mult), stt(rows[:, 1], rows[:, 1], 1.0, rtmp[:, 1], ALU.add, ALU.mult),
               tt(rows[:, 3], rows[:, 3], rtmp[:, 2], ALU.mult), V.memset(selcum[:, 0, :], 0.0), V.memset(ones64, 1.0))
            V.tensor_copy(ndt[:, 3:4], ndt[:, 0:1]).then_inc(s_row_ready, 1)
            dve.wait_ge(s_wr_in, 32)

            def choose(i):
                dve.wait_ge(s_sc_ready, i + 1)
                do(tt(biased, scores, rbias, ALU.add))
                for g in range(NG):
                    add(V.max(v8[:, g, :], biased[:, g * 8:(g + 1) * 8]))
                sync()
                do(tt(gs, v8[:, :, 0], v8[:, :, 1], ALU.add))
                mine, other = gs.unsqueeze(2).to_broadcast([P, NG, NG]), gs.unsqueeze(1).to_broadcast([P, NG, NG])
                do(tt(cmpa, other, mine, ALU.is_gt), tt(cmpb, other, mine, ALU.is_equal))
                do(tt(cmpb, cmpb, sel8[:, :, :], ALU.mult))
                do(tt(cmpa, cmpa, cmpb, ALU.add))
                do(V.tensor_reduce(rank, cmpa, AX.X, ALU.add))
                do(ts(gm, rank, TOPG - 0.5, None, ALU.is_lt))
                do(ts(gp, gm, -1.0, BIG, ALU.add, ALU.mult))
                b3 = lambda a: a.rearrange("p (g m) -> p g m", g=NG)
                do(tt(b3(bm), b3(biased), gm.unsqueeze(2).to_broadcast([P, NG, 8]), ALU.mult))
                do(tt(b3(bm), b3(bm), gp.unsqueeze(2).to_broadcast([P, NG, 8]), ALU.add))
                do(V.max(t8, bm))
                do(V.match_replace(rep, t8, bm, -3e38))
                do(tt(selall[:, i, :], rep, bm, ALU.not_equal))
                do(V.tensor_copy(selbf[:, i, :], selall[:, i, :]), tt(pen, scores, selall[:, i, :], ALU.mult))
                do(tt(selcum[:, i + 1, :], selcum[:, i, :], selbf[:, i, :], ALU.add), V.tensor_reduce(gsum[:, 0:1], pen, AX.X, ALU.add))
                do(ts(gsum[:, 0:1], gsum[:, 0:1], 1e-20, None, ALU.add))
                do(V.reciprocal(gsum[:, 1:2], gsum[:, 0:1]))
                ts(gwall[:, i, :], pen, gsum[:, 1:2], 2.5, ALU.mult, ALU.mult).then_inc(s_sel_ready, 1)

            dve.wait_ge(s_zero_ok, 1)
            for i in range(NT + 2):
                c0 = 16 * (i % 2)
                if i < NT:
                    dve.wait_ge(s_ss_full, i + 1)
                    ts(st[:, c0:c0 + 2], psm[:, 6, 0:2], 1.0 / CC, EPS, ALU.mult, ALU.add).then_inc(s_ssn_ready, 1)
                    dve.wait_ge(s_ob_full, i + 1)
                    dve.wait_ge(s_oa_ready, i + 1)
                    stt(ob, psm[:, 4:6, :].rearrange("p a n -> p (a n)"), st[:, c0 + 3:c0 + 4], ob, ALU.mult, ALU.add).then_inc(s_o_ready, 1)
                    dve.wait_ge(s_ro_ready, i + 1)
                    stt(ob, ob, st[:, c0 + 6:c0 + 7], rows[:, 0], ALU.mult, ALU.mult).then_inc(s_t_ready, 1)
                    dve.wait_ge(s_r1_ready, i + 1)
                    if i >= 2:
                        dve.wait_ge(s_h2t_full, i - 1)
                        dve.wait_ge([s_h2_out0, s_h2_out1][i % 2], 16 * (i // 2))
                    stt(h2b[:, i % 2, :], xb[:, i % 2, :], st[:, c0 + 9:c0 + 10], rows[:, 1], ALU.mult, ALU.mult).then_inc(s_ha_ready, 1)
                if i >= 2:
                    choose(i - 2)
            dve.wait_ge(s_sel_ready, NT)

            def counts():
                dve.wait_ge(s_pos_full, 1)
                do(ts(cnti, psm[:, 1, DE:DE + E], float(BLK - 1), None, ALU.add))
                do(ts(cnti, cnti, 7, None, ALU.arith_shift_right))
                do(V.tensor_copy(nbf, cnti))
                do(V.tensor_tensor_scan(pend, ones64, nbf, 0.0, ALU.mult, ALU.add))
                do(tt(basef, pend, nbf, ALU.subtract), V.tensor_copy(pint, pend))
                do(ts(basef, basef, float(BLK), 1.0, ALU.mult, ALU.add))
                dve.wait_ge(s_rinit_ready, 1)
                for c in range(2):
                    do(ts(cntf, pend, bidx[:, c:c + 1], None, ALU.is_le))
                    do(V.tensor_reduce(bep[:, c:c + 1], cntf, AX.X, ALU.add))
                do(ts(bep, bep, float(E - 1), None, ALU.min))
                V.tensor_copy(bei, bep).then_inc(s_cnt_ready, 1)

            def positions():
                do(tt(DD, psm[:, 6:8, :].rearrange("p a (i e) -> p (a i) e", e=E), basef.unsqueeze(1).to_broadcast([P, NT, E]), ALU.add))
                do(tt(DD, DD, selall, ALU.mult))
                for i in range(NT):
                    add(V.max(d8[:, i, :], DD[:, i, :]))
                sync()

            def weights(k):
                do(tt(eqb, DD, d8[:, :, k:k + 1].to_broadcast([P, NT, E]), ALU.is_equal))
                do(tt(eqb, eqb, gwall, ALU.mult))
                do(V.tensor_reduce(w8[:, :, k], eqb, AX.X, ALU.add))

            def addresses():
                d = d8.rearrange("p i k -> p (i k)")
                do(ts(qi, d, -1.0, None, ALU.add))
                do(ts(bi, qi, 7, None, ALU.arith_shift_right), ts(qi, qi, BLK - 1, None, ALU.bitwise_and))
                do(V.tensor_copy(bf_, bi), V.tensor_copy(qf, qi))
                do(stt(di, qf, float(NB + 2), bf_, ALU.mult, ALU.add))
                V.tensor_copy(pay[:, :, 1], w8.rearrange("p i k -> p (i k)")).then_inc(s_pay_ready, 1)

            steps = [counts, positions] + [lambda k=k: weights(k) for k in range(TOPK)] + [addresses]
            steps = [counts, positions, lambda: [weights(k) for k in (0, 1)], lambda: [weights(k) for k in (2, 3)],
                     lambda: [weights(k) for k in (4, 5)], lambda: [weights(k) for k in (6, 7)], addresses]

            def rows_evac(b, first=False):
                dve.wait_ge(s_xt_full, b + 1)
                if not first:
                    dve.wait_ge(s_gu_full, b)
                V.tensor_copy(XT[:, 4:8, :], tp[1].rearrange("p (k t) -> p k t", k=4)).then_inc(s_xt_dve, 1)

            def block(b, w, first=False, routed=False):
                dve.wait_ge(s_gu_full, b + 1)
                dve.wait_ge(s_sig_ready, b + 1)
                tt(htmp, psm[:, 0, 0:DE], sigb, ALU.mult).then_inc(s_hm_ready, 1)
                dve.wait_ge(s_hm_ready, b + 1)
                if not first:
                    dve.wait_ge(s_ht_full, b)
                stt(hs, htmp, w, psm[:, 0, DE:2 * DE], ALU.mult, ALU.mult).then_inc(s_h_full, 1)
                rows_evac(b + 1)
                dve.wait_ge(s_y_full, b + 1)
                if routed:
                    dve.wait_ge(s_y_free, b - (NT - 1))
                elif not first:
                    dve.wait_ge(s_y_out, b * 16)
                V.tensor_copy(yb[:, 512:1024], dv[1]).then_inc(s_y_dve, 1)

            rows_evac(0, first=True)
            for b in range(NT):
                block(b, 1.0, first=(b == 0))
                if b < len(steps):
                    steps[b]()
            nb = dve.value_load(pint[0:1, E - 1:E], min_val=1, max_val=NB)
            dve.wait_ge(s_rows_back, 16)
            with dve.Fori(NT, nb + NT) as b:
                block(b, tabl[:, bass.ds(b - NT, 1), 1], routed=True)
            dve.wait_ge(s_xp_in, 16 * NT)
            for i in range(NT):
                dve.wait_ge(s_fr_ready, i + 1)
                x = xb[:, i % 3, :]
                stt(x, x, st[:, 32 + i:33 + i], rows[:, 3], ALU.mult, ALU.mult).then_inc(s_ft_ready, 1)
                dve.wait_ge(s_ft_ready, i + 1)
                tt(x, x, xp[:, i, :], ALU.add).then_inc(s_fo_ready, 1)

        @blk.gpsimd
        def _(pool):
            ch = Chain(pool, s_pool_step)
            do, add = ch.do, ch.add
            do(PO.memset(ident[:, :], 0.0), PO.memset(tri[:, :], 1.0), PO.memset(sel8[:, :, :], 1.0),
               PO.memset(oneb[:, :], 1.0), PO.memset(one[:, :], 1.0), PO.memset(mhalf[:, :], -0.5))
            do(PO.affine_select(out=ident[:, :], in_=ident[:, :], compare_op=ALU.not_equal, fill=1.0, base=0, pattern=[[-1, P]], channel_multiplier=1),
               PO.affine_select(out=tri[:, :], in_=tri[:, :], compare_op=ALU.is_gt, fill=0.0, base=0, pattern=[[1, P]], channel_multiplier=-1),
               PO.affine_select(out=sel8[:, :, :], in_=sel8[:, :, :], compare_op=ALU.is_gt, fill=0.0, base=0, pattern=[[1, NG], [-1, NG]], channel_multiplier=0))
            PO.memset(st[:, 63:64], 0.0).then_inc(s_const_ok, 1)

            def rsqrt(out_, tmp, sq, n, done):
                do(PO.tensor_scalar(tmp, sq, 1.0 / n, EPS, ALU.mult, ALU.add))
                PO.tensor_tensor(out_, tmp, mhalf[:, :], ALU.pow).then_inc(done, 1)

            def to_h(h):
                for i in range(TPH):
                    n = h * TPH + i
                    pool.wait_ge(s_sq_ready, n + 1)
                    rsqrt(st[:, 32 + n:33 + n], st[:, 16 + n:17 + n], st[:, n:n + 1], D, s_stat_ready)
                    if n == 0:
                        pool.wait_ge(s_arow_ready, 1)
                    pool.wait_ge(s_xr_ready, n + 1)
                    x = xb[:, n % 3, :]
                    do(PO.tensor_tensor(x, x, arow, ALU.mult))
                    PO.tensor_tensor(x, x, brow, ALU.add).then_inc(s_xn_ready, 1)

            def gate(h):
                for q in range(CT):
                    for b in range(2):
                        pool.wait_ge(s_mm_free, MMN["zc", h, q, b, 1] + 1)
                        k = SGN["zc", h, q, b]
                        o = v[:, q, PAD + b * 512:PAD + (b + 1) * 512]
                        do(PO.tensor_tensor(o, o, sg[k % 2], ALU.mult))
                        PO.memset(st[:, 62:63], 0.0).then_inc(s_sg_free, 1)
                        PO.memset(st[:, 61:62], 0.0).then_inc(s_v_ready, 1)

            def out_slot(key):
                n = BON[key]
                if n >= 2:
                    pool.wait_ge([s_bo_out0, s_bo_out1][n % 2], 16 * (n // 2))
                return bo[:, n % 2, :]

            def glu(h):
                for b in range(2):
                    for q in range(CT):
                        pool.wait_ge(s_mm_free, MMN["glu", h, b, q] + 1)
                        k = SGN["glu", h, b, q]
                        o = out_slot(("glu", h, b, q))
                        do(PO.tensor_tensor(o, gT[:, q, b * 512:(b + 1) * 512], sg[k % 2], ALU.mult))
                        PO.memset(st[:, 62:63], 0.0).then_inc(s_sg_free, 1)
                        PO.memset(st[:, 61:62], 0.0).then_inc(s_bo_full, 1)

            def norm(h):
                def finish(i):
                    k = SGN["ln", h, i]
                    pool.wait_ge(s_ly_full, h * TPH + i + 1)
                    o = out_slot(("ln", h, i))
                    do(PO.tensor_tensor(o, ly[:, :], sg[k % 2], ALU.mult))
                    PO.memset(st[:, 62:63], 0.0).then_inc(s_sg_free, 1)
                    PO.memset(st[:, 61:62], 0.0).then_inc(s_bo_full, 1)

                for i in range(TPH):
                    k = h * TPH + i
                    pool.wait_ge(s_bn_ready, k + 1)
                    do(PO.tensor_scalar(st[:, 48:49], bn[:, 7:8], EPS, None, ALU.add))
                    do(PO.tensor_tensor(st[:, 49:50], st[:, 48:49], mhalf[:, :], ALU.pow))
                    if k:
                        pool.wait_ge(s_tp_full, (TPN["LB", h, i - 1] if i else TPN["LB", 0, TPH - 1]) + 1)
                    PO.tensor_scalar(yn, ytok[:, :], bn[:, 6:7], st[:, 49:50], ALU.subtract, ALU.mult).then_inc(s_yn_ready, 1)
                    if i:
                        finish(i - 1)
                finish(TPH - 1)

            for h in range(NH):
                to_h(h)
                if h == 1:
                    norm(0)
                gate(h)
                glu(h)
            do(PO.memset(xb[:, 2, :], 0.0))
            PO.memset(st[:, 61:62], 0.0).then_inc(s_zero_ok, 1)
            norm(1)
            pool.wait_ge(s_small_in, 16 * NSMALL)
            pool.wait_ge(s_wout_in, 16 * KD)
            for k in range(KD):
                PO.tensor_scalar(wout[:, k, :], wout[:, k, :], gout[:, k:k + 1], None, ALU.mult).then_inc(s_wout_ready, 1)

            pool.wait_ge(s_row_ready, 1)
            for i in range(NT):
                c0 = 16 * (i % 2)
                pool.wait_ge(s_ssn_ready, i + 1)
                for f in range(2):
                    m = PO.tensor_tensor(st[:, c0 + 2 + f:c0 + 3 + f], st[:, c0 + f:c0 + f + 1], mhalf[:, :], ALU.pow)
                    if f == 0:
                        do(m)
                    else:
                        m.then_inc(s_rr_ready, 1)
                pool.wait_ge(s_so_ready, i + 1)
                rsqrt(st[:, c0 + 6:c0 + 7], st[:, c0 + 5:c0 + 6], st[:, c0 + 4:c0 + 5], D, s_ro_ready)
                pool.wait_ge(s_t_ready, i + 1)
                pool.wait_ge([s_xs_in0, s_xs_in1][i % 2], 16 * (i // 2 + 1))
                x = xb[:, i % 2, :]
                PO.tensor_tensor(x, x, ob, ALU.add).then_inc(s_x1_ready, 1)
                pool.wait_ge(s_s1_ready, i + 1)
                rsqrt(st[:, c0 + 9:c0 + 10], st[:, c0 + 8:c0 + 9], st[:, c0 + 7:c0 + 8], D, s_r1_ready)
                pool.wait_ge(s_ha_ready, i + 1)
                h2 = h2b[:, i % 2, :]
                PO.tensor_tensor(h2, h2, rows[:, 2], ALU.add).then_inc(s_h2_ready, 1)

            pool.wait_ge(s_h2_ready, NT)
            do(PO.iota(rinit[:, :, 0].bitcast(I32), pattern=[[0, NB + 2]], base=T, channel_multiplier=1),
               PO.memset(rinit[:, :, 1], 0.0),
               PO.iota(bidx.bitcast(I32), pattern=[[P, 2]], base=0, channel_multiplier=1))
            do(PO.tensor_copy(bidx, bidx.bitcast(I32)))
            PO.memset(st[:, 61:62], 0.0).then_inc(s_rinit_ready, 1)
            PO.dma_start(rows_d.rearrange("(p b) w -> p b w", p=P), rinit).then_inc(s_rinit_out, 16)
            pool.wait_ge(s_cnt_ready, 1)
            PO.dma_start(be_d.rearrange("(t p) -> p t", p=P), bei, allow_slow_non_contiguous=True).then_inc(s_be_out, 16)
            pool.wait_ge(s_be_out, 16)
            PO.dma_start(berow, be_d.unsqueeze(0)).then_inc(s_be_back, 16)
            pool.wait_ge(s_pay_ready, 1)
            do(PO.iota(pay[:, :, 0].bitcast(I32).rearrange("p (i k) -> p i k", i=NT), pattern=[[P, NT], [0, TOPK]], base=0, channel_multiplier=1))
            pool.wait_ge(s_rinit_out, 16)
            for n in range(NT * TOPK):
                PO.indirect_dma_start(rows_d, bass.IndirectOffsetOnAxis(di[:, n:n + 1], 0), pay[:, n, :], None).then_inc(s_disp_out, 16)
            pool.wait_ge(s_disp_out, 16 * NT * TOPK)
            PO.dma_start(tabl, rows_d.rearrange("(p b) w -> p b w", p=P)).then_inc(s_rows_back, 16)
            pool.wait_ge(s_rows_back, 16)

            def hold():
                PO.tensor_tensor(st[:, 60:61], mhalf[:, :], mhalf[:, :], ALU.add)
                pool.drain()

            def gather(b, n):
                pool.wait_ge(s_xt_full, b)
                PO.tensor_copy(idxg, tabl[:, bass.ds(b - NT, 1), 0].bitcast(U32)).then_inc(s_idx_ready, 1)
                pool.wait_ge(s_idx_ready, n)
                hold()
                PO.indirect_dma_start(xg, None, h2_d, bass.IndirectOffsetOnAxis(idxg, 0)).then_inc(s_xr_in, 16)

            gather(NT, 1)
            pool.wait_ge(s_y_out, 16 * NT)
            PO.tensor_tensor(st[:, 59:60], mhalf[:, :], mhalf[:, :], ALU.add).then_inc(s_y_free, 1)
            gather(NT + 1, 2)
            nb = pool.value_load(pint[0:1, E - 1:E], min_val=1, max_val=NB)
            with pool.Fori(NT, nb + NT) as b:
                PO.tensor_copy(idxs, tabl[:, bass.ds(b - NT, 1), 0].bitcast(U32)).then_inc(s_idy_ready, 1)
                gather(b + 2, b - (NT - 3))
                pool.wait_ge(s_idy_ready, b - (NT - 1))
                pool.wait_ge(s_y_act, b + 1)
                pool.wait_ge(s_y_dve, b + 1)
                hold()
                PO.indirect_dma_start(acc_d, bass.IndirectOffsetOnAxis(idxs, 0), yb, None, compute_op=ALU.add).then_inc(s_ya_out, 16)
                pool.wait_ge(s_ya_out, (b - (NT - 1)) * 16)
                PO.tensor_tensor(st[:, 59:60], mhalf[:, :], mhalf[:, :], ALU.add).then_inc(s_y_free, 1)
            for i in range(NT):
                pool.wait_ge(s_fs_ready, i + 1)
                rsqrt(st[:, 32 + i:33 + i], st[:, 16 + i:17 + i], st[:, i:i + 1], D, s_fr_ready)


_INS = ["x", "c", "w_ada", "b_ada", "g_pre_mix", "g_post_mix", "w_in", "conv_w", "conv_b", "conv_ln_g", "conv_ln_b",
        "ssm_a_re", "ssm_a_im", "ssm_log_dt", "ssm_b_re", "ssm_b_im", "ssm_c_re", "ssm_c_im", "ssm_d", "ssm_w_glu",
        "ssm_b_glu", "g_out_conv", "g_out_ssm", "w_out", "g_pre_ffn", "g_post_ffn", "w_router", "b_router", "we_gate",
        "we_up", "we_down", "ws_gate", "ws_up", "ws_down"]


def kernel(**inputs):
    import numpy as _np
    import concourse.bacc as _bacc
    from concourse import mybir as _mybir
    from concourse.bass_utils import run_bass_kernel_spmd as _run

    nc = _bacc.Bacc("TRN2", target_bir_lowering=False, num_devices=1)
    arrays, args = {}, {}
    for name in _INS:
        a = _np.ascontiguousarray(inputs[name])
        arrays[f"in_{name}_dram"] = a
        args[name] = nc.dram_tensor(f"in_{name}_dram", a.shape, _mybir.dt.from_np(a.dtype), kind="ExternalInput").ap()
    out = nc.dram_tensor("out_0_dram", (1, T, D), _mybir.dt.float32, kind="ExternalOutput").ap()
    build(nc, args, out)
    r = _run(nc, [arrays], core_ids=[0])
    return r.results[0]["out_0_dram"]
```

```python
from contextlib import ExitStack

import numpy as np
import concourse.bass as bass
from concourse import mybir

ALU = mybir.AluOpType
ACT = mybir.ActivationFunctionType
AX = mybir.AxisListType
F32 = mybir.dt.float32
F32R = mybir.dt.float32r
BF16 = mybir.dt.bfloat16
I32 = mybir.dt.int32
U32 = mybir.dt.uint32

P = 128
T, D = 2048, 1024
KD = D // P
NH = 2
HT = T // NH
TPH = HT // P
NT = T // P
CC = 512
CT = CC // P
TAPS = 31
PAD = TAPS - 1
CH = TPH
NC = HT // CH
G, HG, S = 32, 16, 64
NPR = G // 2
E, TOPK, NG, TOPG = 64, 8, 8, 4
DE = 256
FE = DE // P
BLK = 128
NB = (T * TOPK + E * (BLK - 1)) // BLK + 1
NB += NB % 2
NROW = NB + 2
NCOL = NB + 4
XPOOL = (TPH, TPH + 1, TPH + 2)
XDVE = tuple(n for n in range(NT) if n not in XPOOL)
EPS = 1e-6
AREA = 50104
BIG = 1e30
WG = 2 * KD * DE
WSLOT = WG + FE * D
NGC = 4
GC = WG // NGC
WC = WSLOT // 3



class Chain:

    def __init__(self, eng, sem):
        self.eng, self.sem, self.n = eng, sem, 0

    def add(self, ins):
        ins.then_inc(self.sem, 1)
        self.n += 1
        return self.n

    def sync(self):
        self.eng.wait_ge(self.sem, self.n)

    def do(self, *instructions):
        for ins in instructions:
            self.add(ins)
        self.sync()


def numbered(keys):
    return {k: n for n, k in enumerate(keys)}


def build(nc, A, out):
    ctx = ExitStack()
    with ctx:
        def sb(name, shape, dt=F32):
            return ctx.enter_context(nc.sbuf_tensor(name, shape, dt))

        def sem(name):
            return ctx.enter_context(nc.semaphore(name))

        def dram(name, shape, dt=F32):
            return nc.dram_tensor(name, shape, dt).ap()

        mod_d = dram("mod_d", [6, D])
        tab_d = dram("tab_d", [P, 12288])
        et_d = dram("et_d", [P, 4096])
        mix_d = dram("mix_d", [NT, P, KD, P])
        x1_d = dram("x1_d", [T, D])
        h2_d = dram("h2_d", [T + BLK, D])
        acc_d = dram("acc_d", [T + BLK, D])
        rows_d = dram("rows_d", [P * NCOL, 2])
        be_d = dram("be_d", [3 * P], I32)

        with nc.sbuf_tensor("arena", [P, AREA], F32) as arena:
            pass
        with ExitStack() as low:
            raw = low.enter_context(nc.sbuf_tensor("raw", [P, 2 * WSLOT], F32))
            whi = low.enter_context(nc.sbuf_tensor("whi", [P, 2 * WSLOT], F32R))
            wlo = low.enter_context(nc.sbuf_tensor("wlo", [P, 2 * WSLOT], F32R))
            with nc.sbuf_tensor("ws_raw", [P, WC], F32) as ws_raw:
                pass
            xhi, xlo = (low.enter_context(nc.sbuf_tensor(n, [P, D], F32R)) for n in ("xhi", "xlo"))
            hhi, hlo = (low.enter_context(nc.sbuf_tensor(n, [P, DE], F32R)) for n in ("hhi", "hlo"))
        sb("held", [P, AREA])
        pos = [0]

        def cut(n):
            a = pos[0]
            pos[0] += n
            assert pos[0] <= AREA, pos[0]
            return arena[:, a:a + n]

        big0 = cut(8192)
        us = cut(4096)
        ut = cut(4096)
        eg = cut(6144)
        tabs = cut(8192)
        vacc = cut(4216 + 4096)
        wio = cut(4096)
        xbr = cut(3072)
        work = cut(3904)
        hT = big0.rearrange("p (k t) -> p k t", k=KD)
        U = us.rearrange("p (g j h) -> p g j h", g=G, j=CH)
        SR = us[:, 0:2048].rearrange("p (r c) -> p r c", r=NPR)
        SI = us[:, 2048:4096].rearrange("p (r c) -> p r c", r=NPR)
        UT = ut.rearrange("p (g c) -> p g c", g=G)
        GA = ut.rearrange("p (q i c) -> p q i c", q=CT, i=CH)
        EC = eg[:, 0:2048].rearrange("p (r c) -> p r c", r=NPR)
        ES = eg[:, 2048:4096].rearrange("p (r c) -> p r c", r=NPR)
        gT = eg[:, 0:4096].rearrange("p (q t) -> p q t", q=CT)
        arow, brow = eg[:, 4096:5120], eg[:, 5120:6144]
        RT = tabs[:, 0:4096].rearrange("p (g m) -> p g m", g=G)
        TOE = tabs[:, 0:4096].rearrange("p (g m) -> p g m", g=G)
        COR = tabs[:, 4096:6144].rearrange("p (r m) -> p r m", r=NPR)
        COI = tabs[:, 6144:8192].rearrange("p (r m) -> p r m", r=NPR)
        v = vacc[:, 0:4216].rearrange("p (q t) -> p q t", q=CT)
        cacc = vacc[:, 4216:8312].rearrange("p (q t) -> p q t", q=CT)
        wz = wio.rearrange("p (s n) -> p s n", s=2)
        xb = xbr.rearrange("p (s n) -> p s n", s=3)
        rot = work[:, 0:2048].rearrange("p (s n) -> p s n", s=4)
        sg = [work[:, 2048:2560], work[:, 2560:3072]]
        ytok = sb("ytok", [P, 512])
        yn = work[:, 3072:3584]
        bo = sb("bo", [P, 2, 512])
        ly = sb("ly", [P, 512])

        ident = sb("ident", [P, P])
        tri = sb("tri", [P, P], BF16)
        oneb = sb("oneb", [P, P], BF16)
        one = sb("one", [P, 1])
        mhalf = sb("mhalf", [P, 1])
        sel8 = sb("sel8", [P, NG, NG])
        cw = sb("cw", [P, CT, TAPS])
        col = sb("col", [P, 4, CT])
        gout = sb("gout", [P, KD])
        ccol = sb("ccol", [P, KD])
        csig = sb("csig", [P, KD])
        st = sb("st", [P, 64])
        bn = sb("bn", [P, 8])
        lam8 = sb("lam8", [P, 6, NPR])
        last = sb("last", [P, 4, NPR])
        seg = bo
        segb = [ytok, ly]

        psm = ctx.enter_context(nc.psum_tensor("psm", [P, 8, 512], F32))
        mm = [psm[:, b, :] for b in (0, 1)]
        tp = [psm[:, b, :] for b in (2, 3)]
        dv = [psm[:, b, :] for b in (4, 5, 6, 7)]

        s_fin_in0 = sem("fin_in0")
        s_fin_in1 = sem("fin_in1")
        s_fin_in2 = sem("fin_in2")
        s_fin_in3 = sem("fin_in3")
        s_fin_in4 = sem("fin_in4")
        s_fin_in5 = sem("fin_in5")
        s_fin_in6 = sem("fin_in6")
        s_fin_in7 = sem("fin_in7")
        s_par_in = sem("par_in")
        s_dv_full = sem("dv_full")
        s_seg_ok = sem("seg_ok")
        s_ada_in0 = sem("ada_in0")
        s_ada_in1 = sem("ada_in1")
        s_small_in = sem("small_in")
        s_mod_out0 = sem("mod_out0")
        s_mod_out1 = sem("mod_out1")
        s_rt_ready = sem("rt_ready")
        s_tab_out = sem("tab_out")
        s_phasor_ready = sem("phasor_ready")
        s_et_out = sem("et_out")
        s_toe_ready = sem("toe_ready")
        s_rows_in = sem("rows_in")
        s_x_in0 = sem("x_in0")
        s_x_in1 = sem("x_in1")
        s_x_in2 = sem("x_in2")
        s_arow_ready = sem("arow_ready")
        s_tp_full = sem("tp_full")
        s_mm_full = sem("mm_full")
        s_wz_in0 = sem("wz_in0")
        s_wz_in1 = sem("wz_in1")
        s_tab_in = sem("tab_in")
        s_bo_full = sem("bo_full")
        s_bo_out0 = sem("bo_out0")
        s_bo_out1 = sem("bo_out1")
        s_et_in = sem("et_in")
        s_wout_in = sem("wout_in")
        s_row_in = sem("row_in")
        s_wr_in = sem("wr_in")
        s_wlo_ready = sem("wlo_ready")
        s_wgate_in = sem("wgate_in")
        s_wup_in = sem("wup_in")
        s_wlow_ready = sem("wlow_ready")
        s_wdown_in = sem("wdown_in")
        s_ob_full = sem("ob_full")
        s_sqm_ready = sem("sqm_ready")
        s_x1_out0 = sem("x1_out0")
        s_x1_out1 = sem("x1_out1")
        s_s1_ready = sem("s1_ready")
        s_ha_ready = sem("ha_ready")
        s_mix_in0 = sem("mix_in0")
        s_mix_in1 = sem("mix_in1")
        s_xs_in0 = sem("xs_in0")
        s_xs_in1 = sem("xs_in1")
        s_ws_in = sem("ws_in")
        s_zero_ok = sem("zero_ok")
        s_h2z_out = sem("h2z_out")
        s_x1_ready = sem("x1_ready")
        s_h2_ready = sem("h2_ready")
        s_h2_out0 = sem("h2_out0")
        s_h2_out1 = sem("h2_out1")
        s_ws_lo = sem("ws_lo")
        s_xg_in0 = sem("xg_in0")
        s_xg_in1 = sem("xg_in1")
        s_y_act = sem("y_act")
        s_y_out0 = sem("y_out0")
        s_y_out1 = sem("y_out1")
        s_xt_full = sem("xt_full")
        s_cnt_ready = sem("cnt_ready")
        s_be_out = sem("be_out")
        s_be_back = sem("be_back")
        s_xp_in = sem("xp_in")
        s_y_free = sem("y_free")
        s_fo_ready = sem("fo_ready")
        s_fin_out = sem("fin_out")
        s_tp_free = sem("tp_free")
        s_mm_free = sem("mm_free")
        s_dv_free = sem("dv_free")
        s_const_ok = sem("const_ok")
        s_nat_ready = sem("nat_ready")
        s_csig_ok = sem("csig_ok")
        s_c_ready = sem("c_ready")
        s_r_ready = sem("r_ready")
        s_xnp_ready = sem("xnp_ready")
        s_xn_ready = sem("xn_ready")
        s_states_ready = sem("states_ready")
        s_conv_ready = sem("conv_ready")
        s_yn_ready = sem("yn_ready")
        s_wout_ready = sem("wout_ready")
        s_h2t_free = sem("h2t_free")
        s_h2t_full = sem("h2t_full")
        s_sc_ready = sem("sc_ready")
        s_lg_full = sem("lg_full")
        s_ssn_ready = sem("ssn_ready")
        s_ss_full = sem("ss_full")
        s_oa_ready = sem("oa_ready")
        s_oa_full = sem("oa_full")
        s_o_ready = sem("o_ready")
        s_sel_ready = sem("sel_ready")
        s_pos_full = sem("pos_full")
        s_xr_in0 = sem("xr_in0")
        s_xr_in1 = sem("xr_in1")
        s_xt_ready = sem("xt_ready")
        s_gu_full = sem("gu_full")
        s_ht_ready = sem("ht_ready")
        s_y_full = sem("y_full")
        s_h_full = sem("h_full")
        s_ht_full = sem("ht_full")
        s_br_ready = sem("br_ready")
        s_act_step = sem("act_step")
        s_dt_ready = sem("dt_ready")
        s_nat_angle = sem("nat_angle")
        s_nat_trig = sem("nat_trig")
        s_sq_ready = sem("sq_ready")
        s_sg_free = sem("sg_free")
        s_stat_ready = sem("stat_ready")
        s_xr_ready = sem("xr_ready")
        s_v_tail = sem("v_tail")
        s_ly_full = sem("ly_full")
        s_rr_ready = sem("rr_ready")
        s_so_ready = sem("so_ready")
        s_ws_hi = sem("ws_hi")
        s_xt_high = sem("xt_high")
        s_sig_ready = sem("sig_ready")
        s_ht_high = sem("ht_high")
        s_whi_ready = sem("whi_ready")
        s_whid_ready = sem("whid_ready")
        s_rows_back = sem("rows_back")
        s_fs_ready = sem("fs_ready")
        s_dve_step = sem("dve_step")
        s_v_ready = sem("v_ready")
        s_bn_ready = sem("bn_ready")
        s_row_ready = sem("row_ready")
        s_ro_ready = sem("ro_ready")
        s_t_ready = sem("t_ready")
        s_r1_ready = sem("r1_ready")
        s_rinit_ready = sem("rinit_ready")
        s_pay_ready = sem("pay_ready")
        s_hm_ready = sem("hm_ready")
        s_fr_ready = sem("fr_ready")
        s_ft_ready = sem("ft_ready")
        s_pool_step = sem("pool_step")
        s_rinit_out = sem("rinit_out")
        s_disp_out = sem("disp_out")
        s_idx_ready = sem("idx_ready")
        s_idy_ready = sem("idy_ready")
        s_ya_out = sem("ya_out")

        tpk = []
        mmk = []
        for h in range(NH):
            tpk += [("hT", h, i, b) for i in range(TPH) for b in range(2)]
            if h == 1:
                for i in range(TPH + 1):
                    tpk += [("LF", 0, i)] if i < TPH else []
                    tpk += [("LB", 0, i - 1)] if i >= 1 else []
            tpk += [("UT", h, n) for n in range(8)]
            tpk += [("GT", h, q, b) for q in range(CT) for b in range(2)]
            mmk += [("zs", h, j) for j in range(CH)]
            mmk += [("zc", h, q, b, w) for q in range(CT) for b in range(2) for w in range(2)]
            mmk += [("Y", h, n) for n in range(8)]
            mmk += [("glu", h, b, q) for b in range(2) for q in range(CT)]
        for i in range(TPH + 1):
            tpk += [("LF", 1, i)] if i < TPH else []
            tpk += [("LB", 1, i - 1)] if i >= 1 else []
        dvk = [("nat", 0)] + [("ada", n) for n in range(12)] + [("C", n) for n in range(3)]
        dvk += [("RT", n) for n in range(8)] + [("TOE", n) for n in range(8)]
        for h in range(NH):
            dvk += [("V", h, n, w) for n in range(4) for w in range(2)]
        TPN, MMN, DVN = numbered(tpk), numbered(mmk), numbered(dvk)

        C1, C2 = 6.28125, float(np.float32(2 * np.pi - 6.28125))
        C3 = float(2 * np.pi - 6.28125 - np.float64(np.float32(2 * np.pi - 6.28125)))
        MAGIC = 1.5 * 2.0 ** 23

        nat = [xbr[0:G, n * P:(n + 1) * P] for n in range(20)]
        (nar, nai, nth, nn, nr_, nmag, nsin, ncos, nlr, nli, nden, nkr, nki, nm8, nc8, ns8, nd, nt1,
         nt2, nt3) = nat
        cwn = xbr[0:TAPS, 20 * P:24 * P]
        ndt = sb("ndt", [G, 4])
        L = work[:, 0:9 * G * 2].rearrange("p (w k g) -> p w k g", w=2, k=9)
        LP = work[:, 576:576 + 9 * NPR * 2].rearrange("p (w k r) -> p w k r", w=2, k=9)
        dup = work[:, 864:864 + 256].rearrange("p (n g) -> p n g", n=8)
        Y1 = work[:, 1120:1632].rearrange("p (g h) -> p g h", g=G)
        CRP = work[:, 1632:1888].rearrange("p (r h) -> p r h", r=NPR)
        CIP = work[:, 1888:2144].rearrange("p (r h) -> p r h", r=NPR)
        CN = work[:, 2144:3680].rearrange("p (w q m) -> p w q m", w=3, q=4)
        X1 = wio[:, 0:512].rearrange("p (g h) -> p g h", g=G)
        X2 = wio[:, 512:1024].rearrange("p (g h) -> p g h", g=G)
        BB1 = wio[:, 1024:1536].rearrange("p (g h) -> p g h", g=G)
        BB2 = wio[:, 1536:2048].rearrange("p (g h) -> p g h", g=G)
        PT = [wio[:, 2048 + n * 1024:3072 + n * 1024] for n in range(2)] + [eg[:, 4096:5120], eg[:, 5120:6144]]
        R = big0[:, 0:G * 15 * HG].rearrange("p (g s h) -> p g s h", g=G, s=15)
        ctoe = cacc.rearrange("p q t -> p (q t)").rearrange("p (g m) -> p g m", g=G)
        vflat = vacc[:, 0:4096]
        ccor = vflat[:, 0:2048].rearrange("p (r i h) -> p r i h", r=NPR, i=CH)
        ccoi = vflat[:, 2048:4096].rearrange("p (r i h) -> p r i h", r=NPR, i=CH)
        wada = [us.rearrange("p (k n) -> p k n", k=KD), ut.rearrange("p (k n) -> p k n", k=KD)]

        x_t = A["x"][0].rearrange("(i p) d -> i p d", p=P)
        wada_d = A["w_ada"][0].rearrange("(k p) n -> p k n", p=P)
        bada_d = A["b_ada"]
        win_d = A["w_in"][0].rearrange("(k p) n -> p k n", p=P)
        modf = mod_d.rearrange("a n -> (a n)")

        first = [(nar[:, 0:S], A["ssm_a_re"][0]), (nar[:, S:P], A["ssm_a_re"][0]),
                 (nai[:, 0:S], A["ssm_a_im"][0]), (nai[:, S:P], A["ssm_a_im"][0]),
                 (ndt[:, 0:1], A["ssm_log_dt"][0].unsqueeze(1)),
                 (nd[:, 0:HG], A["ssm_d"][0].rearrange("(g h) -> g h", g=G)), (cwn, A["conv_w"][0, :, 0, :]),
                 (ccol[:, :], A["c"][0].rearrange("(k p) -> p k", p=P))]
        b_re = A["ssm_b_re"][0].rearrange("g p h -> p g h")
        b_im = A["ssm_b_im"][0].rearrange("g p h -> p g h")
        small = [(X1[0:S], b_re), (X1[S:P], b_im), (X2[0:S], b_im), (X2[S:P], b_re)]
        c_re = A["ssm_c_re"][0].rearrange("(q a) h p -> (a h) q p", a=8)
        c_im = A["ssm_c_im"][0].rearrange("(q a) h p -> (a h) q p", a=8)
        for w, (lo, hi) in enumerate(((c_re, c_im), (c_re, c_re), (c_im, c_im))):
            small += [(CN[:, w, :, 0:S], lo), (CN[:, w, :, S:P], hi)]
        for n, a in enumerate(("conv_b", "conv_ln_g", "conv_ln_b", "ssm_b_glu")):
            small += [(col[:, n, :], A[a][0].rearrange("(q p) -> p q", p=P))]
        small += [(gout[:, 0:CT], A["g_out_conv"][0].rearrange("(q p) -> p q", p=P)),
                  (gout[:, CT:KD], A["g_out_ssm"][0].rearrange("(q p) -> p q", p=P))]
        NSMALL, NFIRST = len(small), len(first)

        def wz_conv(q):
            return wz[:, q % 2, :].rearrange("p (w k n) -> p w k n", w=2, k=KD)


        blk = ctx.enter_context(nc.Block())
        V, SC, TE, PO, SY = nc.vector, nc.scalar, nc.tensor, nc.gpsimd, nc.sync

        wout = big0.rearrange("p (k n) -> p k n", k=KD)
        mixb = us[:, 0:2048].rearrange("p (s k t) -> p s k t", s=2, k=KD)
        sqb = us[:, 2048:3072].rearrange("p (k t) -> p k t", k=KD)
        h2T = us[:, 3072:4096].rearrange("p (k t) -> p k t", k=KD)
        ob = ut[:, 0:1024]
        h2b = ut[:, 1024:3072].rearrange("p (s n) -> p s n", s=2)
        junk = ut[:, 3072:4096]
        rows = wio.rearrange("p (n d) -> p n d", n=4)
        rtmp = tabs[:, 4096:7168].rearrange("p (n d) -> p n d", n=3)
        cur = [2048]

        def cut2(size, shape=None, dt=F32, base=tabs, **kw):
            a = cur[0]
            cur[0] += size
            r = base[:, a:a + size]
            if dt is not F32:
                r = r.bitcast(dt)
            return r.rearrange(shape, **kw) if shape else r

        wr = cut2(512, "p (k e) -> p k e", k=KD)
        scores, biased, bm, rep, pen, rbias = (cut2(64) for _ in range(6))
        v8 = cut2(64, "p (g m) -> p g m", g=NG)
        cmpa, cmpb = (cut2(64, "p (g m) -> p g m", g=NG) for _ in range(2))
        gs, rank, gm, gp, t8 = (cut2(8) for _ in range(5))
        gsum = cut2(8)
        selbf = cut2(512, "p (i e) -> p i e", dt=BF16, i=NT)
        selcum = cut2(544, "p (i e) -> p i e", dt=BF16, i=NT + 1)
        selall = cut2(1024, "p (i e) -> p i e", i=NT)
        gwall = cut2(1024, "p (i e) -> p i e", i=NT)
        DD = ut[:, 0:1024].rearrange("p (i e) -> p i e", i=NT)
        eqb = ut[:, 3072:4096].rearrange("p (i e) -> p i e", i=NT)
        d8 = cut2(128, "p (i k) -> p i k", i=NT)
        qi = cut2(128, dt=I32)
        bi = cut2(128, dt=I32)
        bf_ = cut2(128)
        qf = cut2(128)
        di = cut2(128, dt=U32)
        pay = cut2(256, "p (n w) -> p n w", n=P)
        pay4 = pay.rearrange("p (i k) w -> p i k w", i=NT)
        cntf, nbf, pend, basef, ones64 = (cut2(64) for _ in range(5))
        cnti = cut2(64, dt=I32)
        assert cur[0] <= 8192, cur[0]
        cur[0] = 2816
        W = work
        rinit = cut2(2 * NCOL, "p (b w) -> p b w", base=W, w=2)
        tabl = cut2(2 * NCOL, "p (b w) -> p b w", base=W, w=2)
        pint = cut2(64, dt=I32, base=W)
        bep = cut2(3, base=W)
        bei = cut2(3, dt=I32, base=W)
        bidx = cut2(2, base=W)
        mint = cut2(1, dt=I32, base=W)
        idxg = [cut2(1, dt=U32, base=W) for _ in range(2)]
        nbi = cut2(1, dt=I32, base=W)
        nbm = cut2(1, dt=I32, base=W)
        idxs = cut2(1, dt=U32, base=W)
        assert cur[0] <= 3904, cur[0]
        bof = bo.rearrange("p a n -> p (a n)")
        berow = bof[0:1, 0:3 * P].bitcast(I32)
        bef, news, rone = (bof[0:1, 3 * P + n * NROW:3 * P + (n + 1) * NROW] for n in range(3))
        mf = bof[0:1, 3 * P + 3 * NROW:3 * P + 3 * NROW + 1]
        ordf = ly[0:1, 0:NROW]
        n_split, n_come, n_base = (ly[0:1, NROW + n * E:NROW + (n + 1) * E].bitcast(I32) for n in range(3))
        ordi, splits = (ytok[0:1, n * NROW:(n + 1) * NROW].bitcast(I32) for n in range(2))
        xg = [xbr[:, 0:1024], xbr[:, 1024:2048]]
        XH, XL = (a[:, :].rearrange("p (k t) -> p k t", k=KD) for a in (xhi, xlo))
        HH, HL = (a[:, :].rearrange("p (f t) -> p f t", f=FE) for a in (hhi, hlo))
        yb = [work[:, 0:1024], xbr[:, 2048:3072]]
        sigb, htmp, hs = (work[:, 1024 + n * DE:1024 + (n + 1) * DE] for n in range(3))
        wsr = ws_raw[:, :]
        fin = [arena[:, 2 * WSLOT + i * D:2 * WSLOT + (i + 1) * D] for i in range(NT)]
        fin_in = [s_fin_in0, s_fin_in1, s_fin_in2, s_fin_in3, s_fin_in4, s_fin_in5, s_fin_in6, s_fin_in7]
        xps = [arena[:, i * D:(i + 1) * D] for i in range(12)] + [rows[:, 1], rows[:, 2], work[:, 1792:2816], arena[:, 0:D]]

        sgk, bok = [], []
        for h in range(NH):
            if h == 1:
                sgk += [("ln", 0, i) for i in range(TPH)]
            sgk += [("zc", h, q, b) for q in range(CT) for b in range(2)]
            sgk += [("glu", h, b, q) for b in range(2) for q in range(CT)]
        sgk += [("ln", 1, i) for i in range(TPH)]
        bok = [k for k in sgk if k[0] != "zc"]
        SGN, BON = numbered(sgk), numbered(bok)

        @blk.sync
        def _(sp):
            for dst, src in first:
                SY.dma_start(dst, src, allow_slow_non_contiguous=True).then_inc(s_par_in, 16)
            for n in range(12):
                if n >= 2:
                    sp.wait_ge(s_dv_full, DVN["ada", n - 2] + 1)
                    sp.wait_ge(s_seg_ok, n - 1)
                SY.dma_start(wada[n % 2], wada_d[:, :, n * 512:(n + 1) * 512]).then_inc([s_ada_in0, s_ada_in1][n % 2], 16)
                SY.dma_start(segb[n % 2][0:1, :], bada_d[:, n * 512:(n + 1) * 512]).then_inc([s_ada_in0, s_ada_in1][n % 2], 16)
                if n == 1:
                    for dst, src in small:
                        SY.dma_start(dst, src, allow_slow_non_contiguous=True).then_inc(s_small_in, 16)
                if n >= 1:
                    sp.wait_ge(s_seg_ok, n)
                    SY.dma_start(modf[(n - 1) * 512:n * 512].unsqueeze(0), seg[0:1, (n - 1) % 2, :]).then_inc([s_mod_out0, s_mod_out1][(n - 1) % 2], 16)
            sp.wait_ge(s_seg_ok, 12)
            SY.dma_start(modf[11 * 512:12 * 512].unsqueeze(0), seg[0:1, 1, :]).then_inc(s_mod_out1, 16)
            sp.wait_ge(s_rt_ready, 8)
            SY.dma_start(tab_d[:, 0:4096], tabs[:, 0:4096]).then_inc(s_tab_out, 16)
            sp.wait_ge(s_phasor_ready, 1)
            SY.dma_start(et_d, eg[:, 0:4096]).then_inc(s_et_out, 16)
            sp.wait_ge(s_mod_out0, 6 * 16)
            sp.wait_ge(s_mod_out1, 6 * 16)
            sp.wait_ge(s_toe_ready, 1)
            SY.dma_start(brow, mod_d[0].partition_broadcast(P)).then_inc(s_rows_in, 16)
            SY.dma_start(arow, mod_d[1].partition_broadcast(P)).then_inc(s_rows_in, 16)
            SY.dma_start(xb[:, 2, :], A["g_pre_mix"][0].partition_broadcast(P)).then_inc(s_rows_in, 16)
            xin = [s_x_in0, s_x_in1, s_x_in2]

            def load_x(n):
                if n == 2:
                    sp.wait_ge(s_arow_ready, 1)
                if n >= 3:
                    h, i = divmod(n - 3, TPH)
                    sp.wait_ge(s_tp_full, TPN["hT", h, i, 1] + 1)
                SY.dma_start(xb[:, n % 3, :], x_t[n]).then_inc(xin[n % 3], 16)

            def load_wz_ssm(h):
                if h:
                    sp.wait_ge(s_mm_full, MMN["glu", 0, 1, 3] + 1)
                for w in range(2):
                    SY.dma_start(wz[:, w, :].rearrange("p (k n) -> p k n", k=4),
                                 win_d[:, 4 * w:4 * w + 4, 2 * CC:3 * CC]).then_inc([s_wz_in0, s_wz_in1][w], 16)

            def load_wz_conv(h, q):
                sp.wait_ge(s_mm_full, (MMN["zs", h, 7] if q < 2 else MMN["zc", h, q - 2, 1, 1]) + 1)
                for w in range(2):
                    SY.dma_start(wz_conv(q)[:, w], win_d[:, :, w * CC + q * P:w * CC + (q + 1) * P])\
                      .then_inc([s_wz_in0, s_wz_in1][q % 2], 16)

            def load_wglu(h):
                sp.wait_ge(s_mm_full, MMN["zc", h, 2, 1, 1] + 1)
                SY.dma_start(wz[:, 0, :].rearrange("p (q n) -> p q n", q=CT),
                             A["ssm_w_glu"][0].rearrange("(q p) n -> p q n", p=P)).then_inc(s_wz_in0, 16)

            def load_toe(h):
                sp.wait_ge(s_dv_full, DVN["V", h, 3, 1] + 1)
                if h == 0:
                    sp.wait_ge(s_tab_out, 48)
                SY.dma_start(tabs, tab_d[:, 4096:12288]).then_inc(s_tab_in, 16)

            def store_bo(key):
                n = BON[key]
                sp.wait_ge(s_bo_full, n + 1)
                o = [s_bo_out0, s_bo_out1][n % 2]
                src = bo[:, n % 2, :].rearrange("p (a t) -> p a t", a=4)
                if key[0] == "ln":
                    SY.dma_start(mix_d[key[1] * TPH + key[2], :, 0:CT, :], src).then_inc(o, 16)
                else:
                    _, h, b, q = key
                    i0 = h * TPH + 4 * b
                    SY.dma_start(mix_d[i0:i0 + 4, :, CT + q, :].rearrange("i p t -> p i t"), src).then_inc(o, 16)

            sp.wait_ge(s_toe_ready, 1)
            load_x(0)
            load_x(1)
            load_wz_ssm(0)
            for n in range(2, TPH + 3):
                load_x(n)
                if n == TPH - 1:
                    SY.dma_start(tab_d[:, 4096:8192], vacc[:, 4216:8312]).then_inc(s_tab_out, 16)
                    SY.dma_start(tab_d[:, 8192:12288], vflat).then_inc(s_tab_out, 16)
            load_wz_conv(0, 0)
            load_wz_conv(0, 1)
            load_toe(0)
            load_wz_conv(0, 2)
            load_wz_conv(0, 3)
            load_wglu(0)
            sp.wait_ge(s_mm_full, MMN["Y", 0, 7] + 1)
            SY.dma_start(tabs[:, 0:4096], tab_d[:, 0:4096]).then_inc(s_tab_in, 16)
            for b in range(2):
                for q in range(CT):
                    store_bo(("glu", 0, b, q))
            load_wz_ssm(1)
            SY.dma_start(eg[:, 0:4096], et_d).then_inc(s_et_in, 16)
            for n in range(TPH + 3, NT):
                load_x(n)
            for i in range(TPH):
                store_bo(("ln", 0, i))
            load_wz_conv(1, 0)
            load_wz_conv(1, 1)
            load_toe(1)
            load_wz_conv(1, 2)
            load_wz_conv(1, 3)
            load_wglu(1)
            sp.wait_ge(s_mm_full, MMN["zc", 1, 3, 1, 1] + 1)
            for k in range(KD):
                SY.dma_start(wout[:, k, :], A["w_out"][0, k * P:(k + 1) * P, :]).then_inc(s_wout_in, 16)
            for b in range(2):
                for q in range(CT):
                    store_bo(("glu", 1, b, q))
            for dst, src in ((rows[:, 0], mod_d[2]), (rows[:, 1], mod_d[4]), (rows[:, 2], mod_d[3]), (rows[:, 3], mod_d[5]),
                             (rtmp[:, 0], A["g_post_mix"][0]), (rtmp[:, 1], A["g_pre_ffn"][0]), (rtmp[:, 2], A["g_post_ffn"][0])):
                SY.dma_start(dst, src.partition_broadcast(P)).then_inc(s_row_in, 16)
            SY.dma_start(wr, A["w_router"][0].rearrange("(k p) e -> p k e", p=P)).then_inc(s_wr_in, 16)
            SY.dma_start(rbias, A["b_router"][0].partition_broadcast(P)).then_inc(s_wr_in, 16)

            def load_w(base, gate, up, down, number, split=None):
                gu = raw[:, bass.ds(base, WG)].rearrange("p (k w f) -> p k w f", k=KD, w=2)
                if split is not None:
                    sp.wait_ge(s_wlo_ready, split)
                if number is not None:
                    sp.wait_ge(s_wgate_in, number)
                SY.dma_start(gu[:, :, 0, :], gate.rearrange("(k p) f -> p k f", p=P)).then_inc(s_wgate_in, 16)
                if number is not None:
                    sp.wait_ge(s_wup_in, number)
                SY.dma_start(gu[:, :, 1, :], up.rearrange("(k p) f -> p k f", p=P)).then_inc(s_wup_in, 16)
                if split is not None:
                    sp.wait_ge(s_wlow_ready, split)
                if number is not None:
                    sp.wait_ge(s_wdown_in, number)
                SY.dma_start(raw[:, bass.ds(base + WG, FE * D)].rearrange("p (k f) -> p k f", k=FE),
                             down.rearrange("(k p) f -> p k f", p=P)).then_inc(s_wdown_in, 16)

            def load_expert(n, number):
                e = sp.value_load(berow[0:1, bass.ds(n + 2 * P, 1)], min_val=0, max_val=E - 1)
                base, split = (n & 1) * WSLOT, None
                if not isinstance(n, int):
                    split, number, base = (sp.value_load(a[:, bass.ds(n, 1)], min_val=m, max_val=t)
                                           for a, m, t in ((n_split, 1, E), (n_come, 16, 16 * E), (n_base, 0, WSLOT)))
                load_w(base, A["we_gate"][0, bass.ds(e, 1)].rearrange("a k f -> (a k) f"),
                       A["we_up"][0, bass.ds(e, 1)].rearrange("a k f -> (a k) f"),
                       A["we_down"][0, bass.ds(e, 1)].rearrange("a k f -> (a k) f"), number, split)

            def load_tile(i):
                if i >= 2:
                    sp.wait_ge(s_ob_full, i - 1)
                    sp.wait_ge(s_sqm_ready, i - 1)
                    sp.wait_ge([s_x1_out0, s_x1_out1][i % 2], 16 * (i // 2))
                    sp.wait_ge(s_s1_ready, i - 1)
                    sp.wait_ge(s_ha_ready, i - 1)
                SY.dma_start(mixb[:, i % 2], mix_d[i]).then_inc([s_mix_in0, s_mix_in1][i % 2], 16)
                SY.dma_start(xb[:, i % 2, :], x_t[i]).then_inc([s_xs_in0, s_xs_in1][i % 2], 16)

            for w in range(2):
                sp.wait_ge([s_bo_out0, s_bo_out1][w], 16 * sum(k[1] == 0 and BON[k] % 2 == w for k in bok))
            load_tile(0)
            load_tile(1)
            for i in range(TPH):
                store_bo(("ln", 1, i))
            sp.wait_ge(s_tp_full, TPN["LF", 1, TPH - 1] + 1)
            gu = wsr.rearrange("p (k w f) -> p k w f", k=KD // 2, w=2)
            SY.dma_start(gu[:, :, 0, :], A["ws_gate"][0, 0:D // 2].rearrange("(k p) f -> p k f", p=P)).then_inc(s_ws_in, 16)
            SY.dma_start(gu[:, :, 1, :], A["ws_up"][0, 0:D // 2].rearrange("(k p) f -> p k f", p=P)).then_inc(s_ws_in, 16)
            for w in range(2):
                sp.wait_ge([s_bo_out0, s_bo_out1][w], 16 * (len(bok) // 2))

            sp.wait_ge(s_zero_ok, 1)
            SY.dma_start(h2_d[T:T + BLK, :], xb[:, 2, :]).then_inc(s_h2z_out, 16)
            SY.dma_start(acc_d[T:T + BLK, :], xb[:, 2, :]).then_inc(s_h2z_out, 16)
            for i in range(NT):
                sp.wait_ge(s_x1_ready, i + 1)
                SY.dma_start(x1_d[i * P:(i + 1) * P, :], xb[:, i % 2, :]).then_inc([s_x1_out0, s_x1_out1][i % 2], 16)
                sp.wait_ge(s_h2_ready, i + 1)
                SY.dma_start(h2_d[i * P:(i + 1) * P, :], h2b[:, i % 2, :]).then_inc([s_h2_out0, s_h2_out1][i % 2], 16)
                if i + 2 < NT:
                    load_tile(i + 2)
                if i == 7:
                    sp.wait_ge(s_ws_lo, 1)
                    SY.dma_start(gu[:, :, 0, :], A["ws_gate"][0, D // 2:D].rearrange("(k p) f -> p k f", p=P)).then_inc(s_ws_in, 16)
                    SY.dma_start(gu[:, :, 1, :], A["ws_up"][0, D // 2:D].rearrange("(k p) f -> p k f", p=P)).then_inc(s_ws_in, 16)
                if i == 12:
                    sp.wait_ge(s_ws_lo, 2)
                    SY.dma_start(wsr.rearrange("p (k f) -> p k f", k=FE), A["ws_down"][0].rearrange("(k p) f -> p k f", p=P)).then_inc(s_ws_in, 16)
            for w in range(2):
                sp.wait_ge([s_h2_out0, s_h2_out1][w], 16 * (NT // 2))
                sp.wait_ge([s_x1_out0, s_x1_out1][w], 16 * (NT // 2))
            sp.wait_ge(s_h2z_out, 32)

            def load_rows(b, w):
                SY.dma_start(xg[w], h2_d[bass.ds(b * BLK, BLK), :]).then_inc([s_xg_in0, s_xg_in1][w], 16)

            def store_y(b, w):
                sp.wait_ge(s_y_act, b + 1)
                SY.dma_start(acc_d[bass.ds(b * BLK, BLK), :], yb[w]).then_inc([s_y_out0, s_y_out1][w], 16)

            def step_rows(b, w):
                sp.wait_ge(s_xt_full, b + 2)
                load_rows(b + 3, 1 - w)
                store_y(b - 1, 1 - w)

            load_rows(0, 0)
            load_rows(1, 1)
            sp.wait_ge(s_cnt_ready, 1)
            SY.dma_start(be_d.rearrange("(t p) -> p t", p=P), bei, allow_slow_non_contiguous=True).then_inc(s_be_out, 16)
            sp.wait_ge(s_be_out, 16)
            SY.dma_start(berow, be_d.unsqueeze(0)).then_inc(s_be_back, 16)
            sp.wait_ge(s_xt_full, 1)
            load_rows(2, 0)
            sp.wait_ge(s_xt_full, 2)
            load_rows(3, 1)
            step_rows(1, 1)
            with sp.Fori(2, 6, 2) as b:
                step_rows(b, 0)
                step_rows(b + 1, 1)
            sp.wait_ge(s_be_back, 16)
            load_expert(0, None)
            load_expert(1, 16)
            with sp.Fori(6, NT - 4, 2) as b:
                step_rows(b, 0)
                step_rows(b + 1, 1)
            step_rows(NT - 4, 0)
            for b in range(NT - 4, NT):
                store_y(b, b % 2)
            for i in range(12, 15):
                SY.dma_start(xps[i], x1_d[i * P:(i + 1) * P, :]).then_inc(s_xp_in, 16)
            nexp = sp.value_load(mint[0:1, 0:1], min_val=TOPK, max_val=E)
            with sp.Fori(2, nexp) as n:
                load_expert(n, 0)
            nexp = sp.value_load(mint[0:1, 0:1], min_val=TOPK, max_val=E)
            for i in range(12):
                if i == 0:
                    sp.wait_ge(s_wlo_ready, nexp)
                    sp.wait_ge(s_wlow_ready, nexp)
                SY.dma_start(xps[i], x1_d[i * P:(i + 1) * P, :]).then_inc(s_xp_in, 16)
            nb = sp.value_load(nbi[0:1, 0:1], min_val=TOPK, max_val=NB)
            sp.wait_ge(s_y_free, nb + 1)
            for i in range(NT):
                if i >= 8:
                    sp.wait_ge(fin_in[i % 8], 16)
                SY.dma_start(fin[i], acc_d[i * P:(i + 1) * P, :]).then_inc(fin_in[i % 8], 16)
            for i in range(NT):
                sp.wait_ge(s_fo_ready, i + 1)
                SY.dma_start(out[0, i * P:(i + 1) * P, :], fin[i]).then_inc(s_fin_out, 16)
                if i == 0:
                    SY.dma_start(xps[15], x1_d[15 * P:16 * P, :]).then_inc(s_xp_in, 16)
            sp.wait_ge(s_fin_out, 16 * NT)

        @blk.tensor
        def _(pe):
            def take(ring, n, full, free, banks):
                if n >= banks:
                    pe.wait_ge(free, n - banks + 1)
                return ring[n % banks]

            def take_tp(key):
                return take(tp, TPN[key], s_tp_full, s_tp_free, 2)

            def take_mm(key):
                return take(mm, MMN[key], s_mm_full, s_mm_free, 2)

            def take_dv(key):
                return take(dv, DVN[key], s_dv_full, s_dv_free, 4)

            pe.wait_ge(s_const_ok, 1)
            pe.wait_ge(s_nat_ready, 1)
            b = take_dv(("nat", 0))
            for n, a in enumerate((nlr, nli, nkr, nki, nm8, nc8, ns8, nt3)):
                TE.transpose(b[:, n * G:(n + 1) * G], a, ident[0:G, 0:G])
            for q in range(CT):
                m = TE.transpose(b[:, 8 * G + q * TAPS:8 * G + (q + 1) * TAPS], cwn[:, q * P:(q + 1) * P], ident[0:TAPS, 0:TAPS])
            m.then_inc(s_dv_full, 1)
            pe.wait_ge(s_csig_ok, 2)
            for n in range(12):
                b = take_dv(("ada", n))
                pe.wait_ge([s_ada_in0, s_ada_in1][n % 2], 32 * (n // 2 + 1))
                for k in range(KD):
                    m = TE.matmul(b[0:1, :], ccol[:, k:k + 1], wada[n % 2][:, k, :], start=(k == 0), stop=(k == KD - 1))
                m.then_inc(s_dv_full, 1)
            pe.wait_ge(s_small_in, 16 * NSMALL)
            pe.wait_ge(s_c_ready, 1)
            for w in range(3):
                b = take_dv(("C", w))
                for q in range(4):
                    m = TE.transpose(b[:, q * P:(q + 1) * P], CN[:, w, q, :], ident[:, :])
                m.then_inc(s_dv_full, 1)
            pe.wait_ge(s_r_ready, 1)
            for n in range(8):
                b = take_dv(("RT", n))
                for j in range(4):
                    m = TE.transpose(b[:, j * P:(j + 1) * P], R[:, 4 * n + j, 0:CH, :].rearrange("p s h -> p (s h)"), ident[:, :])
                m.then_inc(s_dv_full, 1)
            pe.wait_ge(s_c_ready, 2)
            for n in range(8):
                b = take_dv(("TOE", n))
                for j in range(4):
                    g = 4 * n + j
                    for i in range(CH):
                        m = TE.matmul(b[:, j * P + i * HG:j * P + (i + 1) * HG],
                                      R[:, g, CH - 1 - i:2 * CH - 1 - i, :].rearrange("p s h -> p (s h)"), Y1[:, g, :],
                                      start=True, stop=True)
                m.then_inc(s_dv_full, 1)

            def to_hT(h):
                for i in range(TPH):
                    n = h * TPH + i
                    if n in XPOOL:
                        pe.wait_ge(s_xnp_ready, XPOOL.index(n) + 1)
                    else:
                        pe.wait_ge(s_xn_ready, XDVE.index(n) + 1)
                    for c in range(2):
                        b = take_tp(("hT", h, i, c))
                        for k in range(4):
                            m = TE.transpose(b[:, k * P:(k + 1) * P], xb[:, n % 3, (4 * c + k) * P:(4 * c + k + 1) * P], ident[:, :])
                        m.then_inc(s_tp_full, 1)

            def z_ssm(h, steps=range(CH)):
                for j in steps:
                    if j == 0:
                        pe.wait_ge(s_tp_free, TPN["hT", h, TPH - 1, 1] + 1)
                        pe.wait_ge(s_wz_in0, 96 * h + 16)
                        pe.wait_ge(s_wz_in1, 80 * h + 16)
                    b = take_mm(("zs", h, j))
                    for k in range(KD):
                        m = TE.matmul(b[:, :], hT[:, k, :].rearrange("p (c j) -> p j c", j=CH)[:, j, :],
                                      wio[:, k * CC:(k + 1) * CC], start=(k == 0), stop=(k == KD - 1))
                    m.then_inc(s_mm_full, 1)

            def u_transposed(h):
                pe.wait_ge(s_mm_free, MMN["zs", h, CH - 1] + 1)
                for n in range(8):
                    b = take_tp(("UT", h, n))
                    for j in range(4):
                        m = TE.transpose(b[:, j * P:(j + 1) * P], us[:, (4 * n + j) * P:(4 * n + j + 1) * P], ident[:, :])
                    m.then_inc(s_tp_full, 1)

            def inputs_to_state(h):
                pe.wait_ge(s_tp_free, TPN["UT", h, 7] + 1)
                if h == 0:
                    pe.wait_ge(s_rt_ready, 8)
                else:
                    pe.wait_ge(s_tab_in, 32)
                for n in range(4):
                    for w in range(2):
                        b = take_dv(("V", h, n, w))
                        for r in range(4):
                            for f in range(2):
                                g = 2 * (4 * n + r) + f
                                m = TE.matmul(b[f * S:(f + 1) * S, r * P:(r + 1) * P], RT[:, g, w * S:(w + 1) * S],
                                              UT[:, g, :], start=True, stop=True)
                        m.then_inc(s_dv_full, 1)

            def z_conv(h):
                for q in range(CT):
                    pe.wait_ge([s_wz_in0, s_wz_in1][q % 2], (96, 80)[q % 2] * h + 16 + 32 * (q // 2 + 1))
                    for b2 in range(2):
                        for w in range(2):
                            b = take_mm(("zc", h, q, b2, w))
                            for k in range(KD):
                                m = TE.matmul(b[:, :], wz_conv(q)[:, w, k, :], hT[:, k, b2 * 512:(b2 + 1) * 512],
                                              start=(k == 0), stop=(k == KD - 1))
                            m.then_inc(s_mm_full, 1)

            def outputs(h):
                pe.wait_ge(s_tab_in, 16 + 32 * h)
                for n in range(8):
                    b = take_mm(("Y", h, n))
                    pe.wait_ge(s_states_ready, 4 * h + n // 2 + 1)
                    for j in range(4):
                        g = 8 * (n // 2) + 2 * j + n % 2
                        r, lo = g // 2, (n % 2) * S
                        o = b[:, j * P:(j + 1) * P]
                        TE.matmul(o, UT[:, g, :], TOE[:, g, :], start=True, stop=False)
                        TE.matmul(o, SR[lo:lo + S, r, :], COR[lo:lo + S, r, :], start=False, stop=False)
                        m = TE.matmul(o, SI[lo:lo + S, r, :], COI[lo:lo + S, r, :], start=False, stop=True)
                    m.then_inc(s_mm_full, 1)

            def g_transposed(h):
                for q in range(CT):
                    pe.wait_ge(s_mm_free, MMN["Y", h, 2 * q + 1] + 1)
                    for c in range(2):
                        b = take_tp(("GT", h, q, c))
                        for i in range(4):
                            m = TE.transpose(b[:, i * P:(i + 1) * P], GA[:, q, 4 * c + i, :], ident[:, :])
                        m.then_inc(s_tp_full, 1)

            def glu(h):
                pe.wait_ge(s_tp_free, TPN["GT", h, CT - 1, 1] + 1)
                pe.wait_ge(s_wz_in0, 96 * (h + 1))
                for b2 in range(2):
                    for o in range(CT):
                        b = take_mm(("glu", h, b2, o))
                        for q in range(CT):
                            m = TE.matmul(b[:, :], wz[:, 0, q * CC + o * P:q * CC + (o + 1) * P], gT[:, q, b2 * 512:(b2 + 1) * 512],
                                          start=(q == 0), stop=(q == CT - 1))
                        m.then_inc(s_mm_full, 1)

            def norm_turns(h):
                pe.wait_ge(s_conv_ready, CT * (h + 1))
                for i in range(TPH + 1):
                    if i < TPH:
                        b = take_tp(("LF", h, i))
                        for q in range(CT):
                            m = TE.transpose(b[:, q * P:(q + 1) * P], cacc[:, q, i * P:(i + 1) * P], ident[:, :])
                        m.then_inc(s_tp_full, 1)
                    if i >= 1:
                        b = take_tp(("LB", h, i - 1))
                        pe.wait_ge(s_yn_ready, h * TPH + i)
                        for q in range(CT):
                            m = TE.transpose(b[:, q * P:(q + 1) * P], yn[:, q * P:(q + 1) * P], ident[:, :])
                        m.then_inc(s_tp_full, 1)
                    if h == 0 and i < TPH:
                        z_ssm(1, [i])

            for h in range(NH):
                to_hT(h)
                if h == 0:
                    z_ssm(0)
                else:
                    norm_turns(0)
                u_transposed(h)
                inputs_to_state(h)
                z_conv(h)
                outputs(h)
                g_transposed(h)
                glu(h)
            norm_turns(1)

            pe.wait_ge(s_mm_free, len(mmk))
            pe.wait_ge(s_tp_free, len(tpk))
            pe.wait_ge(s_dv_free, len(dvk))
            pe.wait_ge(s_wout_ready, KD)
            pe.wait_ge(s_wr_in, 32)

            def turn_h2(i):
                pe.wait_ge(s_h2_ready, i + 1)
                if i:
                    pe.wait_ge(s_h2t_free, i)
                for k in range(KD):
                    m = TE.transpose(psm[:, 2 + k // 4, (k % 4) * P:(k % 4 + 1) * P], h2b[:, i % 2, k * P:(k + 1) * P], ident[:, :])
                m.then_inc(s_h2t_full, 1)

            def route(i):
                pe.wait_ge(s_h2t_free, i + 1)
                if i:
                    pe.wait_ge(s_sc_ready, i)
                for k in range(KD):
                    m = TE.matmul(psm[:, 7, 0:E], h2T[:, k, :], wr[:, k, :], start=(k == 0), stop=(k == KD - 1))
                m.then_inc(s_lg_full, 1)

            for i in range(NT + 2):
                if i < NT:
                    pe.wait_ge(s_sqm_ready, i + 1)
                    if i:
                        pe.wait_ge(s_ssn_ready, i)
                    for f in range(2):
                        for q in range(CT):
                            m = TE.matmul(psm[:, 6, f:f + 1], sqb[:, f * CT + q, :], one[:, :], start=(q == 0), stop=(q == CT - 1))
                    m.then_inc(s_ss_full, 1)
                    pe.wait_ge([s_mix_in0, s_mix_in1][i % 2], 16 * (i // 2 + 1))
                    if i:
                        pe.wait_ge(s_oa_ready, i)
                    for c in range(2):
                        for q in range(CT):
                            m = TE.matmul(psm[:, c, :], mixb[:, i % 2, q, :], wout[:, q, c * 512:(c + 1) * 512],
                                          start=(q == 0), stop=(q == CT - 1))
                    m.then_inc(s_oa_full, 1)
                if i >= 2:
                    turn_h2(i - 2)
                if i < NT:
                    if i:
                        pe.wait_ge(s_o_ready, i)
                    for c in range(2):
                        for q in range(CT):
                            m = TE.matmul(psm[:, 4 + c, :], mixb[:, i % 2, CT + q, :], wout[:, CT + q, c * 512:(c + 1) * 512],
                                          start=(q == 0), stop=(q == CT - 1))
                    m.then_inc(s_ob_full, 1)
                if i >= 2:
                    route(i - 2)
            pe.wait_ge(s_sel_ready, NT)
            pe.wait_ge(s_const_ok, 1)
            for i in range(NT):
                o = psm[:, 6 + i // 8, (i % 8) * E:(i % 8 + 1) * E]
                TE.matmul(o, tri[:, :], selbf[:, i, :], start=True, stop=False)
                TE.matmul(o, oneb[:, :], selcum[:, i, :], start=False, stop=True)
            TE.matmul(psm[:, 1, DE:DE + E], oneb[:, :], selcum[:, NT, :], start=True, stop=True).then_inc(s_pos_full, 1)

            def turn_rows(b, w, routed=False):
                if routed:
                    pe.wait_ge([s_xr_in0, s_xr_in1][w], ((b - NT) >> 1) * 16 + 16)
                else:
                    pe.wait_ge([s_xg_in0, s_xg_in1][w], (b >> 1) * 16 + 16)
                for k in range(KD):
                    m = TE.transpose(psm[:, 2 + k // 4, (k % 4) * P:(k % 4 + 1) * P], xg[w][:, k * P:(k + 1) * P], ident[:, :])
                m.then_inc(s_xt_full, 1)

            def split_products(o, pairs):
                todo = [(a, w) for ah, al, wh, wl in pairs for a, w in ((ah, wh), (ah, wl), (al, wh))]
                for n, (a, w) in enumerate(todo):
                    m = TE.matmul(o, a, w, start=(n == 0), stop=(n == len(todo) - 1))
                return m

            def gate_up(b, slot):
                pe.wait_ge(s_xt_ready, b + 1)
                hi, lo = ((lambda k, a=a: a[:, bass.ds(slot + k * 2 * DE, 2 * DE)]) for a in (whi, wlo))
                split_products(psm[:, 0, :], [(XH[:, k, :], XL[:, k, :], hi(k), lo(k)) for k in range(KD)]).then_inc(s_gu_full, 1)

            def down(b, slot, first=False):
                pe.wait_ge(s_ht_ready, b + 1)
                if not first:
                    pe.wait_ge(s_y_act, b)
                for c in range(2):
                    hi, lo = ((lambda f, a=a: a[:, bass.ds(slot + WG + f * D + c * 512, 512)]) for a in (whi, wlo))
                    m = split_products(psm[:, 4 + c, :], [(HH[:, f, :], HL[:, f, :], hi(f), lo(f)) for f in range(FE)])
                m.then_inc(s_y_full, 1)

            def turn_h(b):
                pe.wait_ge(s_h_full, b + 1)
                for f in range(FE):
                    m = TE.transpose(psm[:, 1, f * P:(f + 1) * P], hs[:, f * P:(f + 1) * P], ident[:, :])
                m.then_inc(s_ht_full, 1)

            def step(b, w, routed=False):
                gate_up(b, WSLOT)
                turn_rows(b + 1, 1 - w, routed)
                down(b - 1, WSLOT)
                turn_h(b)

            def routed_step(b, w):
                o = pe.value_load(ordi[0:1, bass.ds(b - NT, 1)], min_val=1, max_val=E)
                q = pe.value_load(ordi[0:1, bass.ds(b - (NT + 1), 1)], min_val=1, max_val=E)
                pe.wait_ge(s_wlo_ready, o)
                gate_up(b, ((o + 1) & 1) * WSLOT)
                turn_rows(b + 1, 1 - w, True)
                pe.wait_ge(s_wlow_ready, q)
                down(b - 1, ((q + 1) & 1) * WSLOT)
                turn_h(b)

            turn_rows(0, 0)
            pe.wait_ge(s_ws_lo, 3)
            gate_up(0, WSLOT)
            turn_rows(1, 1)
            turn_h(0)
            gate_up(1, WSLOT)
            turn_rows(2, 0)
            down(0, WSLOT, first=True)
            turn_h(1)
            with pe.Fori(2, NT - 2, 2) as b:
                step(b, 0)
                step(b + 1, 1)
            step(NT - 2, 0)
            step(NT - 1, 1, routed=True)
            pe.wait_ge(s_wlo_ready, 1)
            gate_up(NT, 0)
            turn_rows(NT + 1, 1, True)
            down(NT - 1, WSLOT)
            turn_h(NT)
            pe.wait_ge(s_br_ready, 1)
            routed_step(NT + 1, 1)
            nb = pe.value_load(nbi[0:1, 0:1], min_val=TOPK, max_val=NB)
            with pe.Fori(NT + 2, nb + NT, 2) as b:
                routed_step(b, 0)
                routed_step(b + 1, 1)
            nb = pe.value_load(nbi[0:1, 0:1], min_val=TOPK, max_val=NB)
            q = pe.value_load(ordi[0:1, bass.ds(nb - 1, 1)], min_val=1, max_val=E)
            pe.wait_ge(s_wlow_ready, q)
            down(nb + (NT - 1), ((q + 1) & 1) * WSLOT)

        @blk.scalar
        def _(act):
            ch = Chain(act, s_act_step)
            act.wait_ge(s_par_in, 16 * NFIRST)
            SC.activation(csig[:, :], ccol[:, :], ACT.Sigmoid).then_inc(s_csig_ok, 1)
            ch.do(SC.activation(ndt[:, 1:2], ndt[:, 0:1], ACT.Exp))
            SC.mul(ndt[:, 2:3], ndt[:, 1:2], 8.0).then_inc(s_dt_ready, 1)
            act.wait_ge(s_dt_ready, 1)
            ch.add(SC.activation(nmag, nar, ACT.Exp, scale=ndt[:, 1:2]))
            ch.add(SC.activation(nm8, nar, ACT.Exp, scale=ndt[:, 2:3]))
            act.wait_ge(s_nat_angle, 1)
            ch.add(SC.activation(nsin, nr_, ACT.Sin))
            ch.add(SC.activation(ncos, nr_, ACT.Sin, scale=0.5))
            ch.add(SC.activation(ns8, nn, ACT.Sin))
            ch.add(SC.activation(nc8, nn, ACT.Sin, scale=0.5))
            ch.sync()
            SC.copy(nden, nar).then_inc(s_nat_trig, 1)

            xin = [s_x_in0, s_x_in1, s_x_in2]

            def to_hT(h):
                def square(n):
                    act.wait_ge(xin[n % 3], 16 * (n // 3 + 1))
                    if n:
                        act.wait_ge(s_sq_ready, n)
                    elif h == 0:
                        act.wait_ge(s_toe_ready, 1)
                    SC.activation(work[:, 2048:3072], xb[:, n % 3, :], ACT.Square, accum_out=st[:, n:n + 1]).then_inc(s_sq_ready, 1)

                def evac(i):
                    for c in range(2):
                        n = TPN["hT", h, i, c]
                        act.wait_ge(s_tp_full, n + 1)
                        SC.copy(hT[:, 4 * c:4 * c + 4, i * P:(i + 1) * P], tp[n % 2].rearrange("p (k t) -> p k t", k=4)).then_inc(s_tp_free, 1)

                if h:
                    act.wait_ge(s_sg_free, SGN["glu", 0, 1, CT - 1] + 1)
                square(h * TPH)
                for i in range(TPH):
                    n = h * TPH + i
                    if i + 1 < TPH:
                        square(n + 1)
                    if n in XPOOL:
                        act.wait_ge(s_stat_ready, n + 1)
                        SC.activation(xb[:, n % 3, :], xb[:, n % 3, :], ACT.Copy, scale=st[:, 32 + n:33 + n]).then_inc(s_xr_ready, 1)
                    if i:
                        evac(i - 1)
                evac(TPH - 1)

            def z_ssm(h, steps=range(CH)):
                for j in steps:
                    n = MMN["zs", h, j]
                    act.wait_ge(s_mm_full, n + 1)
                    SC.copy(U[:, :, j, :], mm[n % 2].rearrange("p (g h) -> p g h", g=G)).then_inc(s_mm_free, 1)

            def u_transposed(h):
                for n in range(8):
                    k = TPN["UT", h, n]
                    act.wait_ge(s_tp_full, k + 1)
                    SC.copy(ut[:, n * 512:(n + 1) * 512], tp[k % 2]).then_inc(s_tp_free, 1)

            def z_conv(h):
                for q in range(CT):
                    for b in range(2):
                        n = MMN["zc", h, q, b, 0]
                        act.wait_ge(s_mm_full, n + 1)
                        if h and b == 0:
                            act.wait_ge(s_v_tail, q + 1)
                        if h == 0 and q == 0 and b == 0:
                            act.wait_ge(s_tab_out, 48)
                        SC.copy(v[:, q, PAD + b * 512:PAD + (b + 1) * 512], mm[n % 2]).then_inc(s_mm_free, 1)
                        act.wait_ge(s_mm_full, n + 2)
                        k = SGN["zc", h, q, b]
                        if k >= 2:
                            act.wait_ge(s_sg_free, k - 1)
                        SC.activation(sg[k % 2], mm[(n + 1) % 2], ACT.Sigmoid).then_inc(s_mm_free, 1)

            def outputs(h):
                for n in range(8):
                    k = MMN["Y", h, n]
                    act.wait_ge(s_mm_full, MMN["Y", h, n | 1] + 1)
                    o = GA[:, n // 2].rearrange("p i (g f h) -> p f g i h", f=2, h=HG)[:, n % 2]
                    SC.activation(o, mm[k % 2].rearrange("p (g i h) -> p g i h", g=4, i=CH), ACT.Gelu_apprx_tanh).then_inc(s_mm_free, 1)

            def g_transposed(h):
                for q in range(CT):
                    for c in range(2):
                        n = TPN["GT", h, q, c]
                        act.wait_ge(s_tp_full, n + 1)
                        o = gT[:, q, :].rearrange("p (c i) -> p i c", i=CH)[:, 4 * c:4 * c + 4, :]
                        SC.copy(o, tp[n % 2].rearrange("p (i c) -> p i c", i=4)).then_inc(s_tp_free, 1)

            def glu(h):
                for b in range(2):
                    for q in range(CT):
                        n = MMN["glu", h, b, q]
                        k = SGN["glu", h, b, q]
                        act.wait_ge(s_mm_full, n + 1)
                        act.wait_ge(s_sg_free, k - 1)
                        SC.activation(sg[k % 2], mm[n % 2], ACT.Sigmoid, bias=col[:, 3, q:q + 1]).then_inc(s_mm_free, 1)

            def norm_turns(h):
                for i in range(TPH + 1):
                    if i < TPH:
                        n = TPN["LF", h, i]
                        act.wait_ge(s_tp_full, n + 1)
                        if h * TPH + i:
                            act.wait_ge(s_yn_ready, h * TPH + i)
                        SC.copy(ytok[:, :], tp[n % 2]).then_inc(s_tp_free, 1)
                    if i >= 1:
                        n = TPN["LB", h, i - 1]
                        k = SGN["ln", h, i - 1]
                        act.wait_ge(s_tp_full, n + 1)
                        act.wait_ge(s_sg_free, k)
                        for q in range(CT):
                            m = SC.activation(ly[:, q * P:(q + 1) * P], tp[n % 2][:, q * P:(q + 1) * P], ACT.Identity,
                                              bias=col[:, 2, q:q + 1], scale=col[:, 1, q:q + 1])
                        m.then_inc(s_tp_free, 1)
                        act.wait_ge(s_tp_free, n + 1)
                        SC.activation(sg[k % 2], ly[:, :], ACT.Sigmoid).then_inc(s_ly_full, 1)
                    if h == 0 and i < TPH:
                        z_ssm(1, [i])

            for h in range(NH):
                to_hT(h)
                if h == 0:
                    z_ssm(0)
                else:
                    norm_turns(0)
                u_transposed(h)
                z_conv(h)
                outputs(h)
                g_transposed(h)
                glu(h)
            act.wait_ge(s_small_in, 16 * NSMALL)
            act.wait_ge(s_wout_in, 16 * KD)
            for k in range(KD):
                SC.activation(wout[:, k, :], wout[:, k, :], ACT.Copy, scale=gout[:, k:k + 1]).then_inc(s_wout_ready, 1)
            norm_turns(1)

            def square_mix(i):
                act.wait_ge([s_mix_in0, s_mix_in1][i % 2], 16 * (i // 2 + 1))
                if i:
                    act.wait_ge(s_ss_full, i)
                SC.activation(us[:, 2048:3072], us[:, (i % 2) * 1024:(i % 2 + 1) * 1024], ACT.Square).then_inc(s_sqm_ready, 1)

            square_mix(0)
            for i in range(NT + 2):
                c0 = 16 * (i % 2)
                if i < NT:
                    act.wait_ge(s_oa_full, i + 1)
                    act.wait_ge(s_rr_ready, i + 1)
                    if i:
                        act.wait_ge(s_x1_ready, i)
                    SC.activation(ob, psm[:, 0:2, :].rearrange("p a n -> p (a n)"), ACT.Copy, scale=st[:, c0 + 2:c0 + 3]).then_inc(s_oa_ready, 1)
                if i + 1 < NT:
                    square_mix(i + 1)
                if i >= 2:
                    act.wait_ge(s_h2t_full, i - 1)
                    if i >= 3:
                        act.wait_ge(s_lg_full, i - 2)
                    SC.copy(us[:, 3072:4096], psm[:, 2:4, :].rearrange("p a n -> p (a n)")).then_inc(s_h2t_free, 1)
                if i < NT:
                    act.wait_ge(s_o_ready, i + 1)
                    if i:
                        act.wait_ge(s_s1_ready, i)
                    SC.activation(junk, ob, ACT.Square, accum_out=st[:, c0 + 4:c0 + 5]).then_inc(s_so_ready, 1)
                if i >= 2:
                    act.wait_ge(s_lg_full, i - 1)
                    if i >= 3:
                        act.wait_ge(s_sel_ready, i - 2)
                    SC.activation(scores, psm[:, 7, 0:E], ACT.Sigmoid).then_inc(s_sc_ready, 1)
                if i in (5, 10, 15):
                    n = i // 5 - 1
                    act.wait_ge(s_ws_in, (32, 64, 80)[n])
                    SC.copy(whi[:, WSLOT + n * WC:WSLOT + (n + 1) * WC], wsr).then_inc(s_ws_hi, 1)
                if i < NT:
                    act.wait_ge(s_x1_ready, i + 1)
                    act.wait_ge(s_so_ready, i + 1)
                    SC.activation(junk, xb[:, i % 2, :], ACT.Square, accum_out=st[:, c0 + 7:c0 + 8]).then_inc(s_s1_ready, 1)

            def rows_high(b):
                act.wait_ge(s_xt_full, b + 1)
                SC.copy(xhi[:, :], psm[:, 2:4, :].rearrange("p a n -> p (a n)")).then_inc(s_xt_high, 1)

            def sig(b):
                act.wait_ge(s_gu_full, b + 1)
                SC.activation(sigb, psm[:, 0, 0:DE], ACT.Sigmoid).then_inc(s_sig_ready, 1)

            def out(b, w, stored=None, added=None):
                act.wait_ge(s_y_full, b + 1)
                if stored is not None:
                    act.wait_ge([s_y_out0, s_y_out1][w], stored)
                if added is not None:
                    act.wait_ge(s_y_free, added)
                SC.copy(yb[w], psm[:, 4:6, :].rearrange("p a n -> p (a n)")).then_inc(s_y_act, 1)

            def h_high(b):
                act.wait_ge(s_ht_full, b + 1)
                SC.copy(hhi[:, :], psm[:, 1, 0:DE]).then_inc(s_ht_high, 1)

            def split_high(slot, number):
                act.wait_ge(s_wgate_in, number)
                act.wait_ge(s_wup_in, number)
                for c in range(NGC):
                    SC.copy(whi[:, bass.ds(slot + c * GC, GC)], raw[:, bass.ds(slot + c * GC, GC)]).then_inc(s_whi_ready, 1)

            def split_high_down(slot, number):
                act.wait_ge(s_wdown_in, number)
                SC.copy(whi[:, bass.ds(slot + WG, WC)], raw[:, bass.ds(slot + WG, WC)]).then_inc(s_whid_ready, 1)

            def step(b, w, first_routed=False):
                sig(b)
                rows_high(b + 1)
                if first_routed:
                    fn = act.value_load(splits[0:1, 1:2], min_val=0, max_val=1)
                    with act.If(fn > 0):
                        split_high(0, 48)
                out(b - 1, 1 - w, stored=((b - 1) >> 1) * 16)
                h_high(b)

            def routed_step(b, w, stored=None):
                f = act.value_load(splits[0:1, bass.ds(b - NT, 1)], min_val=0, max_val=1)
                o = act.value_load(ordi[0:1, bass.ds(b - NT, 1)], min_val=1, max_val=E)
                fn = act.value_load(splits[0:1, bass.ds(b - (NT - 1), 1)], min_val=0, max_val=1)
                on = act.value_load(ordi[0:1, bass.ds(b - (NT - 1), 1)], min_val=1, max_val=E)
                sig(b)
                rows_high(b + 1)
                with act.If(fn > 0):
                    split_high((on & 1) * WSLOT, (on + 1) * 16)
                if stored is not None:
                    out(b - 1, 1 - w, stored=stored)
                else:
                    out(b - 1, 1 - w, added=b - (NT + 1))
                h_high(b)
                with act.If(f > 0):
                    split_high_down((o & 1) * WSLOT, (o + 1) * 16)

            rows_high(0)
            sig(0)
            rows_high(1)
            h_high(0)
            sig(1)
            rows_high(2)
            out(0, 0)
            h_high(1)
            sig(2)
            rows_high(3)
            out(1, 1)
            h_high(2)
            step(3, 1)
            with act.Fori(4, NT - 2, 2) as b:
                step(b, 0)
                step(b + 1, 1)
            step(NT - 2, 0)
            act.wait_ge(s_br_ready, 1)
            act.wait_ge(s_rows_back, 16)
            split_high(0, 16)
            split_high_down(0, 16)
            step(NT - 1, 1)
            split_high(WSLOT, 32)
            step(NT, 0, first_routed=True)
            split_high_down(WSLOT, 32)
            routed_step(NT + 1, 1, stored=NT * 8)
            nb = act.value_load(nbi[0:1, 0:1], min_val=TOPK, max_val=NB)
            with act.Fori(NT + 2, nb + NT, 2) as b:
                routed_step(b, 0)
                routed_step(b + 1, 1)
            nb = act.value_load(nbi[0:1, 0:1], min_val=TOPK, max_val=NB)
            out(nb + (NT - 1), 1, added=act.value_load(nbm[0:1, 0:1], min_val=TOPK - 1, max_val=NB))
            for i in range(NT):
                act.wait_ge(fin_in[i % 8], 16 * (i // 8 + 1))
                if i:
                    act.wait_ge(s_fs_ready, i)
                SC.activation(yb[0], fin[i], ACT.Square, accum_out=st[:, i:i + 1]).then_inc(s_fs_ready, 1)

        @blk.vector
        def _(dve):
            ch = Chain(dve, s_dve_step)
            tt, ts, stt = V.tensor_tensor, V.tensor_scalar, V.scalar_tensor_tensor
            do, add, sync = ch.do, ch.add, ch.sync

            def got(key):
                n = DVN[key]
                dve.wait_ge(s_dv_full, n + 1)
                return dv[n % 4]

            dve.wait_ge(s_csig_ok, 1)
            V.tensor_mul(ccol[:, :], ccol[:, :], csig[:, :]).then_inc(s_csig_ok, 1)
            dve.wait_ge(s_dt_ready, 1)
            do(ts(nth, nai, ndt[:, 1:2], None, ALU.mult))
            for mul_, o in ((1.0, nr_), (float(CH), nn)):
                do(ts(nt1, nth, mul_, None, ALU.mult))
                do(ts(nt2, nt1, 1.0 / (2 * np.pi), MAGIC, ALU.mult, ALU.add))
                do(ts(nt2, nt2, MAGIC, None, ALU.subtract))
                for c in (C1, C2, C3):
                    do(stt(nt1, nt2, -c, nt1, ALU.mult, ALU.add))
                do(ts(o, nt1, 3.1415925, -3.1415925, ALU.min, ALU.max))
            V.tensor_copy(nt3.rearrange("g (j h) -> g j h", j=CH),
                          nd[:, 0:HG].unsqueeze(1).to_broadcast([G, CH, HG])).then_inc(s_nat_angle, 1)
            dve.wait_ge(s_nat_trig, 1)
            do(tt(ncos, ncos, ncos, ALU.mult), tt(nc8, nc8, nc8, ALU.mult))
            do(ts(ncos, ncos, -2.0, 1.0, ALU.mult, ALU.add), ts(nc8, nc8, -2.0, 1.0, ALU.mult, ALU.add))
            do(tt(nlr, nmag, ncos, ALU.mult), tt(nli, nmag, nsin, ALU.mult))
            do(tt(nt1, nar, nar, ALU.mult), tt(nt2, nai, nai, ALU.mult))
            do(tt(nden, nt1, nt2, ALU.add), ts(nth, nlr, -1.0, None, ALU.add))
            do(V.reciprocal(nden, nden), tt(nt1, nth, nar, ALU.mult), tt(nt2, nli, nai, ALU.mult))
            do(tt(nkr, nt1, nt2, ALU.add))
            do(tt(nt1, nli, nar, ALU.mult), tt(nt2, nth, nai, ALU.mult))
            do(tt(nki, nt1, nt2, ALU.subtract), tt(nkr, nkr, nden, ALU.mult))
            do(tt(nki, nki, nden, ALU.mult))
            V.tensor_copy(nt1, nki).then_inc(s_nat_ready, 1)
            b = got(("nat", 0))
            dve.wait_ge(s_nat_ready, 1)
            add(V.tensor_copy(cw[:, :, :], b[:, 8 * G:8 * G + CT * TAPS].rearrange("p (q t) -> p q t", q=CT)))
            V.tensor_copy(dup, b[:, 0:8 * G].rearrange("p (n g) -> p n g", n=8)).then_inc(s_dv_free, 1)
            dve.wait_ge(s_dv_free, 1)
            LR_, LI_, KR, KI, M8, C8, S8, DC = (dup[:, n, :] for n in range(8))
            halves = ((0, S, 0), (S, P, 1))

            def powers():
                do(V.memset(L[:, 0, 0, :], 1.0), V.memset(L[:, 1, 0, :], 0.0), V.memset(last[:, :, :], 0.0))
                t = [PT[0][:, n * G:(n + 1) * G] for n in range(4)]
                for k in range(1, CH + 1):
                    do(tt(t[0], L[:, 0, k - 1], LR_, ALU.mult), tt(t[1], L[:, 1, k - 1], LI_, ALU.mult),
                       tt(t[2], L[:, 0, k - 1], LI_, ALU.mult), tt(t[3], L[:, 1, k - 1], LR_, ALU.mult))
                    do(tt(L[:, 0, k], t[0], t[1], ALU.subtract), tt(L[:, 1, k], t[2], t[3], ALU.add))
                for lo, hi, f in halves:
                    pick = lambda a: a.rearrange("p (r f) -> p f r", f=2)[:, f, :]
                    for w in range(2):
                        add(V.tensor_copy(LP[lo:hi, w], L[lo:hi, w].rearrange("p k (r f) -> p f k r", f=2)[:, f]))
                        add(V.tensor_copy(lam8[lo:hi, w], pick(L[lo:hi, w, CH])))
                    for n, a in ((2, M8), (3, C8), (4, S8)):
                        add(V.tensor_copy(lam8[lo:hi, n], pick(a[lo:hi])))
                sync()

            def inputs():
                dve.wait_ge(s_small_in, 16 * NSMALL)
                do(ts(X2[0:S], X2[0:S], -1.0, None, ALU.mult))
                kr, ki = (a.unsqueeze(2).to_broadcast([P, G, HG]) for a in (KR, KI))
                t = [PT[0][:, 0:512].rearrange("p (g h) -> p g h", g=G), PT[0][:, 512:1024].rearrange("p (g h) -> p g h", g=G),
                     PT[1][:, 0:512].rearrange("p (g h) -> p g h", g=G), PT[1][:, 512:1024].rearrange("p (g h) -> p g h", g=G)]
                do(tt(t[0], X1, kr, ALU.mult), tt(t[1], X2, ki, ALU.mult), tt(t[2], X2, kr, ALU.mult), tt(t[3], X1, ki, ALU.mult))
                do(tt(BB1, t[0], t[1], ALU.add), tt(BB2, t[2], t[3], ALU.subtract), V.memset(R[:, :, CH:, :], 0.0))
                do(ts(CN[:, 0, :, S:P], CN[:, 0, :, S:P], -1.0, None, ALU.mult))
                V.tensor_copy(ndt[:, 3:4], ndt[:, 0:1]).then_inc(s_c_ready, 1)

            def input_powers(ks):
                for k in ks:
                    t = [PT[2 * (k % 2)][:, 0:512].rearrange("p (g h) -> p g h", g=G), PT[2 * (k % 2) + 1][:, 0:512].rearrange("p (g h) -> p g h", g=G)]
                    do(tt(t[0], BB1, L[:, 0, k].unsqueeze(2).to_broadcast([P, G, HG]), ALU.mult),
                       tt(t[1], BB2, L[:, 1, k].unsqueeze(2).to_broadcast([P, G, HG]), ALU.mult))
                    m = tt(R[:, :, CH - 1 - k, :], t[0], t[1], ALU.add)
                    add(m)
                sync()
                if ks[-1] == CH - 1:
                    V.tensor_copy(ndt[:, 3:4], ndt[:, 0:1]).then_inc(s_r_ready, 1)

            cm = bn[:, 0:4]
            cmt = [PT[3][:, n * NPR:(n + 1) * NPR] for n in range(6)]

            def phasors(ms):
                for m in ms:
                    if m == 1:
                        do(V.memset(EC[:, :, 0], 1.0), V.memset(ES[:, :, 0], 0.0), V.tensor_copy(cmt[0], lam8[:, 3]), V.tensor_copy(cmt[1], lam8[:, 4]))
                    t = [PT[n][:, 0:NPR * min(m, 64)].rearrange("p (r c) -> p r c", r=NPR) for n in range(3)]
                    cr, ci = (cmt[n].unsqueeze(2).to_broadcast([P, NPR, m]) for n in range(2))
                    do(tt(t[0], EC[:, :, 0:m], cr, ALU.mult), tt(t[1], ES[:, :, 0:m], ci, ALU.mult), tt(t[2], ES[:, :, 0:m], cr, ALU.mult))
                    do(tt(EC[:, :, m:2 * m], t[0], t[1], ALU.subtract))
                    do(tt(t[0], EC[:, :, 0:m], ci, ALU.mult), tt(cmt[2], cmt[0], cmt[0], ALU.mult), tt(cmt[3], cmt[1], cmt[1], ALU.mult), tt(cmt[4], cmt[0], cmt[1], ALU.mult))
                    do(tt(ES[:, :, m:2 * m], t[0], t[2], ALU.add), tt(cmt[0], cmt[2], cmt[3], ALU.subtract), ts(cmt[1], cmt[4], 2.0, None, ALU.mult))
                if ms[-1] == 64:
                    V.tensor_copy(ndt[:, 3:4], ndt[:, 0:1]).then_inc(s_phasor_ready, 1)

            pieces = [powers, inputs, lambda: input_powers([0, 1, 2, 3]), lambda: input_powers([4, 5, 6, 7]),
                      lambda: phasors([1, 2, 4]), lambda: phasors([8, 16]), lambda: phasors([32]), lambda: phasors([64])]
            for n in range(12):
                b = got(("ada", n))
                dve.wait_ge([s_ada_in0, s_ada_in1][n % 2], 32 * (n // 2 + 1))
                if n >= 2:
                    dve.wait_ge([s_mod_out0, s_mod_out1][n % 2], 16 * (n // 2))
                tt(seg[0:1, n % 2, :], b[0:1, :], segb[n % 2][0:1, :], ALU.add).then_inc(s_dv_free, 1)
                dve.wait_ge(s_dv_free, DVN["ada", n] + 1)
                V.tensor_copy(ndt[:, 3:4], ndt[:, 0:1]).then_inc(s_seg_ok, 1)
                if n < len(pieces):
                    pieces[n]()
            b = got(("C", 0))
            V.tensor_copy(Y1.rearrange("p g h -> p (g h)"), b).then_inc(s_dv_free, 1)
            for n, o in ((1, CRP), (2, CIP)):
                b = got(("C", n)).rearrange("p (r f h) -> p f r h", f=2, h=HG)
                add(V.tensor_copy(o[0:S], b[0:S, 0]))
                V.tensor_copy(o[S:P], b[S:P, 1]).then_inc(s_dv_free, 1)
            sync()
            dve.wait_ge(s_dv_free, DVN["C", 2] + 1)
            V.tensor_copy(ndt[:, 3:4], ndt[:, 0:1]).then_inc(s_c_ready, 1)
            for n in range(8):
                b = got(("RT", n))
                V.tensor_copy(tabs[:, n * 512:(n + 1) * 512], b).then_inc(s_dv_free, 1)
                dve.wait_ge(s_dv_free, DVN["RT", n] + 1)
                V.tensor_copy(ndt[:, 3:4], ndt[:, 0:1]).then_inc(s_rt_ready, 1)
            for n in range(8):
                b = got(("TOE", n))
                for j in range(4):
                    g = 4 * n + j
                    m = stt(ctoe[:, g, :], ident[:, :], DC[:, g:g + 1], b[:, j * P:(j + 1) * P], ALU.mult, ALU.add)
                    if j == 3:
                        m.then_inc(s_dv_free, 1)
                    else:
                        add(m)
                lr, li = (LP[:, w, n + 1].unsqueeze(2).to_broadcast([P, NPR, HG]) for w in range(2))
                t = [PT[j][:, 0:256].rearrange("p (r h) -> p r h", r=NPR) for j in range(4)]
                do(tt(t[0], CRP, lr, ALU.mult), tt(t[1], CIP, li, ALU.mult), tt(t[2], CRP, li, ALU.mult), tt(t[3], CIP, lr, ALU.mult))
                do(tt(ccor[:, :, n, :], t[0], t[1], ALU.subtract), stt(ccoi[:, :, n, :], t[2], -1.0, t[3], ALU.mult, ALU.subtract))
            dve.wait_ge(s_dv_free, DVN["TOE", 7] + 1)
            V.tensor_copy(ndt[:, 3:4], ndt[:, 0:1]).then_inc(s_toe_ready, 1)
            dve.wait_ge(s_rows_in, 48)
            stt(arow, arow, 1.0, xb[:, 2, :], ALU.add, ALU.mult).then_inc(s_arow_ready, 1)

            def modulate(h):
                for n in range(h * TPH, (h + 1) * TPH):
                    if n in XDVE:
                        dve.wait_ge(s_stat_ready, n + 1)
                        if n == 0:
                            dve.wait_ge(s_arow_ready, 1)
                        x = xb[:, n % 3, :]
                        do(stt(x, x, st[:, 32 + n:33 + n], arow, ALU.mult, ALU.mult))
                        tt(x, x, brow, ALU.add).then_inc(s_xn_ready, 1)

            modulate(0)
            dve.wait_ge(s_tab_out, 48)
            do(V.memset(v[:, :, 0:PAD], 0.0))

            def states(h):
                if h:
                    dve.wait_ge(s_et_in, 16)
                    c8, s8, l0, l1 = lam8[:, 3], lam8[:, 4], last[:, 0], last[:, 1]
                    t = [rot[:, n, 0:NPR] for n in range(4)]
                    do(tt(t[0], c8, l0, ALU.mult), tt(t[1], s8, l1, ALU.mult), tt(t[2], s8, l0, ALU.mult), tt(t[3], c8, l1, ALU.mult))
                    do(tt(last[:, 2], t[0], t[1], ALU.subtract), tt(last[:, 3], t[2], t[3], ALU.add))
                t = [rot[:, n, :].rearrange("p (r c) -> p r c", r=4) for n in range(4)]
                for n in range(4):
                    r = slice(4 * n, 4 * n + 4)
                    vr = got(("V", h, n, 0)).rearrange("p (r c) -> p r c", r=4)
                    add(tt(t[0], vr, EC[:, r], ALU.mult))
                    tt(t[3], vr, ES[:, r], ALU.mult).then_inc(s_dv_free, 1)
                    vi = got(("V", h, n, 1)).rearrange("p (r c) -> p r c", r=4)
                    add(tt(t[1], vi, ES[:, r], ALU.mult))
                    tt(t[2], vi, EC[:, r], ALU.mult).then_inc(s_dv_free, 1)
                    sync()
                    dve.wait_ge(s_dv_free, DVN["V", h, n, 1] + 1)
                    do(tt(SR[:, r], t[0], t[1], ALU.add), tt(SI[:, r], t[2], t[3], ALU.subtract))
                    for q in range(4 * n, 4 * n + 4):
                        for w, a in ((0, SR), (1, SI)):
                            add(V.tensor_tensor_scan(a[:, q, :], lam8[:, 2, q:q + 1].to_broadcast([P, NC]), a[:, q, :],
                                                     last[:, 2 + w, q:q + 1] if h else 0.0, ALU.mult, ALU.add))
                    sync()
                    do(tt(t[0], SR[:, r], EC[:, r], ALU.mult), tt(t[1], SI[:, r], ES[:, r], ALU.mult),
                       tt(t[2], SR[:, r], ES[:, r], ALU.mult), tt(t[3], SI[:, r], EC[:, r], ALU.mult))
                    for w, (a, x0, x1, op) in enumerate(((SR, t[0], t[1], ALU.subtract), (SI, t[2], t[3], ALU.add))):
                        add(tt(a[:, r, 1:NC], x0[:, :, 0:NC - 1], x1[:, :, 0:NC - 1], op))
                        if h == 0:
                            add(tt(last[:, w, r], x0[:, :, NC - 1], x1[:, :, NC - 1], op))
                            add(V.memset(a[:, r, 0:1], 0.0))
                        else:
                            add(V.tensor_copy(a[:, r, 0], last[:, w, r]))
                    sync()
                    V.tensor_copy(ndt[:, 3:4], ndt[:, 0:1]).then_inc(s_states_ready, 1)

            def conv(h):
                if h:
                    dve.wait_ge(s_tp_full, TPN["LF", 0, TPH - 1] + 1)
                for q in range(CT):
                    dve.wait_ge(s_v_ready, (h * CT + q + 1) * 2)
                    o = cacc[:, q, :]
                    do(ts(o, v[:, q, 0:HT], cw[:, q, 0:1], col[:, 0, q:q + 1], ALU.mult, ALU.add))
                    for k in range(1, TAPS):
                        m = stt(o, v[:, q, k:k + HT], cw[:, q, k:k + 1], o, ALU.mult, ALU.add)
                        if k < TAPS - 1:
                            do(m)
                        else:
                            m.then_inc(s_conv_ready, 1)
                    if h == 0:
                        dve.wait_ge(s_conv_ready, q + 1)
                        V.tensor_copy(v[:, q, 0:PAD], v[:, q, HT:HT + PAD]).then_inc(s_v_tail, 1)

            def norm_stats(h):
                for i in range(TPH):
                    k = h * TPH + i
                    dve.wait_ge(s_tp_free, TPN["LF", h, i] + 1)
                    if k:
                        dve.wait_ge(s_yn_ready, k)
                    do(V.bn_stats(bn[:, 0:6], ytok[:, :]))
                    V.bn_aggr(bn[:, 6:8], bn[:, 0:6]).then_inc(s_bn_ready, 1)
                    dve.wait_ge(s_bn_ready, k + 1)

            states(0)
            conv(0)
            modulate(1)
            norm_stats(0)
            states(1)
            conv(1)
            norm_stats(1)

            dve.wait_ge(s_row_in, 7 * 16)
            do(tt(rows[:, 0], rows[:, 0], rtmp[:, 0], ALU.mult), stt(rows[:, 1], rows[:, 1], 1.0, rtmp[:, 1], ALU.add, ALU.mult),
               tt(rows[:, 3], rows[:, 3], rtmp[:, 2], ALU.mult), V.memset(selcum[:, 0, :], 0.0), V.memset(ones64, 1.0))
            V.tensor_copy(ndt[:, 3:4], ndt[:, 0:1]).then_inc(s_row_ready, 1)
            dve.wait_ge(s_wr_in, 32)

            def choose(i):
                dve.wait_ge(s_sc_ready, i + 1)
                do(tt(biased, scores, rbias, ALU.add))
                for g in range(NG):
                    add(V.max(v8[:, g, :], biased[:, g * 8:(g + 1) * 8]))
                sync()
                do(tt(gs, v8[:, :, 0], v8[:, :, 1], ALU.add))
                mine, other = gs.unsqueeze(2).to_broadcast([P, NG, NG]), gs.unsqueeze(1).to_broadcast([P, NG, NG])
                do(tt(cmpa, other, mine, ALU.is_gt), tt(cmpb, other, mine, ALU.is_equal))
                do(tt(cmpb, cmpb, sel8[:, :, :], ALU.mult))
                do(tt(cmpa, cmpa, cmpb, ALU.add))
                do(V.tensor_reduce(rank, cmpa, AX.X, ALU.add))
                do(ts(gm, rank, TOPG - 0.5, None, ALU.is_lt))
                do(ts(gp, gm, -1.0, BIG, ALU.add, ALU.mult))
                b3 = lambda a: a.rearrange("p (g m) -> p g m", g=NG)
                do(tt(b3(bm), b3(biased), gm.unsqueeze(2).to_broadcast([P, NG, 8]), ALU.mult))
                do(tt(b3(bm), b3(bm), gp.unsqueeze(2).to_broadcast([P, NG, 8]), ALU.add))
                do(V.max(t8, bm))
                do(V.match_replace(rep, t8, bm, -3e38))
                do(tt(selall[:, i, :], rep, bm, ALU.not_equal))
                do(V.tensor_copy(selbf[:, i, :], selall[:, i, :]), tt(pen, scores, selall[:, i, :], ALU.mult))
                do(tt(selcum[:, i + 1, :], selcum[:, i, :], selbf[:, i, :], ALU.add), V.tensor_reduce(gsum[:, 0:1], pen, AX.X, ALU.add))
                do(ts(gsum[:, 0:1], gsum[:, 0:1], 1e-20, None, ALU.add))
                do(V.reciprocal(gsum[:, 1:2], gsum[:, 0:1]))
                ts(gwall[:, i, :], pen, gsum[:, 1:2], 2.5, ALU.mult, ALU.mult).then_inc(s_sel_ready, 1)

            dve.wait_ge(s_zero_ok, 1)
            for i in range(NT + 2):
                c0 = 16 * (i % 2)
                if i < NT:
                    dve.wait_ge(s_ss_full, i + 1)
                    ts(st[:, c0:c0 + 2], psm[:, 6, 0:2], 1.0 / CC, EPS, ALU.mult, ALU.add).then_inc(s_ssn_ready, 1)
                    dve.wait_ge(s_ob_full, i + 1)
                    dve.wait_ge(s_oa_ready, i + 1)
                    stt(ob, psm[:, 4:6, :].rearrange("p a n -> p (a n)"), st[:, c0 + 3:c0 + 4], ob, ALU.mult, ALU.add).then_inc(s_o_ready, 1)
                    dve.wait_ge(s_ro_ready, i + 1)
                    stt(ob, ob, st[:, c0 + 6:c0 + 7], rows[:, 0], ALU.mult, ALU.mult).then_inc(s_t_ready, 1)
                    dve.wait_ge(s_r1_ready, i + 1)
                    if i >= 2:
                        dve.wait_ge(s_h2t_full, i - 1)
                        dve.wait_ge([s_h2_out0, s_h2_out1][i % 2], 16 * (i // 2))
                    stt(h2b[:, i % 2, :], xb[:, i % 2, :], st[:, c0 + 9:c0 + 10], rows[:, 1], ALU.mult, ALU.mult).then_inc(s_ha_ready, 1)
                if i >= 2:
                    choose(i - 2)
                if i in (6, 11, 16):
                    n = i // 5 - 1
                    dve.wait_ge(s_ws_hi, n + 1)
                    tt(wlo[:, WSLOT + n * WC:WSLOT + (n + 1) * WC], wsr, whi[:, WSLOT + n * WC:WSLOT + (n + 1) * WC], ALU.subtract).then_inc(s_ws_lo, 1)
            dve.wait_ge(s_sel_ready, NT)

            def counts():
                dve.wait_ge(s_pos_full, 1)
                do(ts(cnti, psm[:, 1, DE:DE + E], float(BLK - 1), None, ALU.add))
                do(ts(cnti, cnti, 7, None, ALU.arith_shift_right))
                do(V.tensor_copy(nbf, cnti))
                do(V.tensor_tensor_scan(pend, ones64, nbf, 0.0, ALU.mult, ALU.add))
                do(tt(basef, pend, nbf, ALU.subtract), V.tensor_copy(pint, pend))
                do(ts(nbi, pint[:, E - 1:E], 1, None, ALU.add))
                do(ts(nbi, nbi, 1, None, ALU.arith_shift_right))
                do(ts(nbi, nbi, 2.0, None, ALU.mult))
                do(ts(nbm, nbi, -1.0, None, ALU.add))
                do(ts(basef, basef, float(BLK), 1.0, ALU.mult, ALU.add))
                dve.wait_ge(s_rinit_ready, 1)
                for c in range(2):
                    do(ts(cntf, pend, bidx[:, c:c + 1], None, ALU.is_le))
                    do(V.tensor_reduce(bep[:, c:c + 1], cntf, AX.X, ALU.add))
                do(ts(cntf, nbf, 0.5, None, ALU.is_gt))
                do(V.tensor_tensor_scan(cntf, ones64, cntf, 0.0, ALU.mult, ALU.add))
                do(V.tensor_copy(mf, cntf[0:1, E - 1:E]), V.tensor_copy(mint[0:1, :], cntf[0:1, E - 1:E]),
                   ts(nbf, cntf, bidx[:, 0:1], None, ALU.is_le))
                do(V.tensor_reduce(bep[:, 2:3], nbf, AX.X, ALU.add))
                do(ts(bep, bep, float(E - 1), None, ALU.min))
                V.tensor_copy(bei, bep).then_inc(s_cnt_ready, 1)

            def positions():
                do(tt(DD, psm[:, 6:8, :].rearrange("p a (i e) -> p (a i) e", e=E), basef.unsqueeze(1).to_broadcast([P, NT, E]), ALU.add))
                do(tt(DD, DD, selall, ALU.mult))
                for i in range(NT):
                    add(V.max(d8[:, i, :], DD[:, i, :]))
                sync()

            def weights(k):
                do(tt(eqb, DD, d8[:, :, k:k + 1].to_broadcast([P, NT, E]), ALU.is_equal))
                do(tt(eqb, eqb, gwall, ALU.mult))
                V.tensor_reduce(pay4[:, :, k, 1], eqb, AX.X, ALU.add).then_inc(s_pay_ready, 1)
                dve.wait_ge(s_pay_ready, k + 1)

            def addresses():
                d = d8.rearrange("p i k -> p (i k)")
                do(ts(qi, d, -1.0, None, ALU.add))
                do(ts(bi, qi, 7, None, ALU.arith_shift_right), ts(qi, qi, BLK - 1, None, ALU.bitwise_and))
                do(V.tensor_copy(bf_, bi), V.tensor_copy(qf, qi))
                do(stt(di, qf, float(NCOL), bf_, ALU.mult, ALU.add))

            def block_rows():
                dve.wait_ge(s_be_back, 16)
                do(V.tensor_copy(bef, berow[0:1, 0:NROW]), V.memset(rone, 1.0), V.memset(news[:, 0:1], 1.0))
                do(tt(news[:, 1:NROW], bef[:, 1:NROW], bef[:, 0:NROW - 1], ALU.not_equal))
                do(V.tensor_tensor_scan(ordf, rone, news, 0.0, ALU.mult, ALU.add))
                do(ts(bef, ordf, mf, None, ALU.is_lt), ts(rone, ordf, mf, None, ALU.min))
                do(tt(bef, bef, news, ALU.mult), V.tensor_copy(ordi, rone))
                V.tensor_copy(splits, bef).then_inc(s_br_ready, 1)

            counts()
            positions()
            addresses()
            weights(0)
            steps = [lambda k=k: weights(k) for k in range(1, TOPK)] + [block_rows]

            def rows_low(b):
                dve.wait_ge(s_xt_high, b + 1)
                tt(xlo[:, :], psm[:, 2:4, :].rearrange("p a n -> p (a n)"), xhi[:, :], ALU.subtract).then_inc(s_xt_ready, 1)

            def hidden(b, w):
                dve.wait_ge(s_sig_ready, b + 1)
                tt(htmp, psm[:, 0, 0:DE], sigb, ALU.mult).then_inc(s_hm_ready, 1)
                dve.wait_ge(s_hm_ready, b + 1)
                stt(hs, htmp, w, psm[:, 0, DE:2 * DE], ALU.mult, ALU.mult).then_inc(s_h_full, 1)

            def h_low(b):
                dve.wait_ge(s_ht_high, b + 1)
                tt(hlo[:, :], psm[:, 1, 0:DE], hhi[:, :], ALU.subtract).then_inc(s_ht_ready, 1)

            def split_low(slot, number):
                for c in range(NGC):
                    dve.wait_ge(s_whi_ready, number + c + 1)
                    m = tt(wlo[:, bass.ds(slot + c * GC, GC)], raw[:, bass.ds(slot + c * GC, GC)],
                           whi[:, bass.ds(slot + c * GC, GC)], ALU.subtract)
                m.then_inc(s_wlo_ready, 1)

            def step(b, w=1.0):
                hidden(b, w)
                rows_low(b + 1)
                h_low(b)

            def routed_step(b):
                fn = dve.value_load(splits[0:1, bass.ds(b - (NT - 1), 1)], min_val=0, max_val=1)
                on = dve.value_load(ordi[0:1, bass.ds(b - (NT - 1), 1)], min_val=1, max_val=E)
                hidden(b, tabl[:, bass.ds(b - NT, 1), 1])
                rows_low(b + 1)
                with dve.If(fn > 0):
                    split_low((on & 1) * WSLOT, on * NGC)
                h_low(b)

            rows_low(0)
            for b in range(len(steps)):
                step(b)
                steps[b]()
            with dve.Fori(len(steps), NT - 1) as b:
                step(b)
            split_low(0, 0)
            step(NT - 1)
            split_low(WSLOT, NGC)
            dve.wait_ge(s_br_ready, 1)
            routed_step(NT)
            nb = dve.value_load(nbi[0:1, 0:1], min_val=TOPK, max_val=NB)
            with dve.Fori(NT + 1, nb + NT) as b:
                routed_step(b)
            for i in range(NT):
                dve.wait_ge(s_fr_ready, i + 1)
                x = fin[i]
                stt(x, x, st[:, 32 + i:33 + i], rows[:, 3], ALU.mult, ALU.mult).then_inc(s_ft_ready, 1)
                dve.wait_ge(s_ft_ready, i + 1)
                if i == 0:
                    dve.wait_ge(s_xp_in, 16 * (NT - 1))
                if i == NT - 1:
                    dve.wait_ge(s_xp_in, 16 * NT)
                tt(x, x, xps[i], ALU.add).then_inc(s_fo_ready, 1)

        @blk.gpsimd
        def _(pool):
            ch = Chain(pool, s_pool_step)
            do, add = ch.do, ch.add
            do(PO.memset(ident[:, :], 0.0), PO.memset(tri[:, :], 1.0), PO.memset(sel8[:, :, :], 1.0),
               PO.memset(oneb[:, :], 1.0), PO.memset(one[:, :], 1.0), PO.memset(mhalf[:, :], -0.5))
            do(PO.affine_select(out=ident[:, :], in_=ident[:, :], compare_op=ALU.not_equal, fill=1.0, base=0, pattern=[[-1, P]], channel_multiplier=1),
               PO.affine_select(out=tri[:, :], in_=tri[:, :], compare_op=ALU.is_gt, fill=0.0, base=0, pattern=[[1, P]], channel_multiplier=-1),
               PO.affine_select(out=sel8[:, :, :], in_=sel8[:, :, :], compare_op=ALU.is_gt, fill=0.0, base=0, pattern=[[1, NG], [-1, NG]], channel_multiplier=0))
            PO.memset(st[:, 63:64], 0.0).then_inc(s_const_ok, 1)

            def rsqrt(out_, tmp, sq, n, done):
                do(PO.tensor_scalar(tmp, sq, 1.0 / n, EPS, ALU.mult, ALU.add))
                PO.tensor_tensor(out_, tmp, mhalf[:, :], ALU.pow).then_inc(done, 1)

            def to_h(h):
                for i in range(TPH):
                    n = h * TPH + i
                    pool.wait_ge(s_sq_ready, n + 1)
                    rsqrt(st[:, 32 + n:33 + n], st[:, 16 + n:17 + n], st[:, n:n + 1], D, s_stat_ready)
                    if n in XPOOL:
                        pool.wait_ge(s_arow_ready, 1)
                        pool.wait_ge(s_xr_ready, XPOOL.index(n) + 1)
                        x = xb[:, n % 3, :]
                        do(PO.tensor_tensor(x, x, arow, ALU.mult))
                        PO.tensor_tensor(x, x, brow, ALU.add).then_inc(s_xnp_ready, 1)

            def gate(h):
                for q in range(CT):
                    for b in range(2):
                        pool.wait_ge(s_mm_free, MMN["zc", h, q, b, 1] + 1)
                        k = SGN["zc", h, q, b]
                        o = v[:, q, PAD + b * 512:PAD + (b + 1) * 512]
                        do(PO.tensor_tensor(o, o, sg[k % 2], ALU.mult))
                        PO.memset(st[:, 62:63], 0.0).then_inc(s_sg_free, 1)
                        PO.memset(st[:, 61:62], 0.0).then_inc(s_v_ready, 1)

            def out_slot(key):
                n = BON[key]
                if n >= 2:
                    pool.wait_ge([s_bo_out0, s_bo_out1][n % 2], 16 * (n // 2))
                return bo[:, n % 2, :]

            def glu(h):
                for b in range(2):
                    for q in range(CT):
                        pool.wait_ge(s_mm_free, MMN["glu", h, b, q] + 1)
                        k = SGN["glu", h, b, q]
                        o = out_slot(("glu", h, b, q))
                        do(PO.tensor_tensor(o, gT[:, q, b * 512:(b + 1) * 512], sg[k % 2], ALU.mult))
                        PO.memset(st[:, 62:63], 0.0).then_inc(s_sg_free, 1)
                        PO.memset(st[:, 61:62], 0.0).then_inc(s_bo_full, 1)

            def norm(h):
                def finish(i):
                    k = SGN["ln", h, i]
                    pool.wait_ge(s_ly_full, h * TPH + i + 1)
                    o = out_slot(("ln", h, i))
                    do(PO.tensor_tensor(o, ly[:, :], sg[k % 2], ALU.mult))
                    PO.memset(st[:, 62:63], 0.0).then_inc(s_sg_free, 1)
                    PO.memset(st[:, 61:62], 0.0).then_inc(s_bo_full, 1)

                for i in range(TPH):
                    k = h * TPH + i
                    pool.wait_ge(s_bn_ready, k + 1)
                    do(PO.tensor_scalar(st[:, 48:49], bn[:, 7:8], EPS, None, ALU.add))
                    do(PO.tensor_tensor(st[:, 49:50], st[:, 48:49], mhalf[:, :], ALU.pow))
                    if k:
                        pool.wait_ge(s_tp_full, (TPN["LB", h, i - 1] if i else TPN["LB", 0, TPH - 1]) + 1)
                    PO.tensor_scalar(yn, ytok[:, :], bn[:, 6:7], st[:, 49:50], ALU.subtract, ALU.mult).then_inc(s_yn_ready, 1)
                    if i:
                        finish(i - 1)
                finish(TPH - 1)

            for h in range(NH):
                to_h(h)
                if h == 1:
                    norm(0)
                gate(h)
                glu(h)
            do(PO.memset(xb[:, 2, :], 0.0))
            PO.memset(st[:, 61:62], 0.0).then_inc(s_zero_ok, 1)
            norm(1)
            pool.wait_ge(s_row_ready, 1)
            do(PO.iota(rinit[:, :, 0].bitcast(I32), pattern=[[0, NCOL]], base=T, channel_multiplier=1),
               PO.memset(rinit[:, :, 1], 0.0),
               PO.iota(bidx.bitcast(I32), pattern=[[P, 2]], base=0, channel_multiplier=1),
               PO.iota(n_split, pattern=[[1, E]], base=-1, channel_multiplier=0),
               PO.iota(n_come, pattern=[[16, E]], base=0, channel_multiplier=0),
               PO.iota(n_base, pattern=[[0, E // 2], [WSLOT, 2]], base=0, channel_multiplier=0),
               PO.iota(pay[:, :, 0].bitcast(I32).rearrange("p (i k) -> p i k", i=NT), pattern=[[P, NT], [0, TOPK]], base=0, channel_multiplier=1))
            do(PO.tensor_copy(bidx, bidx.bitcast(I32)))
            PO.memset(st[:, 61:62], 0.0).then_inc(s_rinit_ready, 1)
            PO.dma_start(rows_d.rearrange("(p b) w -> p b w", p=P), rinit).then_inc(s_rinit_out, 16)
            for i in range(NT):
                c0 = 16 * (i % 2)
                pool.wait_ge(s_ssn_ready, i + 1)
                for f in range(2):
                    m = PO.tensor_tensor(st[:, c0 + 2 + f:c0 + 3 + f], st[:, c0 + f:c0 + f + 1], mhalf[:, :], ALU.pow)
                    if f == 0:
                        do(m)
                    else:
                        m.then_inc(s_rr_ready, 1)
                pool.wait_ge(s_so_ready, i + 1)
                rsqrt(st[:, c0 + 6:c0 + 7], st[:, c0 + 5:c0 + 6], st[:, c0 + 4:c0 + 5], D, s_ro_ready)
                pool.wait_ge(s_t_ready, i + 1)
                pool.wait_ge([s_xs_in0, s_xs_in1][i % 2], 16 * (i // 2 + 1))
                x = xb[:, i % 2, :]
                PO.tensor_tensor(x, x, ob, ALU.add).then_inc(s_x1_ready, 1)
                pool.wait_ge(s_s1_ready, i + 1)
                rsqrt(st[:, c0 + 9:c0 + 10], st[:, c0 + 8:c0 + 9], st[:, c0 + 7:c0 + 8], D, s_r1_ready)
                pool.wait_ge(s_ha_ready, i + 1)
                h2 = h2b[:, i % 2, :]
                PO.tensor_tensor(h2, h2, rows[:, 2], ALU.add).then_inc(s_h2_ready, 1)

            pool.wait_ge(s_rinit_out, 16)
            for k in range(TOPK):
                pool.wait_ge(s_pay_ready, k + 1)
                for i in range(NT):
                    n = i * TOPK + k
                    PO.indirect_dma_start(rows_d, bass.IndirectOffsetOnAxis(di[:, n:n + 1], 0), pay[:, n, :], None).then_inc(s_disp_out, 16)
            pool.wait_ge(s_disp_out, 16 * NT * TOPK)
            PO.dma_start(tabl, rows_d.rearrange("(p b) w -> p b w", p=P)).then_inc(s_rows_back, 16)
            pool.wait_ge(s_rows_back, 16)

            def hold():
                PO.tensor_tensor(st[:, 60:61], mhalf[:, :], mhalf[:, :], ALU.add)

            def gather(b, n, w):
                pool.wait_ge(s_xt_full, b - 1)
                PO.tensor_copy(idxg[w], tabl[:, bass.ds(b - NT, 1), 0].bitcast(U32)).then_inc(s_idx_ready, 1)
                pool.wait_ge(s_idx_ready, n)
                hold()
                PO.indirect_dma_start(xg[w], None, h2_d, bass.IndirectOffsetOnAxis(idxg[w], 0)).then_inc([s_xr_in0, s_xr_in1][w], 16)

            def split_low(slot, number):
                pool.wait_ge(s_whid_ready, number)
                PO.tensor_tensor(wlo[:, bass.ds(slot + WG, FE * D)], raw[:, bass.ds(slot + WG, FE * D)],
                                 whi[:, bass.ds(slot + WG, FE * D)], ALU.subtract).then_inc(s_wlow_ready, 1)

            def add_block(b, w):
                PO.tensor_copy(idxs, tabl[:, bass.ds(b - NT, 1), 0].bitcast(U32)).then_inc(s_idy_ready, 1)
                pool.wait_ge(s_idy_ready, b - (NT - 1))
                pool.wait_ge(s_y_act, b + 1)
                hold()
                PO.indirect_dma_start(acc_d, bass.IndirectOffsetOnAxis(idxs, 0), yb[w], None, compute_op=ALU.add).then_inc(s_ya_out, 16)

            def step(b, w, first=False):
                f = pool.value_load(splits[0:1, bass.ds(b - NT, 1)], min_val=0, max_val=1)
                o = pool.value_load(ordi[0:1, bass.ds(b - NT, 1)], min_val=1, max_val=E)
                gather(b + 3, b - (NT - 4), 1 - w)
                if not first:
                    pool.wait_ge(s_ya_out, (b - (NT + 1)) * 16)
                    PO.tensor_tensor(st[:, 59:60], mhalf[:, :], mhalf[:, :], ALU.add).then_inc(s_y_free, 1)
                add_block(b - 1, 1 - w)
                with pool.If(f > 0):
                    split_low((o & 1) * WSLOT, o + 1)

            gather(NT, 1, 0)
            gather(NT + 1, 2, 1)
            split_low(0, 1)
            gather(NT + 2, 3, 0)
            for w in range(2):
                pool.wait_ge([s_y_out0, s_y_out1][w], NT * 8)
            PO.tensor_tensor(st[:, 58:59], mhalf[:, :], mhalf[:, :], ALU.add).then_inc(s_y_free, 1)
            gather(NT + 3, 4, 1)
            split_low(WSLOT, 2)
            pool.wait_ge(s_br_ready, 1)
            step(NT + 1, 1, first=True)
            nb = pool.value_load(nbi[0:1, 0:1], min_val=TOPK, max_val=NB)
            with pool.Fori(NT + 2, nb + NT, 2) as b:
                step(b, 0)
                step(b + 1, 1)
            nb = pool.value_load(nbi[0:1, 0:1], min_val=TOPK, max_val=NB)
            before = pool.value_load(nbm[0:1, 0:1], min_val=TOPK - 1, max_val=NB)
            pool.wait_ge(s_ya_out, before * 16)
            PO.tensor_tensor(st[:, 59:60], mhalf[:, :], mhalf[:, :], ALU.add).then_inc(s_y_free, 1)
            add_block(nb + (NT - 1), 1)
            pool.wait_ge(s_ya_out, nb * 16)
            PO.tensor_tensor(st[:, 58:59], mhalf[:, :], mhalf[:, :], ALU.add)
            pool.wait_ge(s_xr_in0, nb * 8 + 32)
            PO.tensor_tensor(st[:, 57:58], mhalf[:, :], mhalf[:, :], ALU.add)
            pool.wait_ge(s_xr_in1, nb * 8 + 16)
            PO.tensor_tensor(st[:, 56:57], mhalf[:, :], mhalf[:, :], ALU.add).then_inc(s_y_free, 1)
            for i in range(NT):
                pool.wait_ge(s_fs_ready, i + 1)
                rsqrt(st[:, 32 + i:33 + i], st[:, 16 + i:17 + i], st[:, i:i + 1], D, s_fr_ready)


_INS = ["x", "c", "w_ada", "b_ada", "g_pre_mix", "g_post_mix", "w_in", "conv_w", "conv_b", "conv_ln_g", "conv_ln_b",
        "ssm_a_re", "ssm_a_im", "ssm_log_dt", "ssm_b_re", "ssm_b_im", "ssm_c_re", "ssm_c_im", "ssm_d", "ssm_w_glu",
        "ssm_b_glu", "g_out_conv", "g_out_ssm", "w_out", "g_pre_ffn", "g_post_ffn", "w_router", "b_router", "we_gate",
        "we_up", "we_down", "ws_gate", "ws_up", "ws_down"]


def kernel(**inputs):
    import numpy as _np
    import concourse.bacc as _bacc
    from concourse import mybir as _mybir
    from concourse.bass_utils import run_bass_kernel_spmd as _run

    nc = _bacc.Bacc("TRN2", target_bir_lowering=False, num_devices=1)
    arrays, args = {}, {}
    for name in _INS:
        a = _np.ascontiguousarray(inputs[name])
        arrays[f"in_{name}_dram"] = a
        args[name] = nc.dram_tensor(f"in_{name}_dram", a.shape, _mybir.dt.from_np(a.dtype), kind="ExternalInput").ap()
    out = nc.dram_tensor("out_0_dram", (1, T, D), _mybir.dt.float32, kind="ExternalOutput").ap()
    build(nc, args, out)
    r = _run(nc, [arrays], core_ids=[0])
    return r.results[0]["out_0_dram"]
```
